# Optimizing a Trainium2 kernel written in Bass

```python
import jax, jax.numpy as jnp
from jax import lax
import numpy as np

D_MODEL = 1024
BATCH = 1
SEQ = 1024
DEPTH = 1
DEC_BATCH = 8
DEC_SEQ = 8
PAST_LEN = 256
PAGE_SIZE = 128

A_PATTERNS = ((128, 1), (512, 4), (2048, 16))
A_GROUPS = 3
A_HEADS = 4
A_HEAD_DIM = 128
A_GROUP_WIDTH = A_HEADS * A_HEAD_DIM
A_WIDTH = A_HEADS * A_HEAD_DIM
B_HEADS = 8
B_KEY_DIM = D_MODEL // B_HEADS
B_VAL_DIM = D_MODEL // B_HEADS
B_KEY_WIDTH = B_HEADS * B_KEY_DIM
B_WIDTH = B_HEADS * B_VAL_DIM
B_CHUNK = 64
C_WINDOWS = (2, 4, 8, 16)
C_GROUPS = 4
C_GROUP_DIM = 128
C_WIDTH = C_GROUPS * C_GROUP_DIM
C_HIST = 15
N_BRANCH = 3
EPS = 1e-6
NEG = -1e30
IN_SPLITS = (A_GROUPS * A_GROUP_WIDTH, A_GROUPS * A_GROUP_WIDTH, A_GROUPS * A_GROUP_WIDTH, A_WIDTH,
             B_KEY_WIDTH, B_KEY_WIDTH, B_WIDTH, B_WIDTH, C_WIDTH, C_WIDTH, N_BRANCH * D_MODEL)
IN_WIDTH = 13312
F32 = jnp.float32

kernel_name = 'hybrid_dilated_hgrn2_pool_decode_step'

def rmsnorm(x, g):
    xf = x.astype(F32)
    y = xf * lax.rsqrt(jnp.mean(xf * xf, axis=-1, keepdims=True) + EPS)
    return (y * g.astype(F32)).astype(x.dtype)

def split_in(z):
    offs = [int(o) for o in np.cumsum(IN_SPLITS)[:-1]]
    return jnp.split(z, offs, axis=-1)

def dilated_attn_prompt(q, k, v, dilation, n_steps):
    b, s, h, e = q.shape
    L = s // dilation
    nb = -(-L // n_steps)
    Lp = nb * n_steps

    def to_blocks(t):
        t = t.reshape(b, L, dilation, h, e).transpose(0, 2, 1, 3, 4)
        t = jnp.pad(t, ((0, 0), (0, 0), (0, Lp - L), (0, 0), (0, 0)))
        return t.reshape(b, dilation, nb, n_steps, h, e)

    def with_prev(t):
        prev = jnp.pad(t, ((0, 0), (0, 0), (1, 0), (0, 0), (0, 0), (0, 0)))[:, :, :-1]
        return jnp.concatenate([prev, t], axis=3)

    qb = to_blocks(q)
    kk = with_prev(to_blocks(k))
    vv = with_prev(to_blocks(v))
    scores = jnp.einsum('brnqhe,brnkhe->brnhqk', qb, kk, preferred_element_type=F32) * (e ** -0.5)
    qi = jnp.arange(n_steps)[:, None]
    kj = jnp.arange(2 * n_steps)[None, :]
    band = (kj >= qi) & (kj <= qi + n_steps)
    blk = jnp.arange(nb)[:, None, None]
    valid = band[None] & ((blk > 0) | (kj[None] >= n_steps))
    scores = jnp.where(valid[None, None, :, None], scores, NEG)
    lse = jax.nn.logsumexp(scores, axis=-1)
    p = jnp.exp(scores - lse[..., None])
    o = jnp.einsum('brnhqk,brnkhe->brnqhe', p, vv.astype(F32))
    o = o.reshape(b, dilation, Lp, h, e)[:, :, :L].transpose(0, 2, 1, 3, 4).reshape(b, s, h, e)
    lse = lse.transpose(0, 1, 2, 4, 3).reshape(b, dilation, Lp, h)[:, :, :L]
    lse = lse.transpose(0, 2, 1, 3).reshape(b, s, h)
    return o, lse

def dilated_attn_sample(q, k_all, v_all, dilation, n_steps):
    b, T, h, e = q.shape
    n_ctx = k_all.shape[1]
    idx = (n_ctx - T + jnp.arange(T))[:, None] - dilation * jnp.arange(n_steps + 1)[None, :]
    valid = idx >= 0
    idx_c = jnp.maximum(idx, 0)
    kg = k_all[:, idx_c]
    vg = v_all[:, idx_c]
    scores = jnp.einsum('bthe,btjhe->bthj', q, kg, preferred_element_type=F32) * (e ** -0.5)
    scores = jnp.where(valid[None, :, None, :], scores, NEG)
    lse = jax.nn.logsumexp(scores, axis=-1)
    p = jnp.exp(scores - lse[..., None])
    o = jnp.einsum('bthj,btjhe->bthe', p, vg.astype(F32))
    return o, lse

def hgrn2_chunked(q, k, v, logf, s0):
    b, L, h, dk = q.shape
    dv = v.shape[-1]
    c = L if L <= B_CHUNK else B_CHUNK
    n = L // c

    def chunks(t):
        return t.astype(F32).reshape(b, n, c, h, t.shape[-1]).transpose(1, 0, 3, 2, 4)

    causal = jnp.tril(jnp.ones((c, c), dtype=bool))[:, :, None]

    def step(S, inp):
        qi, ki, vi, gi = inp
        A = jnp.cumsum(gi, axis=2)
        diff = A[:, :, :, None, :] - A[:, :, None, :, :]
        decay = jnp.where(causal, jnp.exp(jnp.where(causal, diff, 0.0)), 0.0)
        att = jnp.einsum('bhtk,bhtsk,bhsk->bhts', qi, decay, ki)
        o = jnp.einsum('bhts,bhsv->bhtv', att, vi) + jnp.einsum('bhtk,bhkv->bhtv', qi * jnp.exp(A), S)
        A_last = A[:, :, -1:, :]
        S = jnp.exp(A_last[:, :, 0, :, None]) * S + jnp.einsum('bhsk,bhsv->bhkv', ki * jnp.exp(A_last - A), vi)
        return S, o

    S, o = lax.scan(step, s0.astype(F32), (chunks(q), chunks(k), chunks(v), chunks(logf)))
    o = o.transpose(1, 0, 3, 2, 4).reshape(b, L, h, dv)
    return o, S

def multiscale_pool(u, hist, first_pos, pool_w, pool_scale):
    b, L, _ = u.shape
    ext = jnp.concatenate([hist.astype(u.dtype), u], axis=1)
    cs = jnp.pad(jnp.cumsum(ext.astype(F32), axis=1), ((0, 0), (1, 0), (0, 0)))
    pos = first_pos + jnp.arange(L)
    means = []
    for g, win in enumerate(C_WINDOWS):
        lo, hi = g * C_GROUP_DIM, (g + 1) * C_GROUP_DIM
        s = cs[:, C_HIST + 1:C_HIST + 1 + L, lo:hi] - cs[:, C_HIST + 1 - win:C_HIST + 1 - win + L, lo:hi]
        cnt = jnp.minimum(pos + 1, win).astype(F32)
        means.append(s / cnt[None, :, None])
    pooled = jnp.concatenate(means, axis=-1) - u.astype(F32)
    mixed = jnp.einsum('blgc,gcd->blgd', pooled.reshape(b, L, C_GROUPS, C_GROUP_DIM), pool_w.astype(F32))
    out = mixed.reshape(b, L, C_WIDTH) * pool_scale.astype(F32)
    return out, ext[:, -C_HIST:]

def mixer_layer(x, kv_hist, s0, pool_hist, first_pos, lb, norm_pre, norm_post, w_in, hgrn_norm,
                pool_w, pool_scale, w_br_a, w_br_b, w_br_c, w_out):
    b, L, _ = x.shape
    dt = x.dtype
    xn = rmsnorm(x, norm_pre)
    z = jnp.einsum('bld,dn->bln', xn, w_in)
    aq, ak, av, ag, bq, bfg, bi, bg, cu, cg, mg = split_in(z)

    shp = (b, L, A_GROUPS, A_HEADS, A_HEAD_DIM)
    aq, ak, av = aq.reshape(shp), ak.reshape(shp), av.reshape(shp)
    outs, lses, new_kv = [], [], []
    for g, (win, dil) in enumerate(A_PATTERNS):
        n_steps = win // dil
        q, k, v = aq[:, :, g], ak[:, :, g], av[:, :, g]
        if kv_hist is None:
            o, lse = dilated_attn_prompt(q, k, v, dil, n_steps)
            rows = min(win, L)
            new_kv.append(jnp.stack([k[:, L - rows:], v[:, L - rows:]], axis=2))
        else:
            kv_new = jnp.stack([k, v], axis=2).astype(kv_hist[g].dtype)
            full = jnp.concatenate([kv_hist[g], kv_new], axis=1)
            o, lse = dilated_attn_sample(q, full[:, :, 0], full[:, :, 1], dil, n_steps)
            new_kv.append(kv_new)
        outs.append(o)
        lses.append(lse)
    w_grp = jax.nn.softmax(jnp.stack(lses, axis=0), axis=0)
    o_a = jnp.einsum('gblh,gblhe->blhe', w_grp, jnp.stack(outs, axis=0)).reshape(b, L, A_WIDTH)
    y_a = (o_a * jax.nn.silu(ag.astype(F32))).astype(dt)

    f = lb + (1.0 - lb) * jax.nn.sigmoid(bfg.astype(F32))
    logf = jnp.log(f)
    kin = 1.0 - f
    o_b, s_new = hgrn2_chunked(bq.reshape(b, L, B_HEADS, B_KEY_DIM), kin.reshape(b, L, B_HEADS, B_KEY_DIM),
                               bi.reshape(b, L, B_HEADS, B_VAL_DIM), logf.reshape(b, L, B_HEADS, B_KEY_DIM), s0)
    o_b = rmsnorm(o_b, hgrn_norm).reshape(b, L, B_WIDTH)
    y_b = (o_b * jax.nn.silu(bg.astype(F32))).astype(dt)

    o_c, pool_new = multiscale_pool(cu, pool_hist, first_pos, pool_w, pool_scale)
    y_c = (o_c * jax.nn.silu(cg.astype(F32))).astype(dt)

    gates = jax.nn.sigmoid(mg.reshape(b, L, N_BRANCH, D_MODEL))
    merged = (gates[:, :, 0] * (y_a @ w_br_a) + gates[:, :, 1] * (y_b @ w_br_b)
              + gates[:, :, 2] * (y_c @ w_br_c))
    out = merged @ w_out
    return x + rmsnorm(out, norm_post), new_kv, s_new.astype(dt), pool_new

def setup_inputs(seed: int = 0) -> dict:
    key = jax.random.key(seed)
    ks = jax.random.split(key, 24)

    def nrm(k, shape, scale):
        return jax.random.normal(k, shape, F32) * scale

    inp = {}
    inp['x_prompt'] = nrm(ks[0], (BATCH, SEQ, D_MODEL), 1.0)
    inp['x_sample'] = nrm(ks[1], (DEC_BATCH, DEC_SEQ, D_MODEL), 1.0)
    for i, (win, _) in enumerate(A_PATTERNS):
        inp['cache_kv_w%d' % win] = nrm(ks[2 + i], (DEPTH, DEC_BATCH, min(win, PAST_LEN), 2, A_HEADS, A_HEAD_DIM), 1.0)
    inp['state_hgrn'] = nrm(ks[5], (DEPTH, DEC_BATCH, B_HEADS, B_KEY_DIM, B_VAL_DIM), 0.5)
    inp['state_pool'] = nrm(ks[6], (DEPTH, DEC_BATCH, C_HIST, C_WIDTH), 1.0)
    inp['norm_pre'] = 1.0 + nrm(ks[7], (DEPTH, D_MODEL), 0.02)
    inp['norm_post'] = 1.0 + nrm(ks[8], (DEPTH, D_MODEL), 0.02)
    inp['w_in'] = nrm(ks[9], (DEPTH, D_MODEL, IN_WIDTH), D_MODEL ** -0.5)
    inp['hgrn_lb_logits'] = nrm(ks[10], (DEPTH, B_KEY_WIDTH), 0.5)
    inp['hgrn_norm'] = 1.0 + nrm(ks[11], (DEPTH, B_VAL_DIM), 0.02)
    inp['pool_w'] = nrm(ks[12], (DEPTH, C_GROUPS, C_GROUP_DIM, C_GROUP_DIM), C_GROUP_DIM ** -0.5)
    inp['pool_scale'] = 1.0 + nrm(ks[13], (DEPTH, C_WIDTH), 0.1)
    inp['w_br_a'] = nrm(ks[14], (DEPTH, A_WIDTH, D_MODEL), A_WIDTH ** -0.5)
    inp['w_br_b'] = nrm(ks[15], (DEPTH, B_WIDTH, D_MODEL), B_WIDTH ** -0.5)
    inp['w_br_c'] = nrm(ks[16], (DEPTH, C_WIDTH, D_MODEL), C_WIDTH ** -0.5)
    inp['w_out'] = nrm(ks[17], (DEPTH, D_MODEL, D_MODEL), D_MODEL ** -0.5)
    return inp

def reference(x_prompt, x_sample, cache_kv_w128, cache_kv_w512, cache_kv_w2048, state_hgrn, state_pool,
              norm_pre, norm_post, w_in, hgrn_lb_logits, hgrn_norm, pool_w, pool_scale,
              w_br_a, w_br_b, w_br_c, w_out):
    p = jax.nn.softmax(hgrn_lb_logits.astype(F32), axis=0)
    lower_bounds = jnp.cumsum(p, axis=0) - p[0]
    hp, hs = x_prompt, x_sample
    b_p = x_prompt.shape[0]
    kv_p = ([], [], [])
    kv_s = ([], [], [])
    hg_p, hg_s, pl_p, pl_s = [], [], [], []
    for l in range(DEPTH):
        lw = (norm_pre[l], norm_post[l], w_in[l], hgrn_norm[l], pool_w[l], pool_scale[l],
              w_br_a[l], w_br_b[l], w_br_c[l], w_out[l])
        s0 = jnp.zeros((b_p, B_HEADS, B_KEY_DIM, B_VAL_DIM), F32)
        ph0 = jnp.zeros((b_p, C_HIST, C_WIDTH), x_prompt.dtype)
        hp, kvs, s_new, ph = mixer_layer(hp, None, s0, ph0, 0, lower_bounds[l], *lw)
        for g in range(A_GROUPS):
            kv_p[g].append(kvs[g])
        hg_p.append(s_new)
        pl_p.append(ph)
        hist = (cache_kv_w128[l], cache_kv_w512[l], cache_kv_w2048[l])
        hs, kvs, s_new, ph = mixer_layer(hs, hist, state_hgrn[l], state_pool[l], PAST_LEN, lower_bounds[l], *lw)
        for g in range(A_GROUPS):
            kv_s[g].append(kvs[g])
        hg_s.append(s_new)
        pl_s.append(ph)
    return (hp, hs,
            jnp.stack(kv_p[0]), jnp.stack(kv_p[1]), jnp.stack(kv_p[2]),
            jnp.stack(kv_s[0]), jnp.stack(kv_s[1]), jnp.stack(kv_s[2]),
            jnp.stack(hg_p), jnp.stack(hg_s), jnp.stack(pl_p), jnp.stack(pl_s))


_drawn_inputs = setup_inputs


def setup_inputs(seed=0):
    import zlib

    import numpy as np

    out = dict(_drawn_inputs(seed))
    spreads = {}
    factors = {}
    for name, (base, spread) in spreads.items():
        noise = np.random.default_rng([zlib.crc32(name.encode()), seed]).standard_normal(out[name].shape)
        drawn = base * np.exp(spread * noise) if base else spread * noise
        out[name] = __import__('jax').numpy.asarray(drawn.astype(out[name].dtype))
    for name, factor in factors.items():
        out[name] = (out[name] * factor).astype(out[name].dtype)
    return out
```

```python
import concourse.bass as bass
from concourse import mybir
from contextlib import ExitStack

F32 = mybir.dt.float32
F32R = mybir.dt.float32r
I32 = mybir.dt.int32
ALU = mybir.AluOpType
ACT = mybir.ActivationFunctionType
AX = mybir.AxisListType

D = 1024
P = 128
KO = D // P
SEQ = 1024
NB, TB = 8, 8
NS = NB * TB
NT = SEQ + NS
TILES = SEQ // P
EPS = 1e-6
NEG = -1e30
SCALE = P ** -0.5
AH, BH, CG, AG = 4, 8, 4, 3
GROUP = AH * P
HIST = 15
WINDOWS = (2, 4, 8, 16)
COL_AQ, COL_AK, COL_AV, COL_AG = 0, 3 * GROUP, 6 * GROUP, 9 * GROUP
COL_BQ = COL_AG + GROUP
COL_BF, COL_BI, COL_BG = COL_BQ + D, COL_BQ + 2 * D, COL_BQ + 3 * D
COL_CU = COL_BG + D
COL_CG = COL_CU + GROUP
COL_MG = COL_CG + GROUP

CHUNKS = ((0, 384), (384, 384), (768, NT - 768))
NCH = len(CHUNKS)
SLOTS = 2
Y_A, Y_C = BH, BH + AH
LEVELS = 8


def constants(np):
    i = np.arange(P)
    c = {}
    c["ident"] = np.eye(P, dtype=np.float32)
    band = np.zeros((P, 2 * P), np.float32)
    band[:, :P] = np.where(i[None, :] >= i[:, None], 0.0, NEG)
    band[:, P:] = np.where(i[None, :] <= i[:, None], 0.0, NEG)
    c["band"] = band
    gap = i[:, None] - i[None, :]
    c["pair"] = np.where((gap >= 0) & (gap % 2 == 0), 0.0, NEG).astype(np.float32)
    lev = np.zeros((P, LEVELS, P), np.int32)
    s, t = i[:, None], i[None, :]
    for n in range(1, LEVELS):
        h = n - 1
        lev[:, n, :] = ((s >> n) == (t >> n)) & (((s >> h) & 1) == 0) & (((t >> h) & 1) == 1)
    c["level"] = lev
    j = np.arange(NS)
    c["own_row"] = ((j[:, None] // TB) == np.arange(NB)[None, :]).astype(np.float32)
    c["own_col"] = np.broadcast_to((np.arange(NB)[:, None] == (j[None, :] // TB)).astype(np.float32),
                                   (P, NB, NS)).copy()
    tq = (j % TB)[:, None]
    m = np.full((NS, 4 * P + 3 * NS), NEG, np.float32)
    m[:, 0:P] = np.where(i[None, :] >= tq, 0.0, NEG)
    for blk in range(2):
        key = P * blk + i[None, :]
        m[:, (1 + blk) * P:(2 + blk) * P] = np.where((256 + tq - key) % 4 == 0, 0.0, NEG)
    key = 16 * (i[None, :] // 8) + i[None, :] % 8
    m[:, 3 * P:4 * P] = np.where((256 + tq - key) % 16 == 0, 0.0, NEG)
    for g, dil in enumerate((1, 4, 16)):
        gap = tq - (j % TB)[None, :]
        ok = ((j[:, None] // TB) == (j[None, :] // TB)) & (gap >= 0) & (gap % dil == 0)
        m[:, 4 * P + g * NS:4 * P + (g + 1) * NS] = np.where(ok, 0.0, NEG)
    c["sample_mask"] = m
    rc = np.zeros((P, CG, HIST), np.float32)
    for g, w in enumerate(WINDOWS):
        rc[:, g, :] = 1.0 / np.minimum(np.arange(HIST) + 1, w)
    c["count"] = rc
    return c


def build(nc, A, OUT):
    ctx = ExitStack()
    with ctx:
        def sb(name, shape, dt=F32, scope=ctx):
            return scope.enter_context(nc.sbuf_tensor(name, list(shape), dt))

        def sem(name, scope):
            h = lot[0].enter_context(nc.semaphore(name))
            taken.append(h.num)
            return h

        lot, taken = [ExitStack()], []

        def fresh_semaphores():
            nums = sorted(taken)
            runs = [[nums[0], nums[0] + 1]]
            for n in nums[1:]:
                if n == runs[-1][1]:
                    runs[-1][1] = n + 1
                else:
                    runs.append([n, n + 1])
            with nc.Block() as block:
                @block.gpsimd
                def _(pool):
                    for a, b in runs:
                        pool.sem_clear(range(a, b))
            lot[0].close()
            lot[0] = ExitStack()
            taken.clear()

        merged_d = nc.dram_tensor("merged_rows", (KO, P, NT), F32, kind="Internal").ap()
        y_d = nc.dram_tensor("branch_outputs", (2 * KO, P, NT), F32, kind="Internal").ap()
        stat_d = nc.dram_tensor("stat_rows", (AH, SEQ, 2, 2), F32, kind="Internal").ap()
        weight_d = nc.dram_tensor("group_weights", (AH, SEQ, 2), F32, kind="Internal").ap()

        psum = ctx.enter_context(nc.psum_tensor("psum", [P, 8, 512], F32))

        ident = sb("ident", (P, P))
        band = sb("band", (P, 2 * P))
        pair = sb("pair", (P, P))
        g_pre = sb("g_pre", (P, KO))
        lb = sb("lb", (P, BH))
        one_lb = sb("one_lb", (P, BH))
        h_norm = sb("h_norm", (P, 1))
        p_scale = sb("p_scale", (P, CG))
        eps = sb("eps", (P, 1))
        w_raw = sb("w_raw", (P, SLOTS, KO, P))
        w_hi = sb("w_hi", (P, SLOTS, KO, P), F32R)
        w_lo = sb("w_lo", (P, SLOTS, KO, P), F32R)
        x_hi = sb("x_hi", (P, KO, NT), F32R)
        x_lo = sb("x_lo", (P, KO, NT), F32R)

        w_in = A["w_in"][0].rearrange("(ko p) n -> p ko n", p=P)
        w_out = A["w_out"][0].rearrange("(ko p) n -> p ko n", p=P)
        w_br = {k: A["w_br_" + k][0].rearrange("(ko p) n -> p ko n", p=P) for k in "abc"}

        def col(w, at):
            return w[:, :, bass.ds(at, P)]

        class Conveyor:

            def __init__(self, tag, scope, misc_banks):
                self.loaded = [sem(f"{tag}_w_loaded{s}", scope) for s in range(SLOTS)]
                self.hi_ready = sem(f"{tag}_w_hi_ready", scope)
                self.split_done = sem(f"{tag}_w_split_done", scope)
                self.proj_done = sem(f"{tag}_proj_done", scope)
                self.bank_free = sem(f"{tag}_bank_free", scope)
                self.misc_done = sem(f"{tag}_misc_done", scope)
                self.misc_free = sem(f"{tag}_misc_free", scope)
                self.held_pe = sem(f"{tag}_held_pe", scope)
                self.held_pool = sem(f"{tag}_held_pool", scope)
                self.held_dve = sem(f"{tag}_held_dve", scope)
                self.banks = misc_banks
                self.ring = len(misc_banks)

            def load(self, sp, u, s, src):
                sp.wait_ge(self.split_done, u + 1)
                sp.dma_start(w_raw[:, s, 0:src.shape[1], :], src).then_inc(self.loaded[s], 16)

            def pool_start(self, pool):
                pool.sem_inc(self.split_done, SLOTS)

            def split(self, pool, u, s, turn, nko):
                pool.wait_ge(self.loaded[s], 16 * turn + 16)
                pool.wait_ge(self.proj_done, NCH * u + NCH)
                pool.sem_inc(self.held_pool, 1)
                pool.tensor_copy(w_hi[:, s, 0:nko, :], w_raw[:, s, 0:nko, :]).then_inc(self.hi_ready, 1)
                pool.wait_ge(self.hi_ready, u + 1)
                pool.tensor_tensor(w_lo[:, s, 0:nko, :], w_raw[:, s, 0:nko, :],
                                   w_hi[:, s, 0:nko, :].bitcast(F32), ALU.subtract)\
                    .then_inc(self.split_done, 1)

            def pe_start(self, pe):
                pe.sem_inc(self.proj_done, SLOTS * NCH)

            def project(self, pe, u, s, c, nko, hi, lo, each=None, k0=0):
                t0, n = CHUNKS[c]
                if c == 0:
                    pe.wait_ge(self.split_done, u + 1 + SLOTS)
                pe.wait_ge(self.bank_free, NCH * u + c + 1)
                for k in range(nko):
                    if each is not None:
                        pe.wait_ge(each, k0 + k + 1)
                    for w, x in ((w_hi, hi), (w_hi, lo), (w_lo, hi)):
                        mm = pe.matmul(psum[:, c, 0:n], w[:, s, k, :], x[:, k, t0:t0 + n],
                                       start=(k == 0 and w is w_hi and x is hi),
                                       stop=(k == nko - 1 and w is w_lo))
                mm.then_inc(self.proj_done, 1)

            def act_start(self, act):
                act.sem_inc(self.bank_free, NCH)

            def empty(self, act, u, c, dst, func, raw=None):
                t0, n = CHUNKS[c]
                act.wait_ge(self.proj_done, NCH * u + c + 1 + SLOTS * NCH)
                if raw is not None:
                    act.activation(raw[:, t0:t0 + n], psum[:, c, 0:n], ACT.Copy)
                act.activation(dst[:, t0:t0 + n], psum[:, c, 0:n], func).then_inc(self.bank_free, 1)

            def emptied(self, eng, u, c=NCH - 1):
                eng.wait_ge(self.bank_free, NCH * u + c + 1 + NCH)

            def dve_start(self, dve):
                dve.sem_inc(self.misc_free, self.ring)

            def bank(self, at, m):
                return psum[:, self.banks[(m + (at if isinstance(at, int) else 0)) % self.ring], :]

            def fill(self, pe, at, m, part=False):
                pe.wait_ge(self.misc_free, at + m + 1)
                if part:
                    pe.sem_inc(self.held_pe, 1)
                return self.bank(at, m)

            def filled(self, dve, at, m, part=False):
                dve.wait_ge(self.misc_done, at + m + 1)
                if part:
                    dve.sem_inc(self.held_dve, 1)
                return self.bank(at, m)

            def copied(self, eng, at, m):
                eng.wait_ge(self.misc_free, at + m + 1 + self.ring)

        class Chain:

            def __init__(self, eng, s):
                self.eng, self.sem, self.n, self.at = eng, s, 0, 0

            def loop(self, at, n):
                self.at, self.start, self.per = at, self.n, n

            def end(self, turns):
                assert self.n - self.start == self.per, ("steps in the body", self.n - self.start)
                self.n, self.at = self.start + turns * self.per, 0

            def step(self, ins):
                ins.then_inc(self.sem, 1)
                self.n += 1
                return ins

            def wait(self):
                self.eng.wait_ge(self.sem, self.at + self.n)

            def link(self, ins):
                self.step(ins)
                self.wait()

        def norm_phase():
            scope = ExitStack()
            with scope:
                xt = sb("xt", (P, TILES + 1, D), F32, scope)
                junk = sb("junk", (P, D), F32, scope)
                ssq = sb("ssq", (P, TILES + 1), F32, scope)
                rs = sb("rs", (P, TILES + 1), F32, scope)
                lg = sb("lg", (P, BH), F32, scope)
                ex = sb("ex", (P, BH), F32, scope)
                x_in = [sem(f"x_in{i}", scope) for i in range(3)]
                const_in = sem("const_in", scope)
                lb_in = sem("lb_in", scope)
                cleared = sem("ssq_cleared", scope)
                squared = sem("squared", scope)
                rms_ready = sem("rms_ready", scope)
                xn_ready = sem("xn_ready", scope)
                xt_done = sem("transposed", scope)
                xh_ready = sem("xh_ready", scope)
                banks_free = sem("banks_free", scope)
                lg_ready = sem("lg_ready", scope)
                exp_ready = sem("exp_ready", scope)
                chain = sem("norm_chain", scope)
                spans = ((0, 4), (4, 4), (8, 1))
                RING = 5
                N_CONST = 6
                uses = [(k, sp_) for k in range(KO) for sp_ in range(3)]

                with nc.Block() as block:
                    @block.sync
                    def _(sp):
                        xv = A["x_prompt"][0].rearrange("(b p) d -> p b d", p=P)
                        sp.dma_start(xt[:, 0:4, :], xv[:, 0:4, :]).then_inc(x_in[0], 16)
                        sp.dma_start(xt[:, 4:8, :], xv[:, 4:8, :]).then_inc(x_in[1], 16)
                        sp.dma_start(xt[0:NS, 8, :], A["x_sample"].rearrange("b t d -> (b t) d"))\
                            .then_inc(x_in[2], 16)
                        for dst, src in ((ident[:, :], A["c_ident"]), (band[:, :], A["c_band"]),
                                         (pair[:, :], A["c_pair"]),
                                         (g_pre[:, :], A["norm_pre"][0].rearrange("(k p) -> p k", p=P)),
                                         (h_norm[:, :], A["hgrn_norm"].rearrange("a p -> p a")),
                                         (p_scale[:, :], A["pool_scale"][0].rearrange("(g p) -> p g", p=P))):
                            sp.dma_start(dst, src, allow_slow_non_contiguous=True).then_inc(const_in, 16)
                        sp.dma_start(lg[:, :], A["hgrn_lb_logits"][0].rearrange("(h p) -> p h", p=P),
                                     allow_slow_non_contiguous=True).then_inc(lb_in, 16)
                        sp.wait_ge(const_in, 16 * N_CONST)

                    @block.scalar
                    def _(act):
                        act.wait_ge(cleared, 1)
                        for t in range(TILES + 1):
                            act.wait_ge(x_in[t // 4], 16)
                            if t > 0:
                                act.wait_ge(squared, t)
                            n = P if t < TILES else NS
                            act.activation(junk[0:n, :], xt[0:n, t, :], ACT.Square,
                                           accum_out=ssq[0:n, t:t + 1]).then_inc(squared, 1)
                        act.wait_ge(squared, TILES + 1)
                        act.activation(rs[:, :], ssq[:, :], ACT.Sqrt, bias=eps[:, :], scale=1.0 / D)\
                            .then_inc(rms_ready, 1)
                        act.wait_ge(const_in, 16 * N_CONST)
                        for m, (k, q) in enumerate(uses):
                            b0, nb = spans[q]
                            n = nb * P if q < 2 else NS
                            act.wait_ge(xt_done, m + 1)
                            act.activation(x_hi[:, k, b0 * P:b0 * P + n], psum[:, 3 + m % RING, 0:n], ACT.Copy,
                                           scale=g_pre[:, k:k + 1]).then_inc(xh_ready, 1)
                        act.wait_ge(lg_ready, 1)
                        act.activation(ex[:, :], lg[:, :], ACT.Exp).then_inc(exp_ready, 1)

                    @block.vector
                    def _(dve):
                        ch = Chain(dve, chain)
                        ch.step(dve.memset(eps[:, :], EPS))
                        dve.memset(ssq[:, :], 1.0).then_inc(cleared, 1)
                        dve.wait_ge(rms_ready, 1)
                        ch.link(dve.reciprocal(rs[:, :], rs[:, :]))
                        for t in range(TILES + 1):
                            n = P if t < TILES else NS
                            dve.tensor_scalar(xt[0:n, t, :], xt[0:n, t, :], rs[0:n, t:t + 1], None,
                                              ALU.mult).then_inc(xn_ready, 1)
                        for m, (k, q) in enumerate(uses):
                            b0, nb = spans[q]
                            n = nb * P if q < 2 else NS
                            xs = slice(b0 * P, b0 * P + n)
                            dve.wait_ge(xh_ready, m + 1)
                            dve.scalar_tensor_tensor(
                                out=x_lo[:, k, xs], in0=psum[:, 3 + m % RING, 0:n], scalar=g_pre[:, k:k + 1],
                                in1=x_hi[:, k, xs].bitcast(F32), op0=ALU.mult, op1=ALU.subtract)\
                                .then_inc(banks_free, 1)
                        dve.wait_ge(lb_in, 16)
                        dve.tensor_tensor(lg[:, :], lg[:, :], lg[:, :], ALU.subtract).then_inc(lg_ready, 1)
                        dve.wait_ge(exp_ready, 1)
                        ch.link(dve.reciprocal(lg[:, :], ex[:, :]))
                        ch.link(dve.tensor_tensor(ex[:, :], ex[:, :], lg[:, :], ALU.mult))
                        ch.link(dve.tensor_tensor(lb[:, :], ex[:, :], ex[:, :], ALU.subtract))
                        ch.link(dve.tensor_scalar(one_lb[:, :], lb[:, :], -1.0, 1.0, ALU.mult, ALU.add))

                    @block.tensor
                    def _(pe):
                        pe.wait_ge(const_in, 16 * N_CONST)
                        for m, (k, q) in enumerate(uses):
                            b0, nb = spans[q]
                            pe.wait_ge(xn_ready, b0 + nb)
                            if m >= RING:
                                pe.wait_ge(banks_free, m - RING + 1)
                            for b in range(nb):
                                n = P if q < 2 else NS
                                mm = pe.transpose(psum[:, 3 + m % RING, b * P:b * P + n],
                                                  xt[0:n, b0 + b, k * P:(k + 1) * P], ident[0:n, 0:n])
                            mm.then_inc(xt_done, 1)

        def merge_phase(tag, y0, pairs, fresh):
            N_PAIR = 2
            OUTER = 2 if fresh else 1
            LOOPS = KO // OUTER
            UNITS = 2 * N_PAIR
            scope = ExitStack()
            with scope:
                cv = Conveyor(tag, scope, (3,))
                y_hi = sb(f"{tag}_y_hi", (P, KO, NT), F32R, scope)
                y_lo = sb(f"{tag}_y_lo", (P, KO, NT), F32R, scope)
                pb = [sb(f"{tag}_product{i}", (P, NT), F32, scope) for i in range(2)]
                gt = [sb(f"{tag}_gate{i}", (P, NT), F32, scope) for i in range(2)]
                mt = sb(f"{tag}_rows", (P, NT), F32, scope)
                y_in = [sem(f"{tag}_y_in{i}", scope) for i in range(2)]
                yh_ready = sem(f"{tag}_yh_ready", scope)
                yl_ready = sem(f"{tag}_yl_ready", scope)
                rows_in = sem(f"{tag}_rows_in", scope)
                gated = sem(f"{tag}_gated", scope)
                rows_out = [sem(f"{tag}_rows_out{i}", scope) for i in range(2)]
                chain = sem(f"{tag}_chain", scope)

                def pair(p):
                    return pairs[p % len(pairs)]

                def tile_of(p, i):
                    return i * OUTER + (p if fresh else 0)

                with nc.Block() as block:
                    @block.sync
                    def _(sp):
                        def turn(i):
                            for p in range(N_PAIR):
                                _, n, w, gate = pair(p)
                                at = i * (OUTER * P) + (p * P if fresh else 0)
                                u = i * UNITS + 2 * p
                                cv.load(sp, u, 0, col(w, at))
                                cv.load(sp, u + 1, 1, col(w_in, at + gate))
                                if p == 0 and not fresh:
                                    sp.wait_ge(rows_out[0], i * 16 + 16)
                                    sp.dma_start(mt[:, :], merged_d[bass.ds(i, 1), :, :]
                                                 .rearrange("o p t -> p (o t)")).then_inc(rows_in, 16)

                        for k in range(KO):
                            if k >= 2:
                                sp.wait_ge(yl_ready, k - 1)
                            sp.dma_start(gt[k % 2][:, :], y_d[y0 + k]).then_inc(y_in[k % 2], 16)
                        with sp.Fori(0, LOOPS) as i:
                            turn(i)

                    @block.gpsimd
                    def _(pool):
                        cv.pool_start(pool)
                        with pool.Fori(0, LOOPS) as i:
                            for p in range(N_PAIR):
                                u = i * UNITS + 2 * p
                                cv.split(pool, u, 0, i * N_PAIR + p, pair(p)[1])
                                cv.split(pool, u + 1, 1, i * N_PAIR + p, KO)

                    @block.tensor
                    def _(pe):
                        cv.pe_start(pe)
                        with pe.Fori(0, LOOPS) as i:
                            for p in range(N_PAIR):
                                k0, n, _, _ = pair(p)
                                u = i * UNITS + 2 * p
                                for c in range(NCH):
                                    cv.project(pe, u, 0, c, n, y_hi[:, k0:k0 + n, :], y_lo[:, k0:k0 + n, :],
                                               each=yl_ready if c == 0 else None, k0=k0)
                                for c in range(NCH):
                                    cv.project(pe, u + 1, 1, c, KO, x_hi, x_lo)

                    @block.scalar
                    def _(act):
                        cv.act_start(act)
                        for j in range(2):
                            act.sem_inc(rows_out[j], 16)
                        act.sem_inc(gated, 2)
                        for k in range(KO):
                            act.wait_ge(y_in[k % 2], 16 * (k // 2 + 1))
                            act.activation(y_hi[:, k, :], gt[k % 2][:, :], ACT.Copy).then_inc(yh_ready, 1)
                        act.wait_ge(yl_ready, KO)
                        with act.Fori(0, LOOPS) as i:
                            for p in range(N_PAIR):
                                u = i * UNITS + 2 * p
                                act.wait_ge(gated, i * N_PAIR + p + 1)
                                if fresh:
                                    act.wait_ge(rows_out[p], i * 16 + 16)
                                for c in range(NCH):
                                    cv.empty(act, u, c, pb[p], ACT.Copy)
                                for c in range(NCH):
                                    cv.empty(act, u + 1, c, gt[p], ACT.Sigmoid)
                                if fresh:
                                    act.wait_ge(gated, i * N_PAIR + p + 3)
                                    act.dma_start(merged_d[bass.ds(i * 2 + p, 1), :, :]
                                                  .rearrange("o p t -> p (o t)"), pb[p][:, :])\
                                        .then_inc(rows_out[p], 16)
                                elif p == 1:
                                    act.wait_ge(gated, i * N_PAIR + p + 3)
                                    act.dma_start(merged_d[bass.ds(i, 1), :, :].rearrange("o p t -> p (o t)"),
                                                  mt[:, :]).then_inc(rows_out[0], 16)
                        for j in range(2 if fresh else 1):
                            act.wait_ge(rows_out[j], 16 * LOOPS + 16)

                    @block.vector
                    def _(dve):
                        ch = Chain(dve, chain)
                        for k in range(KO):
                            dve.wait_ge(yh_ready, k + 1)
                            dve.tensor_tensor(y_lo[:, k, :], gt[k % 2][:, :], y_hi[:, k, :].bitcast(F32),
                                              ALU.subtract).then_inc(yl_ready, 1)
                        with dve.Fori(0, LOOPS) as i:
                            per = 0 if fresh else N_PAIR
                            ch.loop(i * per, per)
                            for p in range(N_PAIR):
                                u = i * UNITS + 2 * p
                                cv.emptied(dve, u + 1)
                                ins = dve.tensor_tensor(pb[p][:, :], pb[p][:, :], gt[p][:, :], ALU.mult)
                                if fresh:
                                    ins.then_inc(gated, 1)
                                    continue
                                ch.link(ins)
                                if p == 0:
                                    dve.wait_ge(rows_in, i * 16 + 16)
                                else:
                                    dve.wait_ge(gated, i * N_PAIR + 3)
                                dve.tensor_tensor(mt[:, :], mt[:, :], pb[p][:, :], ALU.add).then_inc(gated, 1)
                            ch.end(LOOPS)

        def hgrn_phase():
            tag = "b"
            UNITS = 4
            scope = ExitStack()
            with scope:
                cv = Conveyor(tag, scope, (3, 4, 5, 6, 7))
                q_new = sb("b_q_new", (P, NT), F32, scope)
                f_new = sb("b_forget_new", (P, NT), F32, scope)
                v_new = sb("b_v_new", (P, NT), F32, scope)
                g_new = sb("b_gate_new", (P, NT), F32, scope)
                g_raw = sb("b_gate_raw", (P, NT), F32, scope)
                qp = sb("b_q_decayed", (P, NT), F32, scope)
                kr = sb("b_k_decayed", (P, NT), F32, scope)
                ff = sb("b_forget", (P, NT), F32, scope)
                gate = sb("b_gate", (P, NT), F32, scope)
                ft_n = [NT >> n if n <= 3 else SEQ >> n for n in range(LEVELS)]
                ft_at = [0] + [sum(ft_n[1:n]) for n in range(1, LEVELS + 1)]
                fts = sb("b_block_decay", (P, ft_at[LEVELS]), F32, scope)
                att = sb("b_att", (P, TILES + 1, P), F32, scope)
                vrow = sb("b_v_rows", (P, TILES + 1, P), F32, scope)
                krow = sb("b_k_rows", (P, TILES + 1, P), F32, scope)
                vown = sb("b_v_own", (NS, NB, P), F32, scope)
                qown = sb("b_q_own", (P, NB, NS), F32, scope)
                state = sb("b_state", (P, TILES + 1, P), F32, scope)
                s0 = sb("b_sample_state", (P, NB, P), F32, scope)
                osb = sb("b_o_rows", (P, TILES + 1, P), F32, scope)
                osq = krow
                ssq = sb("b_ssq", (P, TILES + 1), F32, scope)
                rms = sb("b_rms", (P, TILES + 1), F32, scope)
                level = sb("b_level", (P, LEVELS, P), I32, scope)
                own_row = sb("b_own_row", (NS, NB), F32, scope)
                own_col = sb("b_own_col", (P, NB, NS), F32, scope)
                const_in = sem("b_const_in", scope)
                s0_in = sem("b_s0_in", scope)
                level_ready = sem("b_level_ready", scope)
                own_ready = sem("b_own_ready", scope)
                states_ready = sem("b_states_ready", scope)
                new_states = sem("b_new_states", scope)
                stored = sem("b_stored", scope)
                gate_ready = sem("b_gate_ready", scope)
                ssq_ready = sem("b_ssq_ready", scope)
                rms_ready = sem("b_rms_ready", scope)
                o_ready = sem("b_o_ready", scope)
                y_ready = sem("b_y_ready", scope)
                y_out = sem("b_y_out", scope)
                chain = sem("b_chain", scope)
                spans = ((0, 4), (4, 4), (8, 1))
                COUNTS = (("v", 3), ("p0", 3), ("p1", 2), ("p2", 2), ("p3", 2), ("p4", 2), ("p5", 1), ("p6", 1),
                          ("p7", 1), ("k", 3), ("ds", 2), ("os", 1), ("dss", 2), ("o", 2), ("y", 3))
                M, MISC = {}, 0
                for name, n in COUNTS:
                    M[name] = MISC
                    MISC += n
                assert MISC % cv.ring == 0
                CHAIN = 17

                def level_uses(n):
                    if n == 0:
                        return ((0, 4, P), (4, 4, P), (8, 1, NS))
                    if n <= 3:
                        return ((0, 8, P), (8, 1, NS))
                    if n == 4:
                        return ((0, 4, P), (4, 4, P))
                    return ((0, 8, P),)

                def second(x, n):
                    if n == 0:
                        return x
                    return x.rearrange("p (n two m) -> p n two m", two=2, m=1 << (n - 1))[:, :, 1, :]

                with nc.Block() as block:
                    @block.sync
                    def _(sp):
                        for dst, src in ((level[:, :, :], A["c_level"]), (own_row[:, :], A["c_own_row"]),
                                         (own_col[:, :, :], A["c_own_col"])):
                            sp.dma_start(dst, src).then_inc(const_in, 16)
                        with sp.Fori(0, BH) as i:
                            for j, base in enumerate((COL_BF, COL_BQ, COL_BI, COL_BG)):
                                cv.load(sp, i * UNITS + j, j % 2, col(w_in, i * P + base))

                    @block.gpsimd
                    def _(pool):
                        cv.pool_start(pool)
                        with pool.Fori(0, BH) as i:
                            for j in range(UNITS):
                                cv.split(pool, i * UNITS + j, j % 2, i * (UNITS // 2) + j // 2, KO)

                    @block.scalar
                    def _(act):
                        cv.act_start(act)
                        act.sem_inc(stored, 32)
                        act.sem_inc(y_ready, 1)
                        act.sem_inc(y_out, 16)

                        def load_states(i):
                            act.wait_ge(stored, i * 32 + 32)
                            act.dma_start(s0[:, :, :], A["state_hgrn"][0, :, bass.ds(i, 1), :, :]
                                          .rearrange("b o k v -> k (o b) v")).then_inc(s0_in, 16)

                        def root(i):
                            act.wait_ge(ssq_ready, i + 1)
                            act.activation(rms[:, :], ssq[:, :], ACT.Sqrt, bias=eps[:, :], scale=1.0 / P)\
                                .then_inc(rms_ready, 1)

                        def store_states(i):
                            act.wait_ge(new_states, i + 1)
                            act.dma_start(OUT["hgrn_p"][0, 0, bass.ds(i, 1), :, :]
                                          .rearrange("o k v -> k (o v)"), state[:, TILES, :]).then_inc(stored, 16)
                            act.dma_start(OUT["hgrn_s"][0, :, bass.ds(i, 1), :, :]
                                          .rearrange("b o k v -> k (o b) v"), s0[:, :, :]).then_inc(stored, 16)

                        def store_y(i):
                            act.wait_ge(y_ready, i + 2)
                            act.dma_start(y_d[bass.ds(i, 1)].rearrange("o p t -> p (o t)"), gate[:, :])\
                                .then_inc(y_out, 16)

                        for j, (dst, func) in enumerate(((f_new, ACT.Sigmoid), (q_new, ACT.Copy), (v_new, ACT.Copy))):
                            for c in range(NCH):
                                cv.empty(act, j, c, dst, func)
                        for c in range(NCH):
                            cv.empty(act, 3, c, g_new, ACT.Sigmoid, raw=g_raw)
                        with act.Fori(0, BH - 1) as i:
                            u = i * UNITS + UNITS
                            load_states(i)
                            act.wait_ge(level_ready, i * 9 + 1)
                            for c in range(NCH):
                                cv.empty(act, u, c, f_new, ACT.Sigmoid)
                            act.wait_ge(level_ready, i * 9 + 2)
                            for c in range(NCH):
                                cv.empty(act, u + 1, c, q_new, ACT.Copy)
                            for c in range(NCH):
                                cv.empty(act, u + 2, c, v_new, ACT.Copy)
                            act.wait_ge(gate_ready, i + 1)
                            cv.empty(act, u + 3, 0, g_new, ACT.Sigmoid, raw=g_raw)
                            store_states(i)
                            root(i)
                            cv.empty(act, u + 3, 1, g_new, ACT.Sigmoid, raw=g_raw)
                            cv.empty(act, u + 3, 2, g_new, ACT.Sigmoid, raw=g_raw)
                            store_y(i)
                        load_states(BH - 1)
                        store_states(BH - 1)
                        root(BH - 1)
                        store_y(BH - 1)
                        act.wait_ge(stored, 32 * BH + 32)
                        act.wait_ge(y_out, 16 * BH + 16)

                    @block.tensor
                    def _(pe):
                        cv.pe_start(pe)
                        pe.wait_ge(const_in, 48)

                        def product(i, n):
                            if n == 0:
                                cv.emptied(pe, i * UNITS + 1)
                            pe.wait_ge(level_ready, i * 9 + 1 + n)
                            q = q_new if n == 0 else qp
                            for m, (b0, nb, w) in enumerate(level_uses(n)):
                                bank = cv.fill(pe, i * MISC, M[f"p{n}"] + m, w < P)
                                wq = w if n == 0 else w // 2
                                for b in range(nb):
                                    ts = slice((b0 + b) * P, (b0 + b) * P + w)
                                    mm = pe.matmul(bank[0:w, b * wq:(b + 1) * wq], kr[:, ts],
                                                   second(q[:, ts], n), start=True, stop=True)
                                mm.then_inc(cv.misc_done, 1)

                        def rows_of(i, src, m):
                            for q, (b0, nb) in enumerate(spans):
                                bank = cv.fill(pe, i * MISC, m + q, q == 2)
                                w = P if q < 2 else NS
                                for b in range(nb):
                                    mm = pe.transpose(bank[0:w, b * P:b * P + P],
                                                      src[:, (b0 + b) * P:(b0 + b) * P + w], ident[:, :])
                                mm.then_inc(cv.misc_done, 1)

                        def own_states(i):
                            cv.copied(pe, i * MISC, M["k"] + 2)
                            for q in range(2):
                                bank = cv.fill(pe, i * MISC, M["ds"] + q)
                                for b in range(4):
                                    mm = pe.matmul(bank[:, b * P:(b + 1) * P], krow[:, 4 * q + b, :],
                                                   vrow[:, 4 * q + b, :], start=True, stop=True)
                                mm.then_inc(cv.misc_done, 1)
                            pe.wait_ge(own_ready, i + 1)
                            pe.wait_ge(s0_in, i * 16 + 16)
                            bank = cv.fill(pe, i * MISC, M["os"], True)
                            pe.matmul(bank[0:NS, 0:P], att[0:NS, TILES, 0:NS], vrow[0:NS, TILES, :],
                                      start=True, stop=False)
                            for b in range(NB):
                                mm = pe.matmul(bank[0:NS, 0:P], qown[:, b, :], s0[:, b, :],
                                               start=False, stop=(b == NB - 1))
                            mm.then_inc(cv.misc_done, 1)
                            for q in range(2):
                                bank = cv.fill(pe, i * MISC, M["dss"] + q, True)
                                pe.matmul(bank[:, :], krow[0:NS, TILES, :], vown[:, 4 * q:4 * q + 4, :],
                                          start=True, stop=True).then_inc(cv.misc_done, 1)

                        def outputs(i):
                            pe.wait_ge(states_ready, i + 1)
                            for q in range(2):
                                bank = cv.fill(pe, i * MISC, M["o"] + q)
                                for b in range(4):
                                    t = 4 * q + b
                                    mm = pe.matmul(bank[:, b * P:(b + 1) * P], att[:, t, :], vrow[:, t, :],
                                                   start=True, stop=(t == 0))
                                    if t > 0:
                                        mm = pe.matmul(bank[:, b * P:(b + 1) * P], qp[:, t * P:(t + 1) * P],
                                                       state[:, t, :], start=False, stop=True)
                                mm.then_inc(cv.misc_done, 1)

                        def back(i):
                            pe.wait_ge(o_ready, i + 1)
                            for q, (b0, nb) in enumerate(spans):
                                bank = cv.fill(pe, i * MISC, M["y"] + q, q == 2)
                                w = P if q < 2 else NS
                                for b in range(nb):
                                    mm = pe.transpose(bank[:, b * P:b * P + w], osb[0:w, b0 + b, :],
                                                      ident[0:w, 0:w])
                                mm.then_inc(cv.misc_done, 1)

                        def start(i):
                            cv.emptied(pe, i * UNITS + 2)
                            rows_of(i, v_new, M["v"])
                            product(i, 0)

                        for j in range(UNITS):
                            for c in range(NCH):
                                cv.project(pe, j, j % 2, c, KO, x_hi, x_lo)
                        with pe.Fori(0, BH - 1) as i:
                            u = i * UNITS + UNITS
                            start(i)
                            cv.project(pe, u, 0, 0, KO, x_hi, x_lo)
                            product(i, 1)
                            cv.project(pe, u, 0, 1, KO, x_hi, x_lo)
                            product(i, 2)
                            cv.project(pe, u, 0, 2, KO, x_hi, x_lo)
                            product(i, 3)
                            cv.project(pe, u + 1, 1, 0, KO, x_hi, x_lo)
                            product(i, 4)
                            cv.project(pe, u + 1, 1, 1, KO, x_hi, x_lo)
                            product(i, 5)
                            cv.project(pe, u + 1, 1, 2, KO, x_hi, x_lo)
                            product(i, 6)
                            cv.project(pe, u + 2, 0, 0, KO, x_hi, x_lo)
                            product(i, 7)
                            cv.project(pe, u + 2, 0, 1, KO, x_hi, x_lo)
                            pe.wait_ge(level_ready, i * 9 + 9)
                            rows_of(i, kr, M["k"])
                            cv.project(pe, u + 2, 0, 2, KO, x_hi, x_lo)
                            own_states(i)
                            cv.project(pe, u + 3, 1, 0, KO, x_hi, x_lo)
                            outputs(i)
                            cv.project(pe, u + 3, 1, 1, KO, x_hi, x_lo)
                            cv.project(pe, u + 3, 1, 2, KO, x_hi, x_lo)
                            back(i)
                        start(BH - 1)
                        for n in range(1, LEVELS):
                            product(BH - 1, n)
                        pe.wait_ge(level_ready, 9 * BH)
                        rows_of(BH - 1, kr, M["k"])
                        own_states(BH - 1)
                        outputs(BH - 1)
                        back(BH - 1)

                    @block.vector
                    def _(dve):
                        ch = Chain(dve, chain)
                        cv.dve_start(dve)
                        ch.step(dve.memset(osb[:, :, :], 0.0))
                        ch.link(dve.memset(att[:, :, :], 0.0))
                        dve.wait_ge(const_in, 48)
                        with dve.Fori(0, BH) as i:
                            ch.loop(i * CHAIN, CHAIN)
                            u, m0 = i * UNITS, i * MISC

                            def take(n):
                                if n > 0:
                                    cv.copied(dve, m0, M[f"p{n}"] - 1)
                                for m, (b0, nb, w) in enumerate(level_uses(n)):
                                    bank = cv.filled(dve, m0, M[f"p{n}"] + m, n > 0)
                                    if n == 0:
                                        dve.tensor_tensor(att[0:w, b0:b0 + nb, 0:w],
                                                          bank[0:w, 0:nb * w].rearrange("p (a b) -> p a b", b=w),
                                                          ident[0:w, 0:w].unsqueeze(1).broadcast_to([w, nb, w]),
                                                          ALU.mult).then_inc(cv.misc_free, 1)
                                        continue
                                    hf = 1 << (n - 1)
                                    nx = w // (2 * hf)

                                    def halves(x):
                                        return x.rearrange("p a (x two m) -> p a x two m", two=2, m=hf)[:, :, :, 1, :]

                                    dst = halves(att[0:w, b0:b0 + nb, 0:w])
                                    msk = halves(level[0:w, n:n + 1, 0:w]).broadcast_to([w, nb, nx, hf])
                                    src = bank[0:w, 0:nb * w // 2].rearrange("p (a x m) -> p a x m", a=nb, m=hf)
                                    dve.copy_predicated(dst, msk, src).then_inc(cv.misc_free, 1)

                            def update(n):
                                dve.wait_ge(cv.misc_done, m0 + M[f"p{n}"] + len(level_uses(n)))
                                dve.wait_ge(level_ready, i * 9 + n + 1)
                                if n == 0:
                                    dve.tensor_tensor(qp[:, :], q_new[:, :], ff[:, :], ALU.mult)\
                                        .then_inc(level_ready, 1)
                                    return
                                nt = NT if n <= 3 else SEQ
                                nb, half_ = nt >> n, 1 << (n - 1)
                                prev = ff if n == 1 else fts[:, ft_at[n - 1]:ft_at[n - 1] + ft_n[n - 1]]
                                fv = prev[:, 0:2 * nb].rearrange("p (n two) -> p n two", two=2)
                                qv = qp[:, 0:nt].rearrange("p (n two m) -> p n two m", two=2, m=half_)
                                kv = kr[:, 0:nt].rearrange("p (n two m) -> p n two m", two=2, m=half_)
                                ch.step(dve.tensor_tensor(fts[:, ft_at[n]:ft_at[n] + nb], fv[:, :, 0], fv[:, :, 1],
                                                          ALU.mult))
                                dve.tensor_tensor(qv[:, :, 1, :], qv[:, :, 1, :],
                                                  fv[:, :, 0:1].broadcast_to([P, nb, half_]), ALU.mult)
                                dve.tensor_tensor(kv[:, :, 0, :], kv[:, :, 0, :],
                                                  fv[:, :, 1:2].broadcast_to([P, nb, half_]), ALU.mult)\
                                    .then_inc(level_ready, 1)

                            def rows_to(dst, m):
                                for q, (b0, nb) in enumerate(spans):
                                    bank = cv.filled(dve, m0, m + q)
                                    w = P if q < 2 else NS
                                    dve.tensor_copy(dst[0:w, b0:b0 + nb, :], bank[0:w, 0:nb * P]
                                                    .rearrange("p (a b) -> p a b", b=P)).then_inc(cv.misc_free, 1)

                            cv.emptied(dve, u)
                            ch.link(dve.tensor_scalar(ff[:, :], f_new[:, :], one_lb[:, bass.ds(i, 1)],
                                                      lb[:, bass.ds(i, 1)], ALU.mult, ALU.add))
                            dve.tensor_scalar(kr[:, :], ff[:, :], -1.0, 1.0, ALU.mult, ALU.add)\
                                .then_inc(level_ready, 1)
                            rows_to(vrow, M["v"])
                            for n in range(4):
                                update(n)
                                take(n)
                            ch.step(dve.tensor_tensor(
                                vown[:, :, :], vrow[0:NS, TILES:TILES + 1, :].broadcast_to([NS, NB, P]),
                                own_row[:, :].unsqueeze(2).broadcast_to([NS, NB, P]), ALU.mult))
                            dve.wait_ge(level_ready, i * 9 + 5)
                            dve.tensor_tensor(qown[:, :, :], qp[:, SEQ:NT].unsqueeze(1)
                                              .broadcast_to([P, NB, NS]), own_col[:, :, :], ALU.mult)\
                                .then_inc(own_ready, 1)
                            for n in range(4, LEVELS):
                                update(n)
                                take(n)
                            cv.emptied(dve, u + 3)
                            dve.wait_ge(y_out, i * 16 + 16)
                            dve.tensor_tensor(gate[:, :], g_new[:, :], g_raw[:, :], ALU.mult)\
                                .then_inc(gate_ready, 1)
                            rows_to(krow, M["k"])
                            f7 = fts[:, ft_at[7]:ft_at[7] + TILES]
                            f3 = fts[:, ft_at[3] + SEQ // TB:ft_at[3] + NT // TB]
                            dve.wait_ge(stored, i * 32 + 32)
                            for t in range(TILES):
                                if t % 4 == 0:
                                    bank = cv.filled(dve, m0, M["ds"] + t // 4)
                                src = bank[:, (t % 4) * P:(t % 4 + 1) * P]
                                if t == 0:
                                    ch.step(dve.tensor_copy(state[:, 1, :], src))
                                    continue
                                ch.wait()
                                ins = dve.scalar_tensor_tensor(
                                    out=state[:, t + 1, :], in0=state[:, t, :], scalar=f7[:, t:t + 1],
                                    in1=src, op0=ALU.mult, op1=ALU.add)
                                if t == 3:
                                    ins.then_inc(cv.misc_free, 1)
                                    cv.copied(dve, m0, M["ds"])
                                elif t == TILES - 1:
                                    ins.then_inc(cv.misc_free, 1)
                                else:
                                    ch.step(ins)
                            cv.copied(dve, m0, M["ds"] + 1)
                            dve.sem_inc(states_ready, 1)
                            bank = cv.filled(dve, m0, M["os"])
                            dve.tensor_copy(osb[0:NS, TILES, :], bank[0:NS, 0:P]).then_inc(cv.misc_free, 1)
                            for q in range(2):
                                bank = cv.filled(dve, m0, M["dss"] + q)
                                for b in range(4 * q, 4 * q + 4):
                                    ins = dve.scalar_tensor_tensor(
                                        out=s0[:, b, :], in0=s0[:, b, :], scalar=f3[:, b:b + 1],
                                        in1=bank[:, (b % 4) * P:(b % 4 + 1) * P], op0=ALU.mult, op1=ALU.add)
                                ins.then_inc(cv.misc_free, 1)
                            cv.copied(dve, m0, M["dss"] + 1)
                            dve.sem_inc(new_states, 1)
                            for q in range(2):
                                bank = cv.filled(dve, m0, M["o"] + q)
                                dve.tensor_copy(osb[:, 4 * q:4 * q + 4, :],
                                                bank[:, :].rearrange("p (a b) -> p a b", b=P))\
                                    .then_inc(cv.misc_free, 1)
                            cv.copied(dve, m0, M["o"] + 1)
                            ch.link(dve.tensor_tensor(osq[:, :, :], osb[:, :, :], osb[:, :, :], ALU.mult))
                            dve.tensor_reduce(ssq[:, :], osq[:, :, :], AX.X, ALU.add).then_inc(ssq_ready, 1)
                            dve.wait_ge(rms_ready, i + 1)
                            ch.link(dve.reciprocal(rms[:, :], rms[:, :]))
                            dve.tensor_tensor(osb[:, :, :], osb[:, :, :],
                                              rms[:, :].unsqueeze(2).broadcast_to([P, TILES + 1, P]), ALU.mult)\
                                .then_inc(o_ready, 1)
                            dve.wait_ge(gate_ready, i + 1)
                            for q, (b0, nb) in enumerate(spans):
                                bank = cv.filled(dve, m0, M["y"] + q)
                                n = nb * P if q < 2 else NS
                                ts = slice(b0 * P, b0 * P + n)
                                dve.scalar_tensor_tensor(out=gate[:, ts], in0=bank[:, 0:n], scalar=h_norm[:, :],
                                                         in1=gate[:, ts], op0=ALU.mult, op1=ALU.mult)\
                                    .then_inc(cv.misc_free, 1)
                            cv.copied(dve, m0, M["y"] + 2)
                            dve.sem_inc(y_ready, 1)
                            ch.end(BH)

        def attention_phase(q_s, k_s, gate_s):
            UNITS, MISC = 10, 39
            scope = ExitStack()
            with scope:
                cv = Conveyor("a", scope, (3, 4, 7))
                R = cv.ring
                qk = [sb(f"a_feature{i}", (P, NT), F32, scope) for i in range(4)]
                vrow = [sb(f"a_v_rows{g}", (P, TILES + 1, P), F32, scope) for g in range(AG)]
                krow = sb("a_k_rows", (P, TILES + 1, P), F32, scope)
                gate = sb("a_gate", (P, NT), F32, scope)
                graw = sb("a_gate_raw", (P, NT), F32, scope)
                T_COLS = [[P] + [2 * P] * 7, [P, 2 * P] * 4, [P] * 8]
                T_AT, at = [], 0
                for g in range(AG):
                    row = []
                    for w in T_COLS[g]:
                        row.append(at)
                        at += w
                    T_AT.append(row)
                prob = sb("a_prob", (P, at), F32, scope)
                pt = [sb(f"a_prob_t{i}", (P, 4, P), F32, scope) for i in range(2)]
                mx = sb("a_max", (P, AG, TILES), F32, scope)
                st = sb("a_stats", (P, AG, TILES, 2), F32, scope)
                comm = sb("a_stats_by_token", (P, TILES, 2, 2), F32, scope)
                nmin = sb("a_least", (P, TILES), F32, scope)
                ex = sb("a_group_exp", (P, AG, TILES), F32, scope)
                lw = sb("a_group_sum", (P, AG, TILES), F32, scope)
                den = sb("a_denominator", (P, TILES), F32, scope)
                wt = sb("a_weight", (P, TILES, 2), F32, scope)
                w0 = sb("a_weight0", (P, TILES), F32, scope)
                w12 = sb("a_weight12", (P, 2, TILES), F32, scope)
                yt = graw

                scores_max = sem("a_negmax_ready", scope)
                exp_done = sem("a_exp_done", scope)
                stats_out = sem("a_stats_out", scope)
                stats_in = sem("a_stats_in", scope)
                spread = sem("a_spread_ready", scope)
                group_exp = sem("a_group_exp_ready", scope)
                weights_ready = sem("a_weights_ready", scope)
                weights_out = sem("a_weights_out", scope)
                weights_in = sem("a_weights_in", scope)
                scaled = sem("a_prob_scaled", scope)
                krow_ready = sem("a_krow_ready", scope)
                krow_out = sem("a_krow_out", scope)
                vrow_out = sem("a_vrow_out", scope)
                o_done = sem("a_o_done", scope)
                y_ready = sem("a_y_ready", scope)
                y_out = sem("a_y_out", scope)
                chain = sem("a_chain", scope)
                CHAIN = 51
                spans = ((0, 4), (4, 4), (8, 1))
                COLS = [COL_AQ, COL_AK, COL_AQ + GROUP, COL_AK + GROUP, COL_AQ + 2 * GROUP,
                        COL_AK + 2 * GROUP, COL_AV, COL_AV + GROUP, COL_AV + 2 * GROUP, COL_AG]
                DST = [qk[0], qk[1], qk[2], qk[3], qk[0], qk[1], qk[2], qk[3], qk[0], gate]
                U_Q, U_K, U_V, U_G = (0, 2, 4), (1, 3, 5), (6, 7, 8), 9
                M_S, M_K, M_V, M_P = (0, 7, 14), (4, 11, 18), (21, 24, 27), 30
                N_KV_OUT = (2, 2, 2)
                V_OUT = 16 * 6

                def tokens(src, g, c):
                    if g == 0:
                        return src[:, c * P:(c + 1) * P]
                    if g == 1:
                        r, n = c // 2, c % 2
                        return src[:, 4 * P * n + r:4 * P * n + r + 4 * (P - 1) + 1:4]
                    return src[:, c:c + 8 * (P - 1) + 1:8]

                def keys(src, g, c):
                    if g == 0 and c > 0:
                        return src[:, (c - 1) * P:(c + 1) * P]
                    if g == 1 and c % 2 == 1:
                        return src[:, c // 2:c // 2 + 4 * (2 * P - 1) + 1:4]
                    return tokens(src, g, c)

                BLOCKS = []
                for g in range(AG):
                    for c in range(TILES):
                        w = T_COLS[g][c] // P
                        for b in range(w):
                            BLOCKS.append((g, c, T_AT[g][c] + b * P, c - (w - 1) + b))
                N_PT = (len(BLOCKS) + 3) // 4

                def kv_out(g, rows, which, h, b0):
                    dst = OUT[("kv128_p", "kv512_p", "kv2048_p")[g]][0, 0, rows, which, bass.ds(h, 1), :]
                    return dst

                with nc.Block() as block:
                    @block.sync
                    def _(sp):
                        with sp.Fori(0, AH) as h:
                            for j in range(UNITS):
                                cv.load(sp, h * UNITS + j, j % 2, col(w_in, h * P + COLS[j]))
                            sp.wait_ge(exp_done, h * AG + AG)
                            d = stat_d[bass.ds(h, 1)]
                            sp.dma_start(d[:, :, 0, :].rearrange("o (n i r) s -> i (o r) n s", n=2, r=4),
                                         st[:, 1, :, :].rearrange("p (r n) s -> p r n s", n=2),
                                         allow_slow_non_contiguous=True).then_inc(stats_out, 16)
                            sp.dma_start(d[:, :, 1, :].rearrange("o (i j) s -> i (o j) s", j=8),
                                         st[:, 2, :, :], allow_slow_non_contiguous=True).then_inc(stats_out, 16)
                            sp.wait_ge(stats_out, h * 32 + 32)
                            sp.dma_start(comm[:, :, :, :], d.rearrange("o (b p) g s -> p (o b) g s", p=P),
                                         allow_slow_non_contiguous=True).then_inc(stats_in, 16)
                            sp.wait_ge(weights_ready, h + 1)
                            d = weight_d[bass.ds(h, 1)]
                            sp.dma_start(d.rearrange("o (b p) g -> p (o b) g", p=P), wt[:, :, :],
                                         allow_slow_non_contiguous=True).then_inc(weights_out, 16)
                            sp.wait_ge(weights_out, h * 16 + 16)
                            for n in range(2):
                                sp.dma_start(w12[:, 0, n:TILES:2],
                                             d[:, :, 0].rearrange("o (n i r) -> n i (o r)", n=2, r=4)[n],
                                             allow_slow_non_contiguous=True).then_inc(weights_in, 16)
                            sp.dma_start(w12[:, 1, :], d[:, :, 1].rearrange("o (i j) -> i (o j)", j=8),
                                         allow_slow_non_contiguous=True).then_inc(weights_in, 16)

                    @block.gpsimd
                    def _(pool):
                        cv.pool_start(pool)
                        with pool.Fori(0, AH) as h:
                            for j in range(UNITS):
                                cv.split(pool, h * UNITS + j, j % 2, h * (UNITS // 2) + j // 2, KO)

                    @block.tensor
                    def _(pe):
                        cv.pe_start(pe)
                        with pe.Fori(0, AH) as h:
                            u, m0 = h * UNITS, h * MISC

                            def unit(j):
                                for c in range(NCH):
                                    cv.project(pe, u + j, j % 2, c, KO, x_hi, x_lo)

                            def scores(g):
                                cv.emptied(pe, u + U_K[g])
                                for n in range(4):
                                    bank = cv.fill(pe, m0, M_S[g] + n)
                                    for c in (2 * n, 2 * n + 1):
                                        w = T_COLS[g][c]
                                        a = (c % 2) * 2 * P
                                        mm = pe.matmul(bank[:, a:a + w], tokens(DST[U_Q[g]], g, c),
                                                       keys(DST[U_K[g]], g, c), start=True, stop=True)
                                    mm.then_inc(cv.misc_done, 1)

                            def rows(src, m, g):
                                for q, (b0, nb) in enumerate(spans):
                                    bank = cv.fill(pe, m0, m + q, q == 2)
                                    for b in range(b0, b0 + nb):
                                        if b == TILES:
                                            mm = pe.transpose(bank[0:NS, 0:P], src[:, SEQ:NT], ident[:, :])
                                        else:
                                            mm = pe.transpose(bank[:, (b % 4) * P:(b % 4 + 1) * P],
                                                              tokens(src, g, b), ident[:, :])
                                    mm.then_inc(cv.misc_done, 1)

                            def v_rows(g):
                                cv.emptied(pe, u + U_V[g])
                                rows(DST[U_V[g]], M_V[g], g)

                            unit(0)
                            unit(1)
                            unit(2)
                            scores(0)
                            rows(DST[U_K[0]], M_K[0], 0)
                            unit(3)
                            unit(4)
                            scores(1)
                            rows(DST[U_K[1]], M_K[1], 0)
                            unit(5)
                            unit(6)
                            scores(2)
                            rows(DST[U_K[2]], M_K[2], 0)
                            unit(7)
                            v_rows(0)
                            unit(8)
                            v_rows(1)
                            unit(9)
                            v_rows(2)

                            def turn(n):
                                bank = cv.fill(pe, m0, M_P + n)
                                for b, (g, c, at, kb) in enumerate(BLOCKS[4 * n:4 * n + 4]):
                                    mm = pe.transpose(bank[:, b * P:(b + 1) * P], prob[:, at:at + P], ident[:, :])
                                mm.then_inc(cv.misc_done, 1)

                            def values(n):
                                cv.copied(pe, m0, M_P + n)
                                mm = None
                                for b, (g, c, at, kb) in enumerate(BLOCKS[4 * n:4 * n + 4]):
                                    rhs = pt[n % 2][:, b, :]
                                    v = vrow[g][:, kb, :]
                                    if g == 0:
                                        mm = pe.matmul(psum[:, 5 + c // 4, (c % 4) * P:(c % 4 + 1) * P], v, rhs,
                                                       start=(c % 4 == 0 and kb == max(c - 1, 0)), stop=False,
                                                       skip_group_check=True)
                                    elif g == 1:
                                        mm = pe.matmul(psum[:, 5 + c % 2, c // 2:c // 2 + 4 * (P - 1) + 1:4], v, rhs,
                                                       start=False, stop=False, skip_group_check=True)
                                    else:
                                        for k in range(2):
                                            mm = pe.matmul(psum[:, 5 + k, c:c + 8 * 63 + 1:8], v,
                                                           rhs[:, 64 * k:64 * k + 64], start=False,
                                                           stop=(c == TILES - 1), skip_group_check=True)
                                return mm

                            pe.wait_ge(scaled, h + 1)
                            pe.wait_ge(y_ready, h + 1)
                            turn(0)
                            for n in range(1, N_PT):
                                turn(n)
                                values(n - 1)
                            values(N_PT - 1).then_inc(o_done, 1)

                    @block.scalar
                    def _(act):
                        cv.act_start(act)
                        act.sem_inc(y_ready, 1)
                        act.sem_inc(y_out, 16)
                        act.sem_inc(krow_out, 32)
                        act.sem_inc(vrow_out, V_OUT)
                        with act.Fori(0, AH) as h:
                            u = h * UNITS

                            def unit(j):
                                for c in range(NCH):
                                    cv.empty(act, u + j, c, DST[j], ACT.Copy)

                            def exps(g):
                                act.wait_ge(scores_max, h * AG + g + 1)
                                for c in range(TILES):
                                    a, w = T_AT[g][c], T_COLS[g][c]
                                    ins = act.activation(prob[:, a:a + w], prob[:, a:a + w], ACT.Exp,
                                                         bias=st[:, g, c, 0:1], scale=SCALE,
                                                         accum_out=st[:, g, c, 1:2])
                                ins.then_inc(exp_done, 1)

                            def rows_out(g, which, src, done):
                                o = OUT[("kv128_p", "kv512_p", "kv2048_p")[g]]
                                hd = bass.ds(h, 1)
                                if g == 0:
                                    act.dma_start(o[0, 0, :, which, hd, :], src[:, TILES - 1:TILES, :]).then_inc(done, 16)
                                elif which == 0:
                                    b0 = 4 if g == 1 else 0
                                    act.dma_start(o[0, 0, :, which, hd, :].rearrange("(b p) o e -> p b (o e)", p=P),
                                                  src[:, b0:TILES, :]).then_inc(done, 16)
                                elif g == 1:
                                    act.dma_start(o[0, 0, :, which, hd, :].rearrange("(i r) o e -> i r (o e)", r=4),
                                                  src[:, 1:TILES:2, :]).then_inc(done, 16)
                                else:
                                    act.dma_start(o[0, 0, :, which, hd, :].rearrange("(i j) o e -> i j (o e)", j=8),
                                                  src[:, 0:TILES, :]).then_inc(done, 16)
                                o = OUT[("kv128_s", "kv512_s", "kv2048_s")[g]]
                                act.dma_start(o[0, :, :, which, hd, :].rearrange("b t o e -> (b t) (o e)"),
                                              src[0:NS, TILES, :]).then_inc(done, 16)

                            unit(0)
                            unit(1)
                            unit(2)
                            unit(3)
                            exps(0)
                            act.wait_ge(krow_ready, h * 6 + 1)
                            rows_out(0, 0, krow, krow_out)
                            unit(4)
                            unit(5)
                            exps(1)
                            act.wait_ge(krow_ready, h * 6 + 2)
                            rows_out(1, 0, krow, krow_out)
                            unit(6)
                            unit(7)
                            exps(2)
                            act.wait_ge(krow_ready, h * 6 + 3)
                            rows_out(2, 0, krow, krow_out)
                            act.wait_ge(spread, h + 1)
                            act.activation(ex[:, :, :], ex[:, :, :], ACT.Exp).then_inc(group_exp, 1)
                            unit(8)
                            act.wait_ge(krow_ready, h * 6 + 4)
                            rows_out(0, 1, vrow[0], vrow_out)
                            act.wait_ge(y_out, h * 16 + 16)
                            for c in range(NCH):
                                cv.empty(act, u + U_G, c, gate, ACT.Sigmoid, raw=graw)
                            act.wait_ge(krow_ready, h * 6 + 5)
                            rows_out(1, 1, vrow[1], vrow_out)
                            act.wait_ge(krow_ready, h * 6 + 6)
                            rows_out(2, 1, vrow[2], vrow_out)
                            act.wait_ge(y_ready, h + 2)
                            act.dma_start(y_d[bass.ds(h + Y_A, 1), :, 0:SEQ].rearrange("o p t -> p (o t)"),
                                          yt[:, 0:SEQ]).then_inc(y_out, 16)
                        act.wait_ge(y_out, 16 * AH + 16)
                        act.wait_ge(krow_out, 96 * AH + 32)
                        act.wait_ge(vrow_out, V_OUT * AH + V_OUT)

                    @block.vector
                    def _(dve):
                        ch = Chain(dve, chain)
                        cv.dve_start(dve)
                        with dve.Fori(0, AH) as h:
                            ch.loop(h * CHAIN, CHAIN)
                            u, m0 = h * UNITS, h * MISC

                            def scores(g):
                                cv.emptied(dve, u + U_K[g])
                                for dst, src in ((q_s, DST[U_Q[g]]), (k_s, DST[U_K[g]])):
                                    ch.step(dve.tensor_copy(dst[:, g, bass.ds(h, 1), :]
                                                            .rearrange("p o t -> p (o t)"), src[:, SEQ:NT]))
                                for n in range(4):
                                    bank = cv.filled(dve, m0, M_S[g] + n)
                                    for c in (2 * n, 2 * n + 1):
                                        a, w = T_AT[g][c], T_COLS[g][c]
                                        mask = pair[:, :] if g == 2 else band[:, 2 * P - w:2 * P]
                                        ps_ = bank[:, (c % 2) * 2 * P:(c % 2) * 2 * P + w]
                                        ins = dve.tensor_tensor(prob[:, a:a + w], ps_, mask, ALU.add)
                                        if c % 2:
                                            ins.then_inc(cv.misc_free, 1)
                                cv.copied(dve, m0, M_S[g] + 3)
                                if g == 0:
                                    parts = ((0, 1, 1, P), (1, 7, 1, 2 * P))
                                elif g == 1:
                                    parts = ((0, 4, 2, P), (1, 4, 2, 2 * P))
                                else:
                                    parts = ((0, 8, 1, P),)
                                for c0, n, step, w in parts:
                                    if g == 1:
                                        pv = prob[:, T_AT[1][0]:T_AT[1][0] + 12 * P]\
                                            .rearrange("p (n w) -> p n w", w=3 * P)[:, :, c0 * P:c0 * P + w]
                                    else:
                                        pv = prob[:, T_AT[g][c0]:T_AT[g][c0] + n * w].rearrange("p (n w) -> p n w", w=w)
                                    ch.step(dve.tensor_reduce(mx[:, g, c0:c0 + step * (n - 1) + 1:step], pv,
                                                              AX.X, ALU.max))
                                ch.wait()
                                dve.tensor_scalar(st[:, g, :, 0], mx[:, g, :], -SCALE, None, ALU.mult)\
                                    .then_inc(scores_max, 1)

                            def rows(dst, m):
                                for q, (b0, nb) in enumerate(spans):
                                    bank = cv.filled(dve, m0, m + q)
                                    w = P if q < 2 else NS
                                    dve.tensor_copy(dst[0:w, b0:b0 + nb, :], bank[0:w, 0:nb * P]
                                                    .rearrange("p (a b) -> p a b", b=P)).then_inc(cv.misc_free, 1)
                                cv.copied(dve, m0, m + 2)
                                dve.sem_inc(krow_ready, 1)

                            scores(0)
                            dve.wait_ge(krow_out, h * 96 + 32)
                            rows(krow, M_K[0])
                            scores(1)
                            dve.wait_ge(krow_out, h * 96 + 64)
                            rows(krow, M_K[1])
                            scores(2)
                            dve.wait_ge(krow_out, h * 96 + 96)
                            rows(krow, M_K[2])
                            dve.wait_ge(exp_done, h * AG + AG)
                            dve.wait_ge(stats_in, h * 16 + 16)
                            nm = [st[:, 0, :, 0], comm[:, :, 0, 0], comm[:, :, 1, 0]]
                            ls = [st[:, 0, :, 1], comm[:, :, 0, 1], comm[:, :, 1, 1]]
                            ch.link(dve.tensor_tensor(nmin[:, :], nm[0], nm[1], ALU.min))
                            ch.link(dve.tensor_tensor(nmin[:, :], nmin[:, :], nm[2], ALU.min))
                            for g in range(AG):
                                ch.step(dve.tensor_tensor(ex[:, g, :], nmin[:, :], nm[g], ALU.subtract))
                            ch.wait()
                            dve.sem_inc(spread, 1)
                            dve.wait_ge(group_exp, h + 1)
                            for g in range(AG):
                                ch.step(dve.tensor_tensor(lw[:, g, :], ex[:, g, :], ls[g], ALU.mult))
                            ch.wait()
                            ch.link(dve.tensor_tensor(den[:, :], lw[:, 0, :], lw[:, 1, :], ALU.add))
                            ch.link(dve.tensor_tensor(den[:, :], den[:, :], lw[:, 2, :], ALU.add))
                            ch.link(dve.reciprocal(den[:, :], den[:, :]))
                            ch.step(dve.tensor_tensor(w0[:, :], ex[:, 0, :], den[:, :], ALU.mult))
                            for g in (1, 2):
                                ch.step(dve.tensor_tensor(wt[:, :, g - 1], ex[:, g, :], den[:, :], ALU.mult))
                            ch.wait()
                            dve.sem_inc(weights_ready, 1)
                            dve.wait_ge(vrow_out, h * V_OUT + V_OUT)
                            rows(vrow[0], M_V[0])
                            rows(vrow[1], M_V[1])
                            dve.wait_ge(weights_in, h * 48 + 48)
                            for g in range(AG):
                                for c in range(TILES):
                                    a, w = T_AT[g][c], T_COLS[g][c]
                                    sc = w0[:, c:c + 1] if g == 0 else w12[:, g - 1, c:c + 1]
                                    ch.step(dve.tensor_scalar(prob[:, a:a + w], prob[:, a:a + w], sc, None, ALU.mult))
                            ch.wait()
                            dve.sem_inc(scaled, 1)
                            rows(vrow[2], M_V[2])
                            cv.emptied(dve, u + U_G)
                            ch.link(dve.tensor_tensor(gate[:, :], gate[:, :], graw[:, :], ALU.mult))
                            ch.step(dve.tensor_copy(gate_s[:, bass.ds(h, 1), :].rearrange("p o t -> p (o t)"),
                                                    gate[:, SEQ:NT]))
                            for n in range(N_PT):
                                bank = cv.filled(dve, m0, M_P + n)
                                nb = min(4, len(BLOCKS) - 4 * n)
                                dve.tensor_copy(pt[n % 2][:, 0:nb, :], bank[:, 0:nb * P]
                                                .rearrange("p (a b) -> p a b", b=P)).then_inc(cv.misc_free, 1)
                            dve.wait_ge(o_done, h + 1)
                            dve.tensor_tensor(yt[:, 0:SEQ], psum[:, 5:7, :].rearrange("p a b -> p (a b)"),
                                              gate[:, 0:SEQ], ALU.mult).then_inc(y_ready, 1)
                            ch.end(AH)

        def sample_attention(q_s, k_s, gate_s):
            KB = 4
            KW = KB * P + AG * NS
            K_G = (0, 1, 1, 2)
            MISC = 12
            scope = ExitStack()
            with scope:
                mask = sb("s_mask", (NS, KW), F32, scope)
                kc = [sb(f"s_k_cache{i}", (P, KB, P), F32, scope) for i in range(NB)]
                vc = [sb(f"s_v_cache{i}", (P, KB, P), F32, scope) for i in range(NB)]
                vn = sb("s_v_new", (NS, AG, P), F32, scope)
                qh = sb("s_q_head", (P, AG, NS), F32, scope)
                kh = sb("s_k_head", (P, AG, NS), F32, scope)
                gh = sb("s_gate_head", (P, NS), F32, scope)
                kt = [sb(f"s_k_feature{i}", (P, KB, P), F32, scope) for i in range(2)]
                sct = sb("s_scores_t", (P, KB, NS), F32, scope)
                prob = sb("s_prob", (NS, KW), F32, scope)
                pt = sb("s_prob_t", (P, KB + AG, NS), F32, scope)
                mx = sb("s_max", (NS, 1), F32, scope)
                nm = sb("s_negmax", (NS, 1), F32, scope)
                sm = sb("s_sum", (NS, 1), F32, scope)
                yt = sb("s_y", (P, NS), F32, scope)
                const_in = sem("s_const_in", scope)
                k_in = [sem(f"s_k_in{b}", scope) for b in range(NB)]
                v_in = [sem(f"s_v_in{b}", scope) for b in range(NB)]
                vn_in = sem("s_v_new_in", scope)
                head_ready = sem("s_head_ready", scope)
                misc_done = sem("s_misc_done", scope)
                misc_free = sem("s_misc_free", scope)
                scores_done = sem("s_scores_done", scope)
                scores_out = sem("s_scores_copied", scope)
                negmax = sem("s_negmax_ready", scope)
                exp_done = sem("s_exp_done", scope)
                prob_ready = sem("s_prob_ready", scope)
                o_done = sem("s_o_done", scope)
                y_ready = sem("s_y_ready", scope)
                y_out = sem("s_y_out", scope)
                chain = sem("s_chain", scope)
                held_pe = sem("s_held_pe", scope)
                CHAIN = 2
                BANKS = (0, 1, 2, 3)
                R = len(BANKS)
                M_NEW, M_SC, M_PT, M_PTN = NB, NB + 1, NB + 2, NB + 3
                caches = [A["cache_kv_w128"][0], A["cache_kv_w512"][0], A["cache_kv_w2048"][0]]

                def load_rows(sp, dst, b, which, hd, done):
                    c = [x[b, :, which, hd, :] for x in caches]
                    sp.dma_start(dst[:, 0:1, :], c[0].rearrange("(n p) o e -> p n (o e)", p=P)).then_inc(done, 16)
                    sp.dma_start(dst[:, 1:3, :], c[1].rearrange("(n p) o e -> p n (o e)", p=P)).then_inc(done, 16)
                    sp.dma_start(dst[:, 3, :], c[2].rearrange("(a r) o e -> a r (o e)", r=16)[:, 0:8, :])\
                        .then_inc(done, 16)

                with nc.Block() as block:
                    @block.sync
                    def _(sp):
                        sp.dma_start(mask[:, :], A["c_sample_mask"]).then_inc(const_in, 16)
                        with sp.Fori(0, AH) as h:
                            hd = bass.ds(h, 1)
                            sp.wait_ge(scores_done, h + 1)
                            for b in range(NB):
                                load_rows(sp, kc[b], b, 0, hd, k_in[b])
                            sp.wait_ge(o_done, h + 1)
                            for b in range(NB):
                                load_rows(sp, vc[b], b, 1, hd, v_in[b])
                            for g, o in enumerate(("kv128_s", "kv512_s", "kv2048_s")):
                                sp.dma_start(vn[:, g, :], OUT[o][0, :, :, 1, hd, :].rearrange("b t o e -> (b t) (o e)"))\
                                    .then_inc(vn_in, 16)

                    @block.tensor
                    def _(pe):
                        pe.sem_inc(scores_done, 1)
                        pe.sem_inc(o_done, 1)

                        def fill(at, m):
                            pe.wait_ge(misc_free, at + m + 1)
                            pe.sem_inc(held_pe, 1)
                            return psum[:, BANKS[m % R], :]

                        with pe.Fori(0, AH) as h:
                            m0 = h * MISC

                            def turn(b):
                                pe.wait_ge(k_in[b], h * 48 + 48)
                                bank = fill(m0, b)
                                for n in range(KB):
                                    mm = pe.transpose(bank[:, n * P:(n + 1) * P], kc[b][:, n, :], ident[:, :])
                                mm.then_inc(misc_done, 1)

                            def scores(b):
                                pe.wait_ge(misc_free, m0 + b + 1 + R)
                                pe.sem_inc(held_pe, 1)
                                for n in range(KB):
                                    mm = pe.matmul(psum[:, 4, n * NS + b * TB:n * NS + (b + 1) * TB],
                                                   kt[b % 2][:, n, :], qh[:, K_G[n], b * TB:(b + 1) * TB],
                                                   start=True, stop=True)
                                return mm

                            pe.wait_ge(head_ready, h + 1)
                            turn(0)
                            for b in range(1, NB):
                                turn(b)
                                scores(b - 1)
                            scores(NB - 1).then_inc(scores_done, 1)
                            bank = fill(m0, M_NEW)
                            for g in range(AG):
                                mm = pe.matmul(bank[0:NS, g * NS:(g + 1) * NS], qh[:, g, :], kh[:, g, :],
                                               start=True, stop=True)
                            mm.then_inc(misc_done, 1)
                            pe.wait_ge(scores_out, h + 1)
                            bank = fill(m0, M_SC)
                            for n in range(KB):
                                mm = pe.transpose(bank[0:NS, n * P:(n + 1) * P], sct[:, n, :], ident[:, :])
                            mm.then_inc(misc_done, 1)
                            pe.wait_ge(prob_ready, h + 1)
                            bank = fill(m0, M_PT)
                            for n in range(KB):
                                mm = pe.transpose(bank[:, n * NS:(n + 1) * NS], prob[:, n * P:(n + 1) * P],
                                                  ident[0:NS, 0:NS])
                            mm.then_inc(misc_done, 1)
                            bank = fill(m0, M_PTN)
                            for g in range(AG):
                                a = KB * P + g * NS
                                mm = pe.transpose(bank[0:NS, g * NS:(g + 1) * NS], prob[:, a:a + NS],
                                                  ident[0:NS, 0:NS])
                            mm.then_inc(misc_done, 1)
                            pe.wait_ge(vn_in, h * 48 + 48)
                            pe.wait_ge(misc_free, m0 + M_PTN + 1 + R)
                            pe.sem_inc(held_pe, 1)
                            for g in range(AG):
                                pe.matmul(psum[:, 5, 0:NS], vn[:, g, :], pt[0:NS, KB + g, :], start=(g == 0),
                                          stop=False, skip_group_check=True)
                            for b in range(NB):
                                pe.wait_ge(v_in[b], h * 48 + 48)
                                for n in range(KB):
                                    mm = pe.matmul(psum[:, 5, b * TB:(b + 1) * TB], vc[b][:, n, :],
                                                   pt[:, n, b * TB:(b + 1) * TB], start=False,
                                                   stop=(b == NB - 1 and n == KB - 1), skip_group_check=True)
                            mm.then_inc(o_done, 1)

                    @block.scalar
                    def _(act):
                        act.sem_inc(y_out, 16)
                        with act.Fori(0, AH) as h:
                            hd = bass.ds(h, 1)
                            act.wait_ge(y_out, h * 16 + 16)
                            act.activation(qh[:, :, :], q_s[:, :, hd, :].rearrange("p g o t -> p g (o t)"), ACT.Copy)
                            act.activation(kh[:, :, :], k_s[:, :, hd, :].rearrange("p g o t -> p g (o t)"), ACT.Copy)
                            act.activation(gh[:, :], gate_s[:, hd, :].rearrange("p o t -> p (o t)"), ACT.Copy)\
                                .then_inc(head_ready, 1)
                            act.wait_ge(negmax, h + 1)
                            act.activation(prob[:, :], prob[:, :], ACT.Exp, bias=nm[:, :], scale=SCALE,
                                           accum_out=sm[:, :]).then_inc(exp_done, 1)
                            act.wait_ge(y_ready, h + 1)
                            act.dma_start(y_d[bass.ds(h + Y_A, 1), :, SEQ:NT].rearrange("o p t -> p (o t)"), yt[:, :])\
                                .then_inc(y_out, 16)
                        act.wait_ge(y_out, 16 * AH + 16)

                    @block.vector
                    def _(dve):
                        ch = Chain(dve, chain)
                        dve.sem_inc(misc_free, R)
                        dve.wait_ge(const_in, 16)

                        def filled(at, m):
                            dve.wait_ge(misc_done, at + m + 1)
                            return psum[:, BANKS[m % R], :]

                        with dve.Fori(0, AH) as h:
                            ch.loop(h * CHAIN, CHAIN)
                            m0, hd = h * MISC, bass.ds(h, 1)
                            for b in range(NB):
                                bank = filled(m0, b)
                                dve.tensor_copy(kt[b % 2][:, :, :], bank[:, :].rearrange("p (a b) -> p a b", b=P))\
                                    .then_inc(misc_free, 1)
                            bank = filled(m0, M_NEW)
                            dve.tensor_tensor(prob[:, KB * P:KW], bank[0:NS, 0:AG * NS], mask[:, KB * P:KW], ALU.add)\
                                .then_inc(misc_free, 1)
                            dve.wait_ge(scores_done, h + 2)
                            dve.tensor_copy(sct[:, :, :], psum[:, 4, 0:KB * NS].rearrange("p (a b) -> p a b", b=NS))\
                                .then_inc(scores_out, 1)
                            bank = filled(m0, M_SC)
                            dve.tensor_tensor(prob[:, 0:KB * P], bank[0:NS, :], mask[:, 0:KB * P], ALU.add)\
                                .then_inc(misc_free, 1)
                            dve.wait_ge(misc_free, m0 + M_SC + 1 + R)
                            ch.link(dve.tensor_reduce(mx[:, :], prob[:, :], AX.X, ALU.max))
                            dve.tensor_scalar(nm[:, :], mx[:, :], -SCALE, None, ALU.mult).then_inc(negmax, 1)
                            dve.wait_ge(exp_done, h + 1)
                            ch.link(dve.reciprocal(sm[:, :], sm[:, :]))
                            dve.tensor_scalar(prob[:, :], prob[:, :], sm[:, :], None, ALU.mult).then_inc(prob_ready, 1)
                            bank = filled(m0, M_PT)
                            dve.tensor_copy(pt[:, 0:KB, :], bank[:, 0:KB * NS].rearrange("p (a b) -> p a b", b=NS))\
                                .then_inc(misc_free, 1)
                            bank = filled(m0, M_PTN)
                            dve.tensor_copy(pt[0:NS, KB:KB + AG, :], bank[0:NS, 0:AG * NS]
                                            .rearrange("p (a b) -> p a b", b=NS)).then_inc(misc_free, 1)
                            dve.wait_ge(o_done, h + 2)
                            dve.tensor_tensor(yt[:, :], psum[:, 5, 0:NS], gh[:, :], ALU.mult).then_inc(y_ready, 1)
                            ch.end(AH)

        def pool_phase():
            EXT = HIST + SEQ
            SEXT = HIST + TB
            scope = ExitStack()
            with scope:
                cv = Conveyor("c", scope, (3, 4, 5, 6))
                R = cv.ring
                hist = sb("c_hist", (NB * HIST, GROUP), F32, scope)
                ext = [sb(f"c_ext{i}", (P, EXT + NB * SEXT), F32, scope) for i in range(2)]
                acc = [sb(f"c_sum{i}", (P, EXT + NB * SEXT), F32, scope) for i in range(2)]
                pooled = sb("c_pooled", (P, NT), F32, scope)
                gate = sb("c_gate", (P, NT), F32, scope)
                graw = sb("c_gate_raw", (P, NT), F32, scope)
                yt = sb("c_y", (P, NT), F32, scope)
                count = sb("c_count", (P, CG, HIST), F32, scope)
                pw = sb("c_pool_w", (P, CG, P), F32, scope)
                last_p = sb("c_last_p", (HIST, GROUP), F32, scope)
                last_s = sb("c_last_s", (NB * HIST, GROUP), F32, scope)
                tail = sb("c_tail", (P, NB * HIST), F32, scope)
                const_in = sem("c_const_in", scope)
                cleared = sem("c_cleared", scope)
                copied_in = sem("c_copied_in", scope)
                tail_ready = sem("c_tail_ready", scope)
                pooled_ready = sem("c_pooled_ready", scope)
                y_ready = sem("c_y_ready", scope)
                y_out = sem("c_y_out", scope)
                rows_out = sem("c_rows_out", scope)
                chain = sem("c_chain", scope)
                MISC = 5
                cols = ((0, 512), (512, 512), (1024, NS))

                def samples(x):
                    return x[:, EXT:EXT + NB * SEXT].rearrange("p (b t) -> p b t", t=SEXT)

                with nc.Block() as block:
                    @block.sync
                    def _(sp):
                        sp.dma_start(hist[:, :], A["state_pool"][0].rearrange("b r c -> (b r) c")).then_inc(const_in, 16)
                        sp.dma_start(count[:, :, :], A["c_count"]).then_inc(const_in, 16)
                        sp.dma_start(pw[:, :, :], A["pool_w"][0].rearrange("g c d -> c g d")).then_inc(const_in, 16)
                        for g in range(CG):
                            cv.load(sp, 2 * g, 0, col(w_in, COL_CU + g * P))
                            cv.load(sp, 2 * g + 1, 1, col(w_in, COL_CG + g * P))
                        cv.copied(sp, (CG - 1) * MISC, 4)
                        sp.dma_start(OUT["pool_p"][0, 0], last_p[:, :]).then_inc(rows_out, 16)
                        sp.dma_start(OUT["pool_s"][0].rearrange("b r c -> (b r) c"), last_s[:, :])\
                            .then_inc(rows_out, 16)
                        sp.wait_ge(rows_out, 32)

                    @block.gpsimd
                    def _(pool):
                        cv.pool_start(pool)
                        for g in range(CG):
                            for j in range(2):
                                cv.split(pool, 2 * g + j, j, g, KO)

                    @block.tensor
                    def _(pe):
                        cv.pe_start(pe)
                        pe.wait_ge(const_in, 48)

                        def mix(g):
                            pe.wait_ge(pooled_ready, g + 1)
                            for q, (t0, n) in enumerate(cols):
                                bank = cv.fill(pe, g * MISC, 1 + q)
                                pe.matmul(bank[:, 0:n], pw[:, g, :], pooled[:, t0:t0 + n], start=True, stop=True)\
                                    .then_inc(cv.misc_done, 1)

                        def last_rows(g):
                            bank = cv.fill(pe, g * MISC, 4)
                            pe.wait_ge(tail_ready, g + 1)
                            pe.transpose(bank[0:HIST, 0:P], ext[g % 2][:, EXT - HIST:EXT], ident[:, :])
                            pe.transpose(bank[0:NB * HIST, P:2 * P], tail[:, :], ident[:, :]).then_inc(cv.misc_done, 1)

                        for g in range(CG):
                            bank = cv.fill(pe, g * MISC, 0)
                            pe.transpose(bank[:, 0:NB * HIST], hist[:, g * P:(g + 1) * P],
                                         ident[0:NB * HIST, 0:NB * HIST]).then_inc(cv.misc_done, 1)
                            for c in range(NCH):
                                cv.project(pe, 2 * g, 0, c, KO, x_hi, x_lo)
                            for c in range(NCH):
                                cv.project(pe, 2 * g + 1, 1, c, KO, x_hi, x_lo)
                            mix(g)
                            last_rows(g)

                    @block.scalar
                    def _(act):
                        cv.act_start(act)
                        for g in range(CG):
                            x = ext[g % 2]
                            act.wait_ge(cleared, 1)
                            if g >= 2:
                                cv.copied(act, (g - 2) * MISC, 4)
                            for c, (t0, n) in enumerate(CHUNKS):
                                act.wait_ge(cv.proj_done, NCH * 2 * g + c + 1 + SLOTS * NCH)
                                if c < NCH - 1:
                                    act.activation(x[:, HIST + t0:HIST + t0 + n], psum[:, c, 0:n], ACT.Copy)\
                                        .then_inc(cv.bank_free, 1)
                                else:
                                    act.activation(x[:, HIST + t0:EXT], psum[:, c, 0:SEQ - t0], ACT.Copy)
                                    act.activation(samples(x)[:, :, HIST:SEXT],
                                                   psum[:, c, SEQ - t0:n].rearrange("p (b t) -> p b t", t=TB),
                                                   ACT.Copy).then_inc(cv.bank_free, 1)
                            if g > 0:
                                act.wait_ge(y_ready, g)
                            for c in range(NCH):
                                cv.empty(act, 2 * g + 1, c, gate, ACT.Sigmoid, raw=graw)
                            act.wait_ge(y_ready, g + 1)
                            act.dma_start(y_d[Y_C + g], yt[:, :]).then_inc(y_out, 16)
                        act.wait_ge(y_out, 16 * CG)

                    @block.vector
                    def _(dve):
                        ch = Chain(dve, chain)
                        cv.dve_start(dve)
                        dve.wait_ge(const_in, 48)
                        ch.step(dve.memset(ext[0][:, 0:HIST], 0.0))
                        ch.link(dve.memset(ext[1][:, 0:HIST], 0.0))
                        dve.sem_inc(cleared, 1)
                        for g, win in enumerate(WINDOWS):
                            x = ext[g % 2]
                            bank = cv.filled(dve, g * MISC, 0)
                            dve.tensor_copy(samples(x)[:, :, 0:HIST], bank[:, 0:NB * HIST]
                                            .rearrange("p (b t) -> p b t", t=HIST)).then_inc(cv.misc_free, 1)
                            cv.copied(dve, g * MISC, 0)
                            cv.emptied(dve, 2 * g)
                            ch.step(dve.tensor_copy(tail[:, :].rearrange("p (b t) -> p b t", t=HIST),
                                                    samples(x)[:, :, TB:SEXT]))
                            src, w, n = x, 1, 0
                            end = EXT + NB * SEXT
                            while w < win:
                                dst = acc[n % 2]
                                ch.link(dve.tensor_tensor(dst[:, 2 * w - 1:end], src[:, 2 * w - 1:end],
                                                          src[:, w - 1:end - w], ALU.add))
                                src, w, n = dst, 2 * w, n + 1
                            if n == 1:
                                ch.wait()
                            dve.sem_inc(tail_ready, 1)
                            ch.step(dve.scalar_tensor_tensor(out=pooled[:, 0:SEQ], in0=src[:, HIST:EXT], scalar=1.0 / win,
                                                             in1=x[:, HIST:EXT], op0=ALU.mult, op1=ALU.subtract))
                            ch.link(dve.scalar_tensor_tensor(
                                out=pooled[:, SEQ:NT].rearrange("p (b t) -> p b t", t=TB),
                                in0=samples(src)[:, :, HIST:SEXT], scalar=1.0 / win,
                                in1=samples(x)[:, :, HIST:SEXT], op0=ALU.mult, op1=ALU.subtract))
                            ch.link(dve.tensor_tensor(pooled[:, 0:HIST], src[:, HIST:2 * HIST], count[:, g, :], ALU.mult))
                            dve.tensor_tensor(pooled[:, 0:HIST], pooled[:, 0:HIST], x[:, HIST:2 * HIST],
                                              ALU.subtract).then_inc(pooled_ready, 1)
                            cv.emptied(dve, 2 * g + 1)
                            ch.link(dve.tensor_tensor(gate[:, :], gate[:, :], graw[:, :], ALU.mult))
                            if g > 0:
                                dve.wait_ge(y_out, 16 * g)
                            for q, (t0, n) in enumerate(cols):
                                bank = cv.filled(dve, g * MISC, 1 + q)
                                dve.scalar_tensor_tensor(out=yt[:, t0:t0 + n], in0=bank[:, 0:n],
                                                         scalar=p_scale[:, g:g + 1], in1=gate[:, t0:t0 + n],
                                                         op0=ALU.mult, op1=ALU.mult).then_inc(cv.misc_free, 1)
                            cv.copied(dve, g * MISC, 3)
                            dve.sem_inc(y_ready, 1)
                            bank = cv.filled(dve, g * MISC, 4)
                            ch.step(dve.tensor_copy(last_p[:, g * P:(g + 1) * P], bank[0:HIST, 0:P]))
                            dve.tensor_copy(last_s[:, g * P:(g + 1) * P], bank[0:NB * HIST, P:2 * P])\
                                .then_inc(cv.misc_free, 1)

        def output_phase():
            scope = ExitStack()
            with scope:
                cv = Conveyor("o", scope, (3, 4, 5))
                R = cv.ring
                xt = sb("o_x", (P, TILES + 1, D), F32, scope)
                rows = sb("o_rows", (P, TILES + 1, D), F32, scope)
                mt = [sb(f"o_merged{i}", (P, NT), F32, scope) for i in range(2)]
                ot = [sb(f"o_feature{i}", (P, NT), F32, scope) for i in range(2)]
                g_post = sb("o_g_post", (P, D), F32, scope)
                junk = sb("o_junk", (P, D), F32, scope)
                ssq = sb("o_ssq", (P, TILES + 1), F32, scope)
                rs = sb("o_rs", (P, TILES + 1), F32, scope)
                m_in = [sem(f"o_merged_in{i}", scope) for i in range(2)]
                x_in = sem("o_x_in", scope)
                mh_ready = sem("o_merged_hi_ready", scope)
                ml_ready = sem("o_merged_lo_ready", scope)
                squared = sem("o_squared", scope)
                cleared = sem("o_cleared", scope)
                rms_ready = sem("o_rms_ready", scope)
                out_ready = sem("o_out_ready", scope)
                stored = sem("o_stored", scope)
                chain = sem("o_chain", scope)
                spans = ((0, 4), (4, 4), (8, 1))
                LOOPS = KO // 2
                MISC = 6

                with nc.Block() as block:
                    @block.sync
                    def _(sp):
                        for k in range(KO):
                            if k >= 2:
                                sp.wait_ge(ml_ready, k - 1)
                            sp.dma_start(mt[k % 2][:, :], merged_d[k]).then_inc(m_in[k % 2], 16)
                            if k < 2:
                                cv.load(sp, k, k, col(w_out, k * P))
                        sp.dma_start(xt[:, 0:TILES, :], A["x_prompt"][0].rearrange("(b p) d -> p b d", p=P)).then_inc(x_in, 16)
                        sp.dma_start(xt[0:NS, TILES, :], A["x_sample"].rearrange("b t d -> (b t) d")).then_inc(x_in, 16)
                        sp.dma_start(g_post[:, :], A["norm_post"].broadcast_to([P, D])).then_inc(x_in, 16)
                        with sp.Fori(1, LOOPS) as i:
                            for j in range(2):
                                cv.load(sp, i * 2 + j, j, col(w_out, i * (2 * P) + j * P))
                        for t in range(TILES + 1):
                            sp.wait_ge(out_ready, t + 1)
                            if t < TILES:
                                sp.dma_start(OUT["y_prompt"][0, t * P:(t + 1) * P, :], rows[:, t, :]).then_inc(stored, 16)
                            else:
                                sp.dma_start(OUT["y_sample"].rearrange("b t d -> (b t) d"), rows[0:NS, t, :])\
                                    .then_inc(stored, 16)
                        sp.wait_ge(stored, 16 * (TILES + 1))

                    @block.gpsimd
                    def _(pool):
                        cv.pool_start(pool)
                        with pool.Fori(0, LOOPS) as i:
                            for j in range(2):
                                cv.split(pool, i * 2 + j, j, i, KO)

                    @block.tensor
                    def _(pe):
                        cv.pe_start(pe)
                        def back(m0, j):
                            for q, (b0, nb) in enumerate(spans):
                                bank = cv.fill(pe, m0, 3 * j + q, q == 2)
                                w = P if q < 2 else NS
                                for b in range(nb):
                                    mm = pe.transpose(bank[0:w, b * P:(b + 1) * P],
                                                      ot[j][:, (b0 + b) * P:(b0 + b) * P + w], ident[:, :])
                                mm.then_inc(cv.misc_done, 1)

                        with pe.Fori(0, LOOPS) as i:
                            for j in range(2):
                                u = i * 2 + j
                                for c in range(NCH):
                                    cv.project(pe, u, j, c, KO, x_hi, x_lo, each=ml_ready if j + c == 0 else None)
                                cv.emptied(pe, u)
                                back(i * MISC, j)

                    @block.scalar
                    def _(act):
                        cv.act_start(act)
                        for k in range(KO):
                            act.wait_ge(m_in[k % 2], 16 * (k // 2 + 1))
                            act.activation(x_hi[:, k, :], mt[k % 2][:, :], ACT.Copy).then_inc(mh_ready, 1)
                        with act.Fori(0, LOOPS) as i:
                            for j in range(2):
                                for c in range(NCH):
                                    cv.empty(act, i * 2 + j, c, ot[j], ACT.Copy)
                        act.wait_ge(cleared, 1)
                        cv.copied(act, 0, LOOPS * MISC - 1)
                        for t in range(TILES + 1):
                            n = P if t < TILES else NS
                            if t > 0:
                                act.wait_ge(squared, t)
                            act.activation(junk[0:n, :], rows[0:n, t, :], ACT.Square,
                                           accum_out=ssq[0:n, t:t + 1]).then_inc(squared, 1)
                        act.wait_ge(squared, TILES + 1)
                        act.activation(rs[:, :], ssq[:, :], ACT.Sqrt, bias=eps[:, :], scale=1.0 / D)\
                            .then_inc(rms_ready, 1)

                    @block.vector
                    def _(dve):
                        ch = Chain(dve, chain)
                        cv.dve_start(dve)
                        dve.memset(ssq[:, :], 1.0).then_inc(cleared, 1)
                        for k in range(KO):
                            dve.wait_ge(mh_ready, k + 1)
                            dve.tensor_tensor(x_lo[:, k, :], mt[k % 2][:, :], x_hi[:, k, :].bitcast(F32),
                                              ALU.subtract).then_inc(ml_ready, 1)
                        with dve.Fori(0, LOOPS) as i:
                            for j in range(2):
                                for q, (b0, nb) in enumerate(spans):
                                    bank = cv.filled(dve, i * MISC, 3 * j + q)
                                    w = P if q < 2 else NS
                                    dve.tensor_copy(rows[0:w, b0:b0 + nb, bass.ds(i * (2 * P) + j * P, P)],
                                                    bank[0:w, 0:nb * P].rearrange("p (a b) -> p a b", b=P))\
                                        .then_inc(cv.misc_free, 1)
                        dve.wait_ge(rms_ready, 1)
                        ch.link(dve.reciprocal(rs[:, :], rs[:, :]))
                        dve.wait_ge(x_in, 48)
                        for t in range(TILES + 1):
                            n = P if t < TILES else NS
                            ch.link(dve.scalar_tensor_tensor(out=rows[0:n, t, :], in0=rows[0:n, t, :],
                                                             scalar=rs[0:n, t:t + 1], in1=g_post[0:n, :],
                                                             op0=ALU.mult, op1=ALU.mult))
                            dve.tensor_tensor(rows[0:n, t, :], rows[0:n, t, :], xt[0:n, t, :],
                                              ALU.add).then_inc(out_ready, 1)

        norm_phase()
        hgrn_phase()
        with ExitStack() as heads:
            q_s = sb("q_sample", (P, AG, AH, NS), F32, heads)
            k_s = sb("k_sample", (P, AG, AH, NS), F32, heads)
            gate_s = sb("gate_sample", (P, AH, NS), F32, heads)
            attention_phase(q_s, k_s, gate_s)
            sample_attention(q_s, k_s, gate_s)
        pool_phase()
        fresh_semaphores()
        merge_phase("mb", 0, ((0, BH, w_br["b"], COL_MG + D),), True)
        merge_phase("mac", Y_A, ((0, AH, w_br["a"], COL_MG), (AH, CG, w_br["c"], COL_MG + 2 * D)), False)
        output_phase()
        lot[0].close()


_INS = ["x_prompt", "x_sample", "cache_kv_w128", "cache_kv_w512", "cache_kv_w2048", "state_hgrn",
        "state_pool", "norm_pre", "norm_post", "w_in", "hgrn_lb_logits", "hgrn_norm", "pool_w",
        "pool_scale", "w_br_a", "w_br_b", "w_br_c", "w_out"]
_OUTS = [("y_prompt", (1, 1024, 1024)), ("y_sample", (8, 8, 1024)),
         ("kv128_p", (1, 1, 128, 2, 4, 128)), ("kv512_p", (1, 1, 512, 2, 4, 128)),
         ("kv2048_p", (1, 1, 1024, 2, 4, 128)), ("kv128_s", (1, 8, 8, 2, 4, 128)),
         ("kv512_s", (1, 8, 8, 2, 4, 128)), ("kv2048_s", (1, 8, 8, 2, 4, 128)),
         ("hgrn_p", (1, 1, 8, 128, 128)), ("hgrn_s", (1, 8, 8, 128, 128)),
         ("pool_p", (1, 1, 15, 512)), ("pool_s", (1, 8, 15, 512))]


def kernel(**inputs):
    import numpy as np
    import concourse.bacc as bacc
    from concourse.bass_utils import run_bass_kernel_spmd

    nc = bacc.Bacc("TRN2", target_bir_lowering=False, num_devices=1)
    arrays, ins, outs = {}, {}, {}
    for name in _INS:
        a = np.ascontiguousarray(inputs[name])
        arrays["in_" + name] = a
        ins[name] = nc.dram_tensor("in_" + name, a.shape, mybir.dt.from_np(a.dtype), kind="ExternalInput").ap()
    for name, a in constants(np).items():
        arrays["const_" + name] = a
        ins["c_" + name] = nc.dram_tensor("const_" + name, a.shape, mybir.dt.from_np(a.dtype),
                                          kind="ExternalInput").ap()
    for name, shape in _OUTS:
        outs[name] = nc.dram_tensor("out_" + name, shape, F32, kind="ExternalOutput").ap()
    build(nc, ins, outs)
    r = run_bass_kernel_spmd(nc, [arrays], core_ids=[0])
    return tuple(r.results[0]["out_" + name] for name, _ in _OUTS)
```

```python
import concourse.bass as bass
from concourse import mybir
from contextlib import ExitStack

F32 = mybir.dt.float32
F32R = mybir.dt.float32r
I32 = mybir.dt.int32
ALU = mybir.AluOpType
ACT = mybir.ActivationFunctionType
AX = mybir.AxisListType

D = 1024
P = 128
KO = D // P
SEQ = 1024
NB, TB = 8, 8
NS = NB * TB
NT = SEQ + NS
TILES = SEQ // P
EPS = 1e-6
NEG = -1e30
SCALE = P ** -0.5
AH, BH, CG, AG = 4, 8, 4, 3
GROUP = AH * P
HIST = 15
WINDOWS = (2, 4, 8, 16)
COL_AQ, COL_AK, COL_AV, COL_AG = 0, 3 * GROUP, 6 * GROUP, 9 * GROUP
COL_BQ = COL_AG + GROUP
COL_BF, COL_BI, COL_BG = COL_BQ + D, COL_BQ + 2 * D, COL_BQ + 3 * D
COL_CU = COL_BG + D
COL_CG = COL_CU + GROUP
COL_MG = COL_CG + GROUP

CHUNKS = ((0, 384), (384, 384), (768, NT - 768))
NCH = len(CHUNKS)
SLOTS = 2
Y_A, Y_C = BH, BH + AH
LEVELS = 8


def constants(np):
    i = np.arange(P)
    c = {}
    c["ident"] = np.eye(P, dtype=np.float32)
    band = np.zeros((P, 2 * P), np.float32)
    band[:, :P] = np.where(i[None, :] >= i[:, None], 0.0, NEG)
    band[:, P:] = np.where(i[None, :] <= i[:, None], 0.0, NEG)
    c["band"] = band
    gap = i[:, None] - i[None, :]
    c["pair"] = np.where((gap >= 0) & (gap % 2 == 0), 0.0, NEG).astype(np.float32)
    lev = np.zeros((P, LEVELS, P), np.int32)
    s, t = i[:, None], i[None, :]
    for n in range(1, LEVELS):
        h = n - 1
        lev[:, n, :] = ((s >> n) == (t >> n)) & (((s >> h) & 1) == 0) & (((t >> h) & 1) == 1)
    c["level"] = lev
    j = np.arange(NS)
    c["own_row"] = ((j[:, None] // TB) == np.arange(NB)[None, :]).astype(np.float32)
    c["own_col"] = np.broadcast_to((np.arange(NB)[:, None] == (j[None, :] // TB)).astype(np.float32),
                                   (P, NB, NS)).copy()
    tq = (j % TB)[:, None]
    m = np.full((NS, 4 * P + 3 * NS), NEG, np.float32)
    m[:, 0:P] = np.where(i[None, :] >= tq, 0.0, NEG)
    for blk in range(2):
        key = P * blk + i[None, :]
        m[:, (1 + blk) * P:(2 + blk) * P] = np.where((256 + tq - key) % 4 == 0, 0.0, NEG)
    key = 16 * (i[None, :] // 8) + i[None, :] % 8
    m[:, 3 * P:4 * P] = np.where((256 + tq - key) % 16 == 0, 0.0, NEG)
    for g, dil in enumerate((1, 4, 16)):
        gap = tq - (j % TB)[None, :]
        ok = ((j[:, None] // TB) == (j[None, :] // TB)) & (gap >= 0) & (gap % dil == 0)
        m[:, 4 * P + g * NS:4 * P + (g + 1) * NS] = np.where(ok, 0.0, NEG)
    c["sample_mask"] = m
    rc = np.zeros((P, CG, HIST), np.float32)
    for g, w in enumerate(WINDOWS):
        rc[:, g, :] = 1.0 / np.minimum(np.arange(HIST) + 1, w)
    c["count"] = rc
    return c


def build(nc, A, OUT):
    ctx = ExitStack()
    with ctx:
        def sb(name, shape, dt=F32, scope=ctx):
            return scope.enter_context(nc.sbuf_tensor(name, list(shape), dt))

        def sem(name, scope):
            h = lot[0].enter_context(nc.semaphore(name))
            taken.append(h.num)
            return h

        lot, taken = [ExitStack()], []

        def fresh_semaphores():
            nums = sorted(taken)
            runs = [[nums[0], nums[0] + 1]]
            for n in nums[1:]:
                if n == runs[-1][1]:
                    runs[-1][1] = n + 1
                else:
                    runs.append([n, n + 1])
            with nc.Block() as block:
                @block.gpsimd
                def _(pool):
                    for a, b in runs:
                        pool.sem_clear(range(a, b))
            lot[0].close()
            lot[0] = ExitStack()
            taken.clear()

        merged_d = nc.dram_tensor("merged_rows", (KO, P, NT), F32, kind="Internal").ap()
        y_d = nc.dram_tensor("branch_outputs", (2 * KO, P, NT), F32, kind="Internal").ap()
        stat_d = nc.dram_tensor("stat_rows", (AH, SEQ, 2, 2), F32, kind="Internal").ap()
        weight_d = nc.dram_tensor("group_weights", (AH, SEQ, 2), F32, kind="Internal").ap()

        psum = ctx.enter_context(nc.psum_tensor("psum", [P, 8, 512], F32))

        ident = sb("ident", (P, P))
        band = sb("band", (P, 2 * P))
        pair = sb("pair", (P, P))
        lb = sb("lb", (P, BH))
        one_lb = sb("one_lb", (P, BH))
        h_norm = sb("h_norm", (P, 1))
        p_scale = sb("p_scale", (P, CG))
        eps = sb("eps", (P, 1))
        w_raw = sb("w_raw", (P, SLOTS, KO, P))
        w_hi = sb("w_hi", (P, SLOTS, KO, P), F32R)
        w_lo = sb("w_lo", (P, SLOTS, KO, P), F32R)
        x_hi = sb("x_hi", (P, KO, NT), F32R)
        x_lo = sb("x_lo", (P, KO, NT), F32R)

        w_in = A["w_in"][0].rearrange("(ko p) n -> p ko n", p=P)
        w_out = A["w_out"][0].rearrange("(ko p) n -> p ko n", p=P)
        w_br = {k: A["w_br_" + k][0].rearrange("(ko p) n -> p ko n", p=P) for k in "abc"}

        def col(w, at):
            return w[:, :, bass.ds(at, P)]

        def nc_sem(name):
            return ctx.enter_context(nc.semaphore(name))

        class Conveyor:

            loaded = [nc_sem(f"w_loaded{s}") for s in range(SLOTS)]
            hi_ready, split_done = nc_sem("w_hi_ready"), nc_sem("w_split_done")
            proj_done, bank_free = nc_sem("proj_done"), nc_sem("bank_free")
            before = 0

            def __init__(self, tag, scope, misc_banks, units):
                assert units % SLOTS == 0
                self.u0 = Conveyor.before
                Conveyor.before += units
                self.misc_done = sem(f"{tag}_misc_done", scope)
                self.misc_free = sem(f"{tag}_misc_free", scope)
                self.held_pe = sem(f"{tag}_held_pe", scope)
                self.held_pool = sem(f"{tag}_held_pool", scope)
                self.held_sp = sem(f"{tag}_held_sp", scope)
                self.held_dve = sem(f"{tag}_held_dve", scope)
                self.banks = misc_banks
                self.ring = len(misc_banks)

            def load(self, sp, u, s, src):
                sp.wait_ge(self.split_done, u + (self.u0 + 1))
                sp.sem_inc(self.held_sp, 1)
                sp.dma_start(w_raw[:, s, 0:src.shape[1], :], src).then_inc(self.loaded[s], 16)

            def split(self, pool, u, s, turn, nko):
                pool.wait_ge(self.loaded[s], turn * 16 + (16 + 16 // SLOTS * self.u0))
                pool.wait_ge(self.proj_done, u * NCH + (NCH + NCH * self.u0))
                pool.sem_inc(self.held_pool, 1)
                pool.tensor_copy(w_hi[:, s, 0:nko, :], w_raw[:, s, 0:nko, :]).then_inc(self.hi_ready, 1)
                pool.wait_ge(self.hi_ready, u + (1 + self.u0))
                pool.tensor_tensor(w_lo[:, s, 0:nko, :], w_raw[:, s, 0:nko, :],
                                   w_hi[:, s, 0:nko, :].bitcast(F32), ALU.subtract)\
                    .then_inc(self.split_done, 1)

            def project(self, pe, u, s, c, nko, hi, lo, each=None, k0=0):
                t0, n = CHUNKS[c]
                if c == 0:
                    pe.wait_ge(self.split_done, u + (1 + SLOTS + self.u0))
                pe.wait_ge(self.bank_free, u * NCH + (c + 1 + NCH * self.u0))
                for k in range(nko):
                    if each is not None:
                        pe.wait_ge(each, k0 + k + 1)
                    for w, x in ((w_hi, hi), (w_hi, lo), (w_lo, hi)):
                        mm = pe.matmul(psum[:, c, 0:n], w[:, s, k, :], x[:, k, t0:t0 + n],
                                       start=(k == 0 and w is w_hi and x is hi),
                                       stop=(k == nko - 1 and w is w_lo))
                mm.then_inc(self.proj_done, 1)

            def projected(self, act, u, c):
                act.wait_ge(self.proj_done, u * NCH + (c + 1 + SLOTS * NCH + NCH * self.u0))

            def empty(self, act, u, c, dst, func, raw=None):
                t0, n = CHUNKS[c]
                self.projected(act, u, c)
                if raw is not None:
                    act.activation(raw[:, t0:t0 + n], psum[:, c, 0:n], ACT.Copy)
                act.activation(dst[:, t0:t0 + n], psum[:, c, 0:n], func).then_inc(self.bank_free, 1)

            def emptied(self, eng, u, c=NCH - 1):
                eng.wait_ge(self.bank_free, u * NCH + (c + 1 + NCH + NCH * self.u0))

            def dve_start(self, dve):
                dve.sem_inc(self.misc_free, self.ring)

            def bank(self, at, m):
                return psum[:, self.banks[(m + (at if isinstance(at, int) else 0)) % self.ring], :]

            def fill(self, pe, at, m, part=False):
                pe.wait_ge(self.misc_free, at + m + 1)
                if part:
                    pe.sem_inc(self.held_pe, 1)
                return self.bank(at, m)

            def filled(self, dve, at, m, part=False):
                dve.wait_ge(self.misc_done, at + m + 1)
                if part:
                    dve.sem_inc(self.held_dve, 1)
                return self.bank(at, m)

            def copied(self, eng, at, m):
                eng.wait_ge(self.misc_free, at + m + 1 + self.ring)

        class Chain:

            def __init__(self, eng, s):
                self.eng, self.sem, self.n, self.at = eng, s, 0, 0

            def loop(self, at, n):
                self.at, self.start, self.per = at, self.n, n

            def end(self, turns):
                assert self.n - self.start == self.per, ("steps in the body", self.n - self.start)
                self.n, self.at = self.start + turns * self.per, 0

            def step(self, ins):
                ins.then_inc(self.sem, 1)
                self.n += 1
                return ins

            def wait(self):
                self.eng.wait_ge(self.sem, self.at + self.n)

            def link(self, ins):
                self.step(ins)
                self.wait()

        def norm_phase(then):
            scope = ExitStack()
            with scope:
                xt = sb("xt", (P, TILES + 1, D), F32, scope)
                g_pre = sb("g_pre", (P, D), F32, scope)
                junk = sb("junk", (P, D), F32, scope)
                ssq = sb("ssq", (P, TILES + 1), F32, scope)
                rs = sb("rs", (P, TILES + 1), F32, scope)
                lg = sb("lg", (P, BH), F32, scope)
                ex = sb("ex", (P, BH), F32, scope)
                x_in = [sem(f"x_in{i}", scope) for i in range(TILES + 1)]
                g_in = sem("g_in", scope)
                ident_in = sem("ident_in", scope)
                const_in = sem("const_in", scope)
                lb_in = sem("lb_in", scope)
                eps_ready = sem("eps_ready", scope)
                squared = sem("squared", scope)
                rms_ready = sem("rms_ready", scope)
                xn_ready = sem("xn_ready", scope)
                xt_done = sem("transposed", scope)
                xh_ready = sem("xh_ready", scope)
                banks_free = sem("banks_free", scope)
                lg_ready = sem("lg_ready", scope)
                exp_ready = sem("exp_ready", scope)
                chain = sem("norm_chain", scope)
                RING = 5
                N_CONST = 4
                LAG = 2
                HALF = KO // 2
                cv = Conveyor("n", scope, (3,), 0)

                def rows(t):
                    return P if t < TILES else NS

                with nc.Block() as block:
                    @block.sync
                    def _(sp):
                        for t in range(TILES):
                            sp.dma_start(xt[:, t, :], A["x_prompt"][0, t * P:(t + 1) * P, :]).then_inc(x_in[t], 16)
                            if t == 0:
                                sp.dma_start(g_pre[:, :], A["norm_pre"].broadcast_to([P, D])).then_inc(g_in, 16)
                                sp.dma_start(ident[:, :], A["c_ident"]).then_inc(ident_in, 16)
                        sp.dma_start(xt[0:NS, TILES, :], A["x_sample"].rearrange("b t d -> (b t) d"))\
                            .then_inc(x_in[TILES], 16)
                        for j in range(SLOTS):
                            cv.load(sp, j, j, then[j])
                        for dst, src in ((band[:, :], A["c_band"]), (pair[:, :], A["c_pair"]),
                                         (h_norm[:, :], A["hgrn_norm"].rearrange("a p -> p a")),
                                         (p_scale[:, :], A["pool_scale"][0].rearrange("(g p) -> p g", p=P))):
                            sp.dma_start(dst, src, allow_slow_non_contiguous=True).then_inc(const_in, 16)
                        sp.dma_start(lg[:, :], A["hgrn_lb_logits"][0].rearrange("(h p) -> p h", p=P),
                                     allow_slow_non_contiguous=True).then_inc(lb_in, 16)
                        sp.wait_ge(const_in, 16 * N_CONST)

                    @block.gpsimd
                    def _(pool):
                        pool.sem_inc(Conveyor.split_done, SLOTS)
                        for j in range(SLOTS):
                            cv.split(pool, j, j, 0, KO)

                    @block.scalar
                    def _(act):
                        act.sem_inc(Conveyor.bank_free, NCH)
                        act.wait_ge(eps_ready, 1)
                        for i in range(TILES + 1 + LAG):
                            if i <= TILES:
                                n = rows(i)
                                act.wait_ge(x_in[i], 16)
                                if i > 0:
                                    act.wait_ge(squared, i)
                                act.activation(junk[0:n, :], xt[0:n, i, :], ACT.Square,
                                               accum_out=ssq[0:n, i:i + 1]).then_inc(squared, 1)
                                act.wait_ge(squared, i + 1)
                                act.activation(rs[0:n, i:i + 1], ssq[0:n, i:i + 1], ACT.Sqrt, bias=eps[0:n, :],
                                               scale=1.0 / D).then_inc(rms_ready, 1)
                            t = i - LAG
                            for m in (2 * t, 2 * t + 1) if t >= 0 else ():
                                k0, n = m % 2 * HALF, rows(t)
                                act.wait_ge(xt_done, m + 1)
                                act.activation(x_hi[:, k0:k0 + HALF, t * P:t * P + n],
                                               psum[:, 3 + m % RING, 0:HALF * n].rearrange("p (k t) -> p k t", t=n),
                                               ACT.Copy).then_inc(xh_ready, 1)
                        act.wait_ge(lg_ready, 1)
                        act.activation(ex[:, :], lg[:, :], ACT.Exp).then_inc(exp_ready, 1)

                    @block.vector
                    def _(dve):
                        ch = Chain(dve, chain)
                        dve.memset(eps[:, :], EPS).then_inc(eps_ready, 1)
                        dve.wait_ge(g_in, 16)
                        for i in range(TILES + 1 + LAG):
                            if i <= TILES:
                                n = rows(i)
                                dve.wait_ge(rms_ready, i + 1)
                                ch.link(dve.reciprocal(rs[0:n, i:i + 1], rs[0:n, i:i + 1]))
                                dve.scalar_tensor_tensor(out=xt[0:n, i, :], in0=xt[0:n, i, :],
                                                         scalar=rs[0:n, i:i + 1], in1=g_pre[0:n, :],
                                                         op0=ALU.mult, op1=ALU.mult).then_inc(xn_ready, 1)
                            t = i - LAG
                            for m in (2 * t, 2 * t + 1) if t >= 0 else ():
                                k0, n = m % 2 * HALF, rows(t)
                                xs = slice(t * P, t * P + n)
                                dve.wait_ge(xh_ready, m + 1)
                                dve.tensor_tensor(x_lo[:, k0:k0 + HALF, xs],
                                                  psum[:, 3 + m % RING, 0:HALF * n].rearrange("p (k t) -> p k t", t=n),
                                                  x_hi[:, k0:k0 + HALF, xs].bitcast(F32), ALU.subtract)\
                                    .then_inc(banks_free, 1)
                        dve.wait_ge(lb_in, 16)
                        dve.tensor_tensor(lg[:, :], lg[:, :], lg[:, :], ALU.subtract).then_inc(lg_ready, 1)
                        dve.wait_ge(exp_ready, 1)
                        ch.link(dve.reciprocal(lg[:, :], ex[:, :]))
                        ch.link(dve.tensor_tensor(ex[:, :], ex[:, :], lg[:, :], ALU.mult))
                        ch.link(dve.tensor_tensor(lb[:, :], ex[:, :], ex[:, :], ALU.subtract))
                        ch.link(dve.tensor_scalar(one_lb[:, :], lb[:, :], -1.0, 1.0, ALU.mult, ALU.add))

                    @block.tensor
                    def _(pe):
                        pe.sem_inc(Conveyor.proj_done, SLOTS * NCH)
                        pe.wait_ge(ident_in, 16)
                        for t in range(TILES + 1):
                            n = rows(t)
                            pe.wait_ge(xn_ready, t + 1)
                            for m in (2 * t, 2 * t + 1):
                                if m >= RING:
                                    pe.wait_ge(banks_free, m - RING + 1)
                                for b in range(HALF):
                                    k = m % 2 * HALF + b
                                    mm = pe.transpose(psum[:, 3 + m % RING, b * n:b * n + n],
                                                      xt[0:n, t, k * P:(k + 1) * P], ident[0:n, 0:n])
                                mm.then_inc(xt_done, 1)

        def merge_phase(tag, y0, pairs, fresh, then):
            N_PAIR = 2
            OUTER = 2 if fresh else 1
            LOOPS = KO // OUTER
            UNITS = 2 * N_PAIR
            scope = ExitStack()
            with scope:
                cv = Conveyor(tag, scope, (3,), LOOPS * UNITS)
                y_hi = sb(f"{tag}_y_hi", (P, KO, NT), F32R, scope)
                y_lo = sb(f"{tag}_y_lo", (P, KO, NT), F32R, scope)
                pb = [sb(f"{tag}_product{i}", (P, NT), F32, scope) for i in range(2)]
                gt = [sb(f"{tag}_gate{i}", (P, NT), F32, scope) for i in range(2)]
                mt = sb(f"{tag}_rows", (P, NT), F32, scope)
                stage = [pb[0], pb[1], gt[1], mt]
                NST = len(stage)
                y_in = [sem(f"{tag}_y_in{i}", scope) for i in range(NST)]
                yh_ready = sem(f"{tag}_yh_ready", scope)
                yl_ready = sem(f"{tag}_yl_ready", scope)
                rows_in = sem(f"{tag}_rows_in", scope)
                gated = sem(f"{tag}_gated", scope)
                rows_out = [sem(f"{tag}_rows_out{i}", scope) for i in range(2)]
                chain = sem(f"{tag}_chain", scope)

                def pair(p):
                    return pairs[p % len(pairs)]

                with nc.Block() as block:
                    @block.sync
                    def _(sp):
                        def load_pair(i, p):
                            _, n, w, gate = pair(p)
                            at = i * (OUTER * P) + (p * P if fresh else 0)
                            u = i * UNITS + 2 * p
                            cv.load(sp, u, 0, col(w_in, at + gate))
                            cv.load(sp, u + 1, 1, col(w, at))

                        def load_rows(i):
                            if fresh:
                                return
                            sp.wait_ge(gated, i * N_PAIR + 1)
                            sp.dma_start(mt[:, :], merged_d[bass.ds(i, 1), :, :]
                                         .rearrange("o p t -> p (o t)")).then_inc(rows_in, 16)

                        for k in range(KO):
                            if k >= NST:
                                sp.wait_ge(yl_ready, k - NST + 1)
                            sp.dma_start(stage[k % NST][:, :], y_d[y0 + k]).then_inc(y_in[k % NST], 16)
                        load_pair(0, 1)
                        sp.wait_ge(yl_ready, KO)
                        load_rows(0)
                        with sp.Fori(1, LOOPS) as i:
                            load_pair(i, 0)
                            load_rows(i)
                            load_pair(i, 1)
                        for j in range(SLOTS):
                            cv.load(sp, LOOPS * UNITS + j, j, then[j])

                    @block.gpsimd
                    def _(pool):
                        def split_pair(i, p, nko):
                            u = i * UNITS + 2 * p
                            cv.split(pool, u, 0, i * N_PAIR + p, KO)
                            cv.split(pool, u + 1, 1, i * N_PAIR + p, nko)

                        split_pair(0, 1, pair(1)[1])
                        with pool.Fori(1, LOOPS) as i:
                            split_pair(i, 0, pair(0)[1])
                            split_pair(i, 1, pair(1)[1])
                        split_pair(LOOPS, 0, then[1].shape[1])

                    @block.tensor
                    def _(pe):
                        with pe.Fori(0, LOOPS) as i:
                            for p in range(N_PAIR):
                                k0, n, _, _ = pair(p)
                                u = i * UNITS + 2 * p
                                for c in range(NCH):
                                    cv.project(pe, u, 0, c, KO, x_hi, x_lo)
                                for c in range(NCH):
                                    cv.project(pe, u + 1, 1, c, n, y_hi[:, k0:k0 + n, :], y_lo[:, k0:k0 + n, :],
                                               each=yl_ready if c == 0 else None, k0=k0)

                    @block.scalar
                    def _(act):
                        for j in range(2):
                            act.sem_inc(rows_out[j], 16)
                        act.sem_inc(gated, 2)
                        for k in range(KO):
                            act.wait_ge(y_in[k % NST], 16 * (k // NST + 1))
                            act.activation(y_hi[:, k, :], stage[k % NST][:, :], ACT.Copy).then_inc(yh_ready, 1)
                        with act.Fori(0, LOOPS) as i:
                            for p in range(N_PAIR):
                                u = i * UNITS + 2 * p
                                act.wait_ge(gated, i * N_PAIR + p + 1)
                                if p == 1:
                                    act.wait_ge(yl_ready, KO)
                                for c in range(NCH):
                                    cv.empty(act, u, c, gt[p], ACT.Sigmoid)
                                if p == 0:
                                    act.wait_ge(yl_ready, KO)
                                if fresh or p == 1:
                                    act.wait_ge(rows_out[p], i * 16 + 16)
                                else:
                                    act.wait_ge(gated, i * N_PAIR + 2)
                                for c in range(NCH):
                                    cv.empty(act, u + 1, c, pb[p], ACT.Copy)
                                if fresh or p == 1:
                                    tile = i * 2 + p if fresh else i
                                    act.wait_ge(gated, i * N_PAIR + p + 3)
                                    act.dma_start(merged_d[bass.ds(tile, 1), :, :]
                                                  .rearrange("o p t -> p (o t)"), pb[p][:, :])\
                                        .then_inc(rows_out[p], 16)
                        for j in range(2) if fresh else (1,):
                            act.wait_ge(rows_out[j], 16 * LOOPS + 16)

                    @block.vector
                    def _(dve):
                        ch = Chain(dve, chain)
                        for k in range(KO):
                            dve.wait_ge(yh_ready, k + 1)
                            dve.tensor_tensor(y_lo[:, k, :], stage[k % NST][:, :], y_hi[:, k, :].bitcast(F32),
                                              ALU.subtract).then_inc(yl_ready, 1)
                        with dve.Fori(0, LOOPS) as i:
                            per = 0 if fresh else N_PAIR
                            ch.loop(i * per, per)
                            for p in range(N_PAIR):
                                u = i * UNITS + 2 * p
                                cv.emptied(dve, u + 1)
                                ins = dve.tensor_tensor(pb[p][:, :], pb[p][:, :], gt[p][:, :], ALU.mult)
                                if fresh:
                                    ins.then_inc(gated, 1)
                                    continue
                                ch.link(ins)
                                if p == 0:
                                    dve.wait_ge(rows_in, i * 16 + 16)
                                else:
                                    dve.wait_ge(gated, i * N_PAIR + 3)
                                dve.tensor_tensor(pb[p][:, :], pb[p][:, :], mt[:, :] if p == 0 else pb[0][:, :],
                                                  ALU.add).then_inc(gated, 1)
                            ch.end(LOOPS)

        def hgrn_phase(then):
            tag = "b"
            UNITS = 4
            scope = ExitStack()
            with scope:
                cv = Conveyor(tag, scope, (3, 4, 5, 6, 7), BH * UNITS)
                q_new = sb("b_q_new", (P, NT), F32, scope)
                f_new = sb("b_forget_new", (P, NT), F32, scope)
                v_new = sb("b_v_new", (P, NT), F32, scope)
                g_new = sb("b_gate_new", (P, NT), F32, scope)
                g_raw = sb("b_gate_raw", (P, NT), F32, scope)
                qp = sb("b_q_decayed", (P, NT), F32, scope)
                kr = sb("b_k_decayed", (P, NT), F32, scope)
                ff = sb("b_forget", (P, NT), F32, scope)
                gate = sb("b_gate", (P, NT), F32, scope)
                ft_n = [NT >> n if n <= 3 else SEQ >> n for n in range(LEVELS)]
                ft_at = [0] + [sum(ft_n[1:n]) for n in range(1, LEVELS + 1)]
                fts = sb("b_block_decay", (P, ft_at[LEVELS]), F32, scope)
                att = sb("b_att", (P, TILES + 1, P), F32, scope)
                vrow = sb("b_v_rows", (P, TILES + 1, P), F32, scope)
                krow = sb("b_k_rows", (P, TILES + 1, P), F32, scope)
                vown = sb("b_v_own", (NS, NB, P), F32, scope)
                qown = sb("b_q_own", (P, NB, NS), F32, scope)
                state = sb("b_state", (P, TILES + 1, P), F32, scope)
                s0 = sb("b_sample_state", (P, NB, P), F32, scope)
                osb = sb("b_o_rows", (P, TILES + 1, P), F32, scope)
                osq = krow
                ssq = sb("b_ssq", (P, TILES + 1), F32, scope)
                rms = sb("b_rms", (P, TILES + 1), F32, scope)
                level = sb("b_level", (P, LEVELS, P), I32, scope)
                own_row = sb("b_own_row", (NS, NB), F32, scope)
                own_col = sb("b_own_col", (P, NB, NS), F32, scope)
                const_in = sem("b_const_in", scope)
                s0_in = sem("b_s0_in", scope)
                level_ready = sem("b_level_ready", scope)
                own_ready = sem("b_own_ready", scope)
                states_ready = sem("b_states_ready", scope)
                new_states = sem("b_new_states", scope)
                stored = sem("b_stored", scope)
                gate_ready = sem("b_gate_ready", scope)
                ssq_ready = sem("b_ssq_ready", scope)
                rms_ready = sem("b_rms_ready", scope)
                o_ready = sem("b_o_ready", scope)
                y_ready = sem("b_y_ready", scope)
                y_out = sem("b_y_out", scope)
                chain = sem("b_chain", scope)
                spans = ((0, 4), (4, 4), (8, 1))
                COUNTS = (("v", 3), ("p0", 3), ("p1", 2), ("p2", 2), ("p3", 2), ("p4", 2), ("p5", 1), ("p6", 1),
                          ("p7", 1), ("k", 3), ("ds", 2), ("os", 1), ("dss", 2), ("o", 2), ("y", 3))
                M, MISC = {}, 0
                for name, n in COUNTS:
                    M[name] = MISC
                    MISC += n
                assert MISC % cv.ring == 0
                CHAIN = 17

                def level_uses(n):
                    if n == 0:
                        return ((0, 4, P), (4, 4, P), (8, 1, NS))
                    if n <= 3:
                        return ((0, 8, P), (8, 1, NS))
                    if n == 4:
                        return ((0, 4, P), (4, 4, P))
                    return ((0, 8, P),)

                def second(x, n):
                    if n == 0:
                        return x
                    return x.rearrange("p (n two m) -> p n two m", two=2, m=1 << (n - 1))[:, :, 1, :]

                with nc.Block() as block:
                    @block.sync
                    def _(sp):
                        for dst, src in ((level[:, :, :], A["c_level"]), (own_row[:, :], A["c_own_row"]),
                                         (own_col[:, :, :], A["c_own_col"])):
                            sp.dma_start(dst, src).then_inc(const_in, 16)
                        with sp.Fori(0, BH - 1) as i:
                            for j, base in enumerate((COL_BI, COL_BG, COL_BF + P, COL_BQ + P)):
                                cv.load(sp, i * UNITS + (SLOTS + j), j % 2, col(w_in, i * P + base))
                        for j, src in enumerate((col(w_in, COL_BI + D - P), col(w_in, COL_BG + D - P), *then)):
                            cv.load(sp, BH * UNITS - SLOTS + j, j % 2, src)

                    @block.gpsimd
                    def _(pool):
                        with pool.Fori(0, BH) as i:
                            for j in range(UNITS):
                                cv.split(pool, i * UNITS + (SLOTS + j), j % 2, i * (UNITS // 2) + (1 + j // 2), KO)

                    @block.scalar
                    def _(act):
                        act.sem_inc(stored, 32)
                        act.sem_inc(y_ready, 1)
                        act.sem_inc(y_out, 16)

                        def load_states(i):
                            act.wait_ge(stored, i * 32 + 32)
                            act.dma_start(s0[:, :, :], A["state_hgrn"][0, :, bass.ds(i, 1), :, :]
                                          .rearrange("b o k v -> k (o b) v")).then_inc(s0_in, 16)

                        def root(i):
                            act.wait_ge(ssq_ready, i + 1)
                            act.activation(rms[:, :], ssq[:, :], ACT.Sqrt, bias=eps[:, :], scale=1.0 / P)\
                                .then_inc(rms_ready, 1)

                        def store_states(i):
                            act.wait_ge(new_states, i + 1)
                            act.dma_start(OUT["hgrn_p"][0, 0, bass.ds(i, 1), :, :]
                                          .rearrange("o k v -> k (o v)"), state[:, TILES, :]).then_inc(stored, 16)
                            act.dma_start(OUT["hgrn_s"][0, :, bass.ds(i, 1), :, :]
                                          .rearrange("b o k v -> k (o b) v"), s0[:, :, :]).then_inc(stored, 16)

                        def store_y(i):
                            act.wait_ge(y_ready, i + 2)
                            act.dma_start(y_d[bass.ds(i, 1)].rearrange("o p t -> p (o t)"), gate[:, :])\
                                .then_inc(y_out, 16)

                        for j, (dst, func) in enumerate(((f_new, ACT.Sigmoid), (q_new, ACT.Copy), (v_new, ACT.Copy))):
                            for c in range(NCH):
                                cv.empty(act, j, c, dst, func)
                        for c in range(NCH):
                            cv.empty(act, 3, c, g_new, ACT.Sigmoid, raw=g_raw)
                        with act.Fori(0, BH - 1) as i:
                            u = i * UNITS + UNITS
                            load_states(i)
                            act.wait_ge(level_ready, i * 9 + 1)
                            for c in range(NCH):
                                cv.empty(act, u, c, f_new, ACT.Sigmoid)
                            act.wait_ge(level_ready, i * 9 + 2)
                            for c in range(NCH):
                                cv.empty(act, u + 1, c, q_new, ACT.Copy)
                            for c in range(NCH):
                                cv.empty(act, u + 2, c, v_new, ACT.Copy)
                            act.wait_ge(gate_ready, i + 1)
                            cv.empty(act, u + 3, 0, g_new, ACT.Sigmoid, raw=g_raw)
                            store_states(i)
                            root(i)
                            cv.empty(act, u + 3, 1, g_new, ACT.Sigmoid, raw=g_raw)
                            cv.empty(act, u + 3, 2, g_new, ACT.Sigmoid, raw=g_raw)
                            store_y(i)
                        load_states(BH - 1)
                        store_states(BH - 1)
                        root(BH - 1)
                        store_y(BH - 1)
                        act.wait_ge(stored, 32 * BH + 32)
                        act.wait_ge(y_out, 16 * BH + 16)

                    @block.tensor
                    def _(pe):
                        def product(i, n):
                            if n == 0:
                                cv.emptied(pe, i * UNITS + 1)
                            pe.wait_ge(level_ready, i * 9 + 1 + n)
                            q = q_new if n == 0 else qp
                            for m, (b0, nb, w) in enumerate(level_uses(n)):
                                bank = cv.fill(pe, i * MISC, M[f"p{n}"] + m, w < P)
                                wq = w if n == 0 else w // 2
                                for b in range(nb):
                                    ts = slice((b0 + b) * P, (b0 + b) * P + w)
                                    mm = pe.matmul(bank[0:w, b * wq:(b + 1) * wq], kr[:, ts],
                                                   second(q[:, ts], n), start=True, stop=True)
                                mm.then_inc(cv.misc_done, 1)

                        def rows_of(i, src, m):
                            for q, (b0, nb) in enumerate(spans):
                                bank = cv.fill(pe, i * MISC, m + q, q == 2)
                                w = P if q < 2 else NS
                                for b in range(nb):
                                    mm = pe.transpose(bank[0:w, b * P:b * P + P],
                                                      src[:, (b0 + b) * P:(b0 + b) * P + w], ident[:, :])
                                mm.then_inc(cv.misc_done, 1)

                        def own_states(i):
                            cv.copied(pe, i * MISC, M["k"] + 2)
                            for q in range(2):
                                bank = cv.fill(pe, i * MISC, M["ds"] + q)
                                for b in range(4):
                                    mm = pe.matmul(bank[:, b * P:(b + 1) * P], krow[:, 4 * q + b, :],
                                                   vrow[:, 4 * q + b, :], start=True, stop=True)
                                mm.then_inc(cv.misc_done, 1)
                            pe.wait_ge(own_ready, i + 1)
                            pe.wait_ge(s0_in, i * 16 + 16)
                            bank = cv.fill(pe, i * MISC, M["os"], True)
                            pe.matmul(bank[0:NS, 0:P], att[0:NS, TILES, 0:NS], vrow[0:NS, TILES, :],
                                      start=True, stop=False)
                            for b in range(NB):
                                mm = pe.matmul(bank[0:NS, 0:P], qown[:, b, :], s0[:, b, :],
                                               start=False, stop=(b == NB - 1))
                            mm.then_inc(cv.misc_done, 1)
                            for q in range(2):
                                bank = cv.fill(pe, i * MISC, M["dss"] + q, True)
                                pe.matmul(bank[:, :], krow[0:NS, TILES, :], vown[:, 4 * q:4 * q + 4, :],
                                          start=True, stop=True).then_inc(cv.misc_done, 1)

                        def outputs(i):
                            pe.wait_ge(states_ready, i + 1)
                            for q in range(2):
                                bank = cv.fill(pe, i * MISC, M["o"] + q)
                                for b in range(4):
                                    t = 4 * q + b
                                    mm = pe.matmul(bank[:, b * P:(b + 1) * P], att[:, t, :], vrow[:, t, :],
                                                   start=True, stop=(t == 0))
                                    if t > 0:
                                        mm = pe.matmul(bank[:, b * P:(b + 1) * P], qp[:, t * P:(t + 1) * P],
                                                       state[:, t, :], start=False, stop=True)
                                mm.then_inc(cv.misc_done, 1)

                        def back(i):
                            pe.wait_ge(o_ready, i + 1)
                            for q, (b0, nb) in enumerate(spans):
                                bank = cv.fill(pe, i * MISC, M["y"] + q, q == 2)
                                w = P if q < 2 else NS
                                for b in range(nb):
                                    mm = pe.transpose(bank[:, b * P:b * P + w], osb[0:w, b0 + b, :],
                                                      ident[0:w, 0:w])
                                mm.then_inc(cv.misc_done, 1)

                        def start(i):
                            cv.emptied(pe, i * UNITS + 2)
                            rows_of(i, v_new, M["v"])
                            product(i, 0)

                        for j in range(UNITS):
                            for c in range(NCH):
                                cv.project(pe, j, j % 2, c, KO, x_hi, x_lo)
                        with pe.Fori(0, BH - 1) as i:
                            u = i * UNITS + UNITS
                            start(i)
                            cv.project(pe, u, 0, 0, KO, x_hi, x_lo)
                            product(i, 1)
                            cv.project(pe, u, 0, 1, KO, x_hi, x_lo)
                            product(i, 2)
                            cv.project(pe, u, 0, 2, KO, x_hi, x_lo)
                            product(i, 3)
                            cv.project(pe, u + 1, 1, 0, KO, x_hi, x_lo)
                            product(i, 4)
                            cv.project(pe, u + 1, 1, 1, KO, x_hi, x_lo)
                            product(i, 5)
                            cv.project(pe, u + 1, 1, 2, KO, x_hi, x_lo)
                            product(i, 6)
                            cv.project(pe, u + 2, 0, 0, KO, x_hi, x_lo)
                            product(i, 7)
                            cv.project(pe, u + 2, 0, 1, KO, x_hi, x_lo)
                            pe.wait_ge(level_ready, i * 9 + 9)
                            rows_of(i, kr, M["k"])
                            cv.project(pe, u + 2, 0, 2, KO, x_hi, x_lo)
                            own_states(i)
                            cv.project(pe, u + 3, 1, 0, KO, x_hi, x_lo)
                            outputs(i)
                            cv.project(pe, u + 3, 1, 1, KO, x_hi, x_lo)
                            cv.project(pe, u + 3, 1, 2, KO, x_hi, x_lo)
                            back(i)
                        start(BH - 1)
                        for n in range(1, LEVELS):
                            product(BH - 1, n)
                        pe.wait_ge(level_ready, 9 * BH)
                        rows_of(BH - 1, kr, M["k"])
                        own_states(BH - 1)
                        outputs(BH - 1)
                        back(BH - 1)

                    @block.vector
                    def _(dve):
                        ch = Chain(dve, chain)
                        cv.dve_start(dve)
                        ch.step(dve.memset(osb[:, :, :], 0.0))
                        ch.link(dve.memset(att[:, :, :], 0.0))
                        dve.wait_ge(const_in, 48)
                        with dve.Fori(0, BH) as i:
                            ch.loop(i * CHAIN, CHAIN)
                            u, m0 = i * UNITS, i * MISC

                            def take(n):
                                if n > 0:
                                    cv.copied(dve, m0, M[f"p{n}"] - 1)
                                for m, (b0, nb, w) in enumerate(level_uses(n)):
                                    bank = cv.filled(dve, m0, M[f"p{n}"] + m, n > 0)
                                    if n == 0:
                                        dve.tensor_tensor(att[0:w, b0:b0 + nb, 0:w],
                                                          bank[0:w, 0:nb * w].rearrange("p (a b) -> p a b", b=w),
                                                          ident[0:w, 0:w].unsqueeze(1).broadcast_to([w, nb, w]),
                                                          ALU.mult).then_inc(cv.misc_free, 1)
                                        continue
                                    hf = 1 << (n - 1)
                                    nx = w // (2 * hf)

                                    def halves(x):
                                        return x.rearrange("p a (x two m) -> p a x two m", two=2, m=hf)[:, :, :, 1, :]

                                    dst = halves(att[0:w, b0:b0 + nb, 0:w])
                                    msk = halves(level[0:w, n:n + 1, 0:w]).broadcast_to([w, nb, nx, hf])
                                    src = bank[0:w, 0:nb * w // 2].rearrange("p (a x m) -> p a x m", a=nb, m=hf)
                                    dve.copy_predicated(dst, msk, src).then_inc(cv.misc_free, 1)

                            def update(n):
                                dve.wait_ge(cv.misc_done, m0 + M[f"p{n}"] + len(level_uses(n)))
                                dve.wait_ge(level_ready, i * 9 + n + 1)
                                if n == 0:
                                    dve.tensor_tensor(qp[:, :], q_new[:, :], ff[:, :], ALU.mult)\
                                        .then_inc(level_ready, 1)
                                    return
                                nt = NT if n <= 3 else SEQ
                                nb, half_ = nt >> n, 1 << (n - 1)
                                prev = ff if n == 1 else fts[:, ft_at[n - 1]:ft_at[n - 1] + ft_n[n - 1]]
                                fv = prev[:, 0:2 * nb].rearrange("p (n two) -> p n two", two=2)
                                qv = qp[:, 0:nt].rearrange("p (n two m) -> p n two m", two=2, m=half_)
                                kv = kr[:, 0:nt].rearrange("p (n two m) -> p n two m", two=2, m=half_)
                                ch.step(dve.tensor_tensor(fts[:, ft_at[n]:ft_at[n] + nb], fv[:, :, 0], fv[:, :, 1],
                                                          ALU.mult))
                                dve.tensor_tensor(qv[:, :, 1, :], qv[:, :, 1, :],
                                                  fv[:, :, 0:1].broadcast_to([P, nb, half_]), ALU.mult)
                                dve.tensor_tensor(kv[:, :, 0, :], kv[:, :, 0, :],
                                                  fv[:, :, 1:2].broadcast_to([P, nb, half_]), ALU.mult)\
                                    .then_inc(level_ready, 1)

                            def rows_to(dst, m):
                                for q, (b0, nb) in enumerate(spans):
                                    bank = cv.filled(dve, m0, m + q)
                                    w = P if q < 2 else NS
                                    dve.tensor_copy(dst[0:w, b0:b0 + nb, :], bank[0:w, 0:nb * P]
                                                    .rearrange("p (a b) -> p a b", b=P)).then_inc(cv.misc_free, 1)

                            cv.emptied(dve, u)
                            ch.link(dve.tensor_scalar(ff[:, :], f_new[:, :], one_lb[:, bass.ds(i, 1)],
                                                      lb[:, bass.ds(i, 1)], ALU.mult, ALU.add))
                            dve.tensor_scalar(kr[:, :], ff[:, :], -1.0, 1.0, ALU.mult, ALU.add)\
                                .then_inc(level_ready, 1)
                            rows_to(vrow, M["v"])
                            for n in range(4):
                                update(n)
                                take(n)
                            ch.step(dve.tensor_tensor(
                                vown[:, :, :], vrow[0:NS, TILES:TILES + 1, :].broadcast_to([NS, NB, P]),
                                own_row[:, :].unsqueeze(2).broadcast_to([NS, NB, P]), ALU.mult))
                            dve.wait_ge(level_ready, i * 9 + 5)
                            dve.tensor_tensor(qown[:, :, :], qp[:, SEQ:NT].unsqueeze(1)
                                              .broadcast_to([P, NB, NS]), own_col[:, :, :], ALU.mult)\
                                .then_inc(own_ready, 1)
                            for n in range(4, LEVELS):
                                update(n)
                                take(n)
                            cv.emptied(dve, u + 3)
                            dve.wait_ge(y_out, i * 16 + 16)
                            dve.tensor_tensor(gate[:, :], g_new[:, :], g_raw[:, :], ALU.mult)\
                                .then_inc(gate_ready, 1)
                            rows_to(krow, M["k"])
                            f7 = fts[:, ft_at[7]:ft_at[7] + TILES]
                            f3 = fts[:, ft_at[3] + SEQ // TB:ft_at[3] + NT // TB]
                            dve.wait_ge(stored, i * 32 + 32)
                            for t in range(TILES):
                                if t % 4 == 0:
                                    bank = cv.filled(dve, m0, M["ds"] + t // 4)
                                src = bank[:, (t % 4) * P:(t % 4 + 1) * P]
                                if t == 0:
                                    ch.step(dve.tensor_copy(state[:, 1, :], src))
                                    continue
                                ch.wait()
                                ins = dve.scalar_tensor_tensor(
                                    out=state[:, t + 1, :], in0=state[:, t, :], scalar=f7[:, t:t + 1],
                                    in1=src, op0=ALU.mult, op1=ALU.add)
                                if t == 3:
                                    ins.then_inc(cv.misc_free, 1)
                                    cv.copied(dve, m0, M["ds"])
                                elif t == TILES - 1:
                                    ins.then_inc(cv.misc_free, 1)
                                else:
                                    ch.step(ins)
                            cv.copied(dve, m0, M["ds"] + 1)
                            dve.sem_inc(states_ready, 1)
                            bank = cv.filled(dve, m0, M["os"])
                            dve.tensor_copy(osb[0:NS, TILES, :], bank[0:NS, 0:P]).then_inc(cv.misc_free, 1)
                            for q in range(2):
                                bank = cv.filled(dve, m0, M["dss"] + q)
                                for b in range(4 * q, 4 * q + 4):
                                    ins = dve.scalar_tensor_tensor(
                                        out=s0[:, b, :], in0=s0[:, b, :], scalar=f3[:, b:b + 1],
                                        in1=bank[:, (b % 4) * P:(b % 4 + 1) * P], op0=ALU.mult, op1=ALU.add)
                                ins.then_inc(cv.misc_free, 1)
                            cv.copied(dve, m0, M["dss"] + 1)
                            dve.sem_inc(new_states, 1)
                            for q in range(2):
                                bank = cv.filled(dve, m0, M["o"] + q)
                                dve.tensor_copy(osb[:, 4 * q:4 * q + 4, :],
                                                bank[:, :].rearrange("p (a b) -> p a b", b=P))\
                                    .then_inc(cv.misc_free, 1)
                            cv.copied(dve, m0, M["o"] + 1)
                            ch.link(dve.tensor_tensor(osq[:, :, :], osb[:, :, :], osb[:, :, :], ALU.mult))
                            dve.tensor_reduce(ssq[:, :], osq[:, :, :], AX.X, ALU.add).then_inc(ssq_ready, 1)
                            dve.wait_ge(rms_ready, i + 1)
                            ch.link(dve.reciprocal(rms[:, :], rms[:, :]))
                            dve.tensor_tensor(osb[:, :, :], osb[:, :, :],
                                              rms[:, :].unsqueeze(2).broadcast_to([P, TILES + 1, P]), ALU.mult)\
                                .then_inc(o_ready, 1)
                            dve.wait_ge(gate_ready, i + 1)
                            for q, (b0, nb) in enumerate(spans):
                                bank = cv.filled(dve, m0, M["y"] + q)
                                n = nb * P if q < 2 else NS
                                ts = slice(b0 * P, b0 * P + n)
                                dve.scalar_tensor_tensor(out=gate[:, ts], in0=bank[:, 0:n], scalar=h_norm[:, :],
                                                         in1=gate[:, ts], op0=ALU.mult, op1=ALU.mult)\
                                    .then_inc(cv.misc_free, 1)
                            cv.copied(dve, m0, M["y"] + 2)
                            dve.sem_inc(y_ready, 1)
                            ch.end(BH)

        def attention_phase(then):
            UNITS, MISC = 10, 51
            KB = 4
            KW = KB * P + AG * NS
            K_G = (0, 1, 1, 2)
            scope = ExitStack()
            with scope:
                cv = Conveyor("a", scope, (3, 4, 7), AH * UNITS)
                qk = [sb(f"a_feature{i}", (P, NT), F32, scope) for i in range(4)]
                vrow = [sb(f"a_v_rows{g}", (P, TILES + 1, P), F32, scope) for g in range(AG)]
                krow = sb("a_k_rows", (P, TILES + 1, P), F32, scope)
                gate = sb("a_gate", (P, NT), F32, scope)
                graw = sb("a_gate_raw", (P, NT), F32, scope)
                T_COLS = [[P] + [2 * P] * 7, [P, 2 * P] * 4, [P] * 8]
                T_AT, at = [], 0
                for g in range(AG):
                    row = []
                    for w in T_COLS[g]:
                        row.append(at)
                        at += w
                    T_AT.append(row)
                prob = sb("a_prob", (P, at), F32, scope)
                pt = [sb(f"a_prob_t{i}", (P, 4, P), F32, scope) for i in range(2)]
                mx = sb("a_max", (P, AG, TILES), F32, scope)
                st = sb("a_stats", (P, AG, TILES, 2), F32, scope)
                comm = sb("a_stats_by_token", (P, TILES, 2, 2), F32, scope)
                nmin = sb("a_least", (P, TILES), F32, scope)
                ex = sb("a_group_exp", (P, AG, TILES), F32, scope)
                lw = sb("a_group_sum", (P, AG, TILES), F32, scope)
                den = sb("a_denominator", (P, TILES), F32, scope)
                wt = sb("a_weight", (P, TILES, 2), F32, scope)
                w0 = sb("a_weight0", (P, TILES), F32, scope)
                w12 = sb("a_weight12", (P, 2, TILES), F32, scope)
                yt = graw
                kv = [sb(f"s_cached{i}", (P, KB, P), F32, scope) for i in range(NB + 4)]
                VC = [8, 9, 10, 11, 0, 1, 2, 3]
                mask = sb("s_mask", (NS, KW), F32, scope)
                qh = sb("s_q", (P, AG, NS), F32, scope)
                kh = sb("s_k", (P, AG, NS), F32, scope)
                kt = [sb(f"s_k_feature{i}", (P, KB, P), F32, scope) for i in range(2)]
                sct = sb("s_scores_t", (P, KB, NS), F32, scope)
                sprob = sb("s_prob", (NS, KW), F32, scope)
                spt = sb("s_prob_t", (P, KB + AG, NS), F32, scope)
                smx = sb("s_max", (NS, 1), F32, scope)
                snm = sb("s_negmax", (NS, 1), F32, scope)
                ssm = sb("s_sum", (NS, 1), F32, scope)
                mask_in = sem("s_mask_in", scope)
                k_in = [sem(f"s_k_in{b}", scope) for b in range(NB)]
                v_in = [sem(f"s_v_in{b}", scope) for b in range(NB)]
                keys_used = sem("s_keys_used", scope)
                s_scores_done = sem("s_scores_done", scope)
                s_scores_out = sem("s_scores_copied", scope)
                s_negmax = sem("s_negmax_ready", scope)
                s_exp_done = sem("s_exp_done", scope)
                s_prob_ready = sem("s_prob_ready", scope)
                s_o_done = sem("s_o_done", scope)
                caches = [A["cache_kv_w128"][0], A["cache_kv_w512"][0], A["cache_kv_w2048"][0]]

                scores_max = sem("a_negmax_ready", scope)
                exp_done = sem("a_exp_done", scope)
                stats_out = sem("a_stats_out", scope)
                stats_in = sem("a_stats_in", scope)
                spread = sem("a_spread_ready", scope)
                group_exp = sem("a_group_exp_ready", scope)
                weights_ready = sem("a_weights_ready", scope)
                weights_out = sem("a_weights_out", scope)
                weights_in = sem("a_weights_in", scope)
                scaled = sem("a_prob_scaled", scope)
                krow_ready = sem("a_krow_ready", scope)
                krow_out = sem("a_krow_out", scope)
                vrow_out = sem("a_vrow_out", scope)
                o_done = sem("a_o_done", scope)
                y_ready = sem("a_y_ready", scope)
                y_out = sem("a_y_out", scope)
                chain = sem("a_chain", scope)
                CHAIN = 52
                spans = ((0, 4), (4, 4), (8, 1))
                COLS = [COL_AQ, COL_AK, COL_AQ + GROUP, COL_AK + GROUP, COL_AQ + 2 * GROUP,
                        COL_AK + 2 * GROUP, COL_AV, COL_AV + GROUP, COL_AV + 2 * GROUP, COL_AG]
                DST = [qk[0], qk[1], qk[2], qk[3], qk[0], qk[1], qk[2], qk[3], qk[0], gate]
                U_Q, U_K, U_V, U_G = (0, 2, 4), (1, 3, 5), (6, 7, 8), 9
                M_S, M_K, M_V = (0, 7, 14), (4, 11, 18), (29, 34, 38)
                M_KT, M_NEW, M_SC, M_SPT, M_O = 21, 32, 33, 37, 42
                M_P = [41] + [43 + n for n in range(8)]
                V_OUT = 16 * 6

                def tokens(src, g, c):
                    if g == 0:
                        return src[:, c * P:(c + 1) * P]
                    if g == 1:
                        r, n = c // 2, c % 2
                        return src[:, 4 * P * n + r:4 * P * n + r + 4 * (P - 1) + 1:4]
                    return src[:, c:c + 8 * (P - 1) + 1:8]

                def keys(src, g, c):
                    if g == 0 and c > 0:
                        return src[:, (c - 1) * P:(c + 1) * P]
                    if g == 1 and c % 2 == 1:
                        return src[:, c // 2:c // 2 + 4 * (2 * P - 1) + 1:4]
                    return tokens(src, g, c)

                BLOCKS = []
                for g in range(AG):
                    for c in range(TILES):
                        w = T_COLS[g][c] // P
                        for b in range(w):
                            BLOCKS.append((g, c, T_AT[g][c] + b * P, c - (w - 1) + b))
                N_PT = (len(BLOCKS) + 3) // 4
                assert N_PT == len(M_P)

                def load_rows(sp, dst, b, which, hd, done):
                    c = [x[b, :, which, hd, :] for x in caches]
                    sp.dma_start(dst[:, 0:1, :], c[0].rearrange("(n p) o e -> p n (o e)", p=P)).then_inc(done, 16)
                    sp.dma_start(dst[:, 1:3, :], c[1].rearrange("(n p) o e -> p n (o e)", p=P)).then_inc(done, 16)
                    sp.dma_start(dst[:, 3, :], c[2].rearrange("(a r) o e -> a r (o e)", r=16)[:, 0:8, :])\
                        .then_inc(done, 16)

                with nc.Block() as block:
                    @block.sync
                    def _(sp):
                        sp.dma_start(mask[:, :], A["c_sample_mask"]).then_inc(mask_in, 16)
                        def head(h, after):
                            hd = bass.ds(h, 1)
                            for j in range(SLOTS, UNITS):
                                cv.load(sp, h * UNITS + j, j % 2, col(w_in, h * P + COLS[j]))
                                if j == 4:
                                    sp.wait_ge(s_o_done, h + 1)
                                    sp.sem_inc(cv.held_sp, 1)
                                if j in (4, 5):
                                    for b in range(4 * (j - 4), 4 * (j - 4) + 4):
                                        load_rows(sp, kv[b], b, 0, hd, k_in[b])
                                if j == 6:
                                    for b in range(4):
                                        load_rows(sp, kv[VC[b]], b, 1, hd, v_in[b])
                            cv.load(sp, h * UNITS + UNITS, 0, after[0])
                            sp.wait_ge(keys_used, h + 1)
                            sp.sem_inc(cv.held_sp, 1)
                            for b in range(4, NB):
                                load_rows(sp, kv[VC[b]], b, 1, hd, v_in[b])
                            sp.wait_ge(exp_done, h * AG + AG)
                            sp.sem_inc(cv.held_sp, 1)
                            d = stat_d[bass.ds(h, 1)]
                            sp.dma_start(d[:, :, 0, :].rearrange("o (n i r) s -> i (o r) n s", n=2, r=4),
                                         st[:, 1, :, :].rearrange("p (r n) s -> p r n s", n=2),
                                         allow_slow_non_contiguous=True).then_inc(stats_out, 16)
                            sp.dma_start(d[:, :, 1, :].rearrange("o (i j) s -> i (o j) s", j=8),
                                         st[:, 2, :, :], allow_slow_non_contiguous=True).then_inc(stats_out, 16)
                            sp.wait_ge(stats_out, h * 32 + 32)
                            sp.sem_inc(cv.held_sp, 1)
                            sp.dma_start(comm[:, :, :, :], d.rearrange("o (b p) g s -> p (o b) g s", p=P),
                                         allow_slow_non_contiguous=True).then_inc(stats_in, 16)
                            cv.load(sp, h * UNITS + (UNITS + 1), 1, after[1])
                            sp.wait_ge(weights_ready, h + 1)
                            sp.sem_inc(cv.held_sp, 1)
                            d = weight_d[bass.ds(h, 1)]
                            sp.dma_start(d.rearrange("o (b p) g -> p (o b) g", p=P), wt[:, :, :],
                                         allow_slow_non_contiguous=True).then_inc(weights_out, 16)
                            sp.wait_ge(weights_out, h * 16 + 16)
                            sp.sem_inc(cv.held_sp, 1)
                            for n in range(2):
                                sp.dma_start(w12[:, 0, n:TILES:2],
                                             d[:, :, 0].rearrange("o (n i r) -> n i (o r)", n=2, r=4)[n],
                                             allow_slow_non_contiguous=True).then_inc(weights_in, 16)
                            sp.dma_start(w12[:, 1, :], d[:, :, 1].rearrange("o (i j) -> i (o j)", j=8),
                                         allow_slow_non_contiguous=True).then_inc(weights_in, 16)

                        with sp.Fori(0, AH - 1) as h:
                            head(h, [col(w_in, h * P + (P + COLS[j])) for j in range(SLOTS)])
                        head(AH - 1, then)

                    @block.gpsimd
                    def _(pool):
                        with pool.Fori(0, AH) as h:
                            for j in range(UNITS):
                                cv.split(pool, h * UNITS + (SLOTS + j), j % 2, h * (UNITS // 2) + (1 + j // 2), KO)

                    @block.tensor
                    def _(pe):
                        pe.sem_inc(s_o_done, 1)
                        with pe.Fori(0, AH) as h:
                            u, m0 = h * UNITS, h * MISC

                            def chunk(j, c):
                                cv.project(pe, u + j, j % 2, c, KO, x_hi, x_lo)

                            def unit(j):
                                for c in range(NCH):
                                    chunk(j, c)

                            def scores(g):
                                cv.emptied(pe, u + U_K[g])
                                for n in range(4):
                                    bank = cv.fill(pe, m0, M_S[g] + n)
                                    for c in (2 * n, 2 * n + 1):
                                        w = T_COLS[g][c]
                                        a = (c % 2) * 2 * P
                                        mm = pe.matmul(bank[:, a:a + w], tokens(DST[U_Q[g]], g, c),
                                                       keys(DST[U_K[g]], g, c), start=True, stop=True)
                                    mm.then_inc(cv.misc_done, 1)

                            def rows(src, m, g):
                                for q, (b0, nb) in enumerate(spans):
                                    bank = cv.fill(pe, m0, m + q, q == 2)
                                    for b in range(b0, b0 + nb):
                                        if b == TILES:
                                            mm = pe.transpose(bank[0:NS, 0:P], src[:, SEQ:NT], ident[:, :])
                                        else:
                                            mm = pe.transpose(bank[:, (b % 4) * P:(b % 4 + 1) * P],
                                                              tokens(src, g, b), ident[:, :])
                                    mm.then_inc(cv.misc_done, 1)

                            def v_rows(g):
                                cv.emptied(pe, u + U_V[g])
                                rows(DST[U_V[g]], M_V[g], g)

                            unit(0)
                            unit(1)
                            unit(2)
                            scores(0)
                            rows(DST[U_K[0]], M_K[0], 0)
                            unit(3)
                            unit(4)
                            scores(1)
                            rows(DST[U_K[1]], M_K[1], 0)
                            unit(5)
                            unit(6)
                            scores(2)
                            rows(DST[U_K[2]], M_K[2], 0)
                            def keys_t(b):
                                pe.wait_ge(k_in[b], h * 48 + 48)
                                bank = cv.fill(pe, m0, M_KT + b)
                                for n in range(KB):
                                    mm = pe.transpose(bank[:, n * P:(n + 1) * P], kv[b][:, n, :], ident[:, :])
                                mm.then_inc(cv.misc_done, 1)

                            def key_scores(b):
                                cv.copied(pe, m0, M_KT + b)
                                pe.sem_inc(cv.held_pe, 1)
                                for n in range(KB):
                                    mm = pe.matmul(psum[:, 5, n * NS + b * TB:n * NS + (b + 1) * TB],
                                                   kt[b % 2][:, n, :], qh[:, K_G[n], b * TB:(b + 1) * TB],
                                                   start=True, stop=True)
                                return mm

                            pe.wait_ge(scores_max, h * AG + AG)
                            pe.wait_ge(y_ready, h + 1)
                            keys_t(0)
                            keys_t(1)
                            chunk(7, 0)
                            key_scores(0)
                            key_scores(1)
                            keys_t(2)
                            keys_t(3)
                            chunk(7, 1)
                            key_scores(2)
                            key_scores(3).then_inc(keys_used, 1)
                            keys_t(4)
                            keys_t(5)
                            chunk(7, 2)
                            key_scores(4)
                            key_scores(5)
                            keys_t(6)
                            keys_t(7)
                            v_rows(0)
                            chunk(8, 0)
                            key_scores(6)
                            key_scores(7).then_inc(s_scores_done, 1)
                            bank = cv.fill(pe, m0, M_NEW, True)
                            for g in range(AG):
                                mm = pe.matmul(bank[0:NS, g * NS:(g + 1) * NS], qh[:, g, :], kh[:, g, :],
                                               start=True, stop=True)
                            mm.then_inc(cv.misc_done, 1)
                            chunk(8, 1)
                            pe.wait_ge(s_scores_out, h + 1)
                            bank = cv.fill(pe, m0, M_SC, True)
                            for n in range(KB):
                                mm = pe.transpose(bank[0:NS, n * P:(n + 1) * P], sct[:, n, :], ident[:, :])
                            mm.then_inc(cv.misc_done, 1)
                            chunk(8, 2)
                            v_rows(1)
                            unit(9)
                            pe.wait_ge(s_prob_ready, h + 1)
                            bank = cv.fill(pe, m0, M_SPT, True)
                            for n in range(KB):
                                mm = pe.transpose(bank[:, n * NS:(n + 1) * NS], sprob[:, n * P:(n + 1) * P],
                                                  ident[0:NS, 0:NS])
                            for n in range(KB, KB + AG):
                                a = KB * P + (n - KB) * NS
                                mm = pe.transpose(bank[0:NS, n * NS:(n + 1) * NS], sprob[:, a:a + NS],
                                                  ident[0:NS, 0:NS])
                            mm.then_inc(cv.misc_done, 1)
                            v_rows(2)

                            def sample_values():
                                cv.copied(pe, m0, M_V[2] + 2)
                                bank = cv.fill(pe, m0, M_O, True)
                                for g in range(AG):
                                    pe.matmul(bank[:, 0:NS], vrow[g][0:NS, TILES, :], spt[0:NS, KB + g, :],
                                              start=(g == 0), stop=False, skip_group_check=True)
                                for b in range(NB):
                                    pe.wait_ge(v_in[b], h * 48 + 48)
                                    for n in range(KB):
                                        mm = pe.matmul(bank[:, b * TB:(b + 1) * TB], kv[VC[b]][:, n, :],
                                                       spt[:, n, b * TB:(b + 1) * TB], start=False,
                                                       stop=(b == NB - 1 and n == KB - 1), skip_group_check=True)
                                mm.then_inc(cv.misc_done, 1)
                                pe.sem_inc(s_o_done, 1)

                            def turn(n):
                                bank = cv.fill(pe, m0, M_P[n])
                                for b, (g, c, at, kb) in enumerate(BLOCKS[4 * n:4 * n + 4]):
                                    mm = pe.transpose(bank[:, b * P:(b + 1) * P], prob[:, at:at + P], ident[:, :])
                                mm.then_inc(cv.misc_done, 1)

                            def values(n):
                                cv.copied(pe, m0, M_P[n])
                                mm = None
                                for b, (g, c, at, kb) in enumerate(BLOCKS[4 * n:4 * n + 4]):
                                    rhs = pt[n % 2][:, b, :]
                                    v = vrow[g][:, kb, :]
                                    if g == 0:
                                        mm = pe.matmul(psum[:, 5 + c // 4, (c % 4) * P:(c % 4 + 1) * P], v, rhs,
                                                       start=(c % 4 == 0 and kb == max(c - 1, 0)), stop=False,
                                                       skip_group_check=True)
                                    elif g == 1:
                                        mm = pe.matmul(psum[:, 5 + c % 2, c // 2:c // 2 + 4 * (P - 1) + 1:4], v, rhs,
                                                       start=False, stop=False, skip_group_check=True)
                                    else:
                                        for k in range(2):
                                            mm = pe.matmul(psum[:, 5 + k, c:c + 8 * 63 + 1:8], v,
                                                           rhs[:, 64 * k:64 * k + 64], start=False,
                                                           stop=(c == TILES - 1), skip_group_check=True)
                                return mm

                            pe.wait_ge(scaled, h + 1)
                            turn(0)
                            sample_values()
                            for n in range(1, N_PT):
                                turn(n)
                                values(n - 1)
                            values(N_PT - 1).then_inc(o_done, 1)

                    @block.scalar
                    def _(act):
                        act.sem_inc(y_ready, 1)
                        act.sem_inc(y_out, 16)
                        act.sem_inc(krow_out, 32)
                        act.sem_inc(vrow_out, V_OUT)
                        with act.Fori(0, AH) as h:
                            u = h * UNITS

                            def unit(j):
                                for c in range(NCH):
                                    cv.empty(act, u + j, c, DST[j], ACT.Copy)

                            def exps(g):
                                act.wait_ge(scores_max, h * AG + g + 1)
                                for c in range(TILES):
                                    a, w = T_AT[g][c], T_COLS[g][c]
                                    ins = act.activation(prob[:, a:a + w], prob[:, a:a + w], ACT.Exp,
                                                         bias=st[:, g, c, 0:1], scale=SCALE,
                                                         accum_out=st[:, g, c, 1:2])
                                ins.then_inc(exp_done, 1)

                            def rows_out(g, which, src, done):
                                o = OUT[("kv128_p", "kv512_p", "kv2048_p")[g]]
                                hd = bass.ds(h, 1)
                                if g == 0:
                                    act.dma_start(o[0, 0, :, which, hd, :], src[:, TILES - 1:TILES, :]).then_inc(done, 16)
                                elif which == 0:
                                    b0 = 4 if g == 1 else 0
                                    act.dma_start(o[0, 0, :, which, hd, :].rearrange("(b p) o e -> p b (o e)", p=P),
                                                  src[:, b0:TILES, :]).then_inc(done, 16)
                                elif g == 1:
                                    act.dma_start(o[0, 0, :, which, hd, :].rearrange("(i r) o e -> i r (o e)", r=4),
                                                  src[:, 1:TILES:2, :]).then_inc(done, 16)
                                else:
                                    act.dma_start(o[0, 0, :, which, hd, :].rearrange("(i j) o e -> i j (o e)", j=8),
                                                  src[:, 0:TILES, :]).then_inc(done, 16)
                                o = OUT[("kv128_s", "kv512_s", "kv2048_s")[g]]
                                act.dma_start(o[0, :, :, which, hd, :].rearrange("b t o e -> (b t) (o e)"),
                                              src[0:NS, TILES, :]).then_inc(done, 16)

                            unit(0)
                            unit(1)
                            unit(2)
                            unit(3)
                            exps(0)
                            act.wait_ge(krow_ready, h * 6 + 1)
                            rows_out(0, 0, krow, krow_out)
                            unit(4)
                            unit(5)
                            exps(1)
                            act.wait_ge(krow_ready, h * 6 + 2)
                            rows_out(1, 0, krow, krow_out)
                            unit(6)
                            unit(7)
                            exps(2)
                            act.wait_ge(krow_ready, h * 6 + 3)
                            rows_out(2, 0, krow, krow_out)
                            act.wait_ge(spread, h + 1)
                            act.activation(ex[:, :, :], ex[:, :, :], ACT.Exp).then_inc(group_exp, 1)
                            unit(8)
                            act.wait_ge(krow_ready, h * 6 + 4)
                            rows_out(0, 1, vrow[0], vrow_out)
                            act.wait_ge(s_negmax, h + 1)
                            act.activation(sprob[:, :], sprob[:, :], ACT.Exp, bias=snm[:, :], scale=SCALE,
                                           accum_out=ssm[:, :]).then_inc(s_exp_done, 1)
                            act.wait_ge(y_out, h * 16 + 16)
                            for c in range(NCH):
                                cv.empty(act, u + U_G, c, gate, ACT.Sigmoid, raw=graw)
                            act.wait_ge(krow_ready, h * 6 + 5)
                            rows_out(1, 1, vrow[1], vrow_out)
                            act.wait_ge(krow_ready, h * 6 + 6)
                            rows_out(2, 1, vrow[2], vrow_out)
                            act.wait_ge(y_ready, h + 2)
                            act.dma_start(y_d[bass.ds(h + Y_A, 1), :, :].rearrange("o p t -> p (o t)"), yt[:, :])\
                                .then_inc(y_out, 16)
                        act.wait_ge(y_out, 16 * AH + 16)
                        act.wait_ge(krow_out, 96 * AH + 32)
                        act.wait_ge(vrow_out, V_OUT * AH + V_OUT)

                    @block.vector
                    def _(dve):
                        ch = Chain(dve, chain)
                        cv.dve_start(dve)
                        dve.wait_ge(mask_in, 16)
                        with dve.Fori(0, AH) as h:
                            ch.loop(h * CHAIN, CHAIN)
                            u, m0 = h * UNITS, h * MISC

                            def scores(g):
                                cv.emptied(dve, u + U_K[g])
                                for dst, src in ((qh, DST[U_Q[g]]), (kh, DST[U_K[g]])):
                                    ch.step(dve.tensor_copy(dst[:, g, :], src[:, SEQ:NT]))
                                for n in range(4):
                                    bank = cv.filled(dve, m0, M_S[g] + n)
                                    for c in (2 * n, 2 * n + 1):
                                        a, w = T_AT[g][c], T_COLS[g][c]
                                        mask = pair[:, :] if g == 2 else band[:, 2 * P - w:2 * P]
                                        ps_ = bank[:, (c % 2) * 2 * P:(c % 2) * 2 * P + w]
                                        ins = dve.tensor_tensor(prob[:, a:a + w], ps_, mask, ALU.add)
                                        if c % 2:
                                            ins.then_inc(cv.misc_free, 1)
                                cv.copied(dve, m0, M_S[g] + 3)
                                if g == 0:
                                    parts = ((0, 1, 1, P), (1, 7, 1, 2 * P))
                                elif g == 1:
                                    parts = ((0, 4, 2, P), (1, 4, 2, 2 * P))
                                else:
                                    parts = ((0, 8, 1, P),)
                                for c0, n, step, w in parts:
                                    if g == 1:
                                        pv = prob[:, T_AT[1][0]:T_AT[1][0] + 12 * P]\
                                            .rearrange("p (n w) -> p n w", w=3 * P)[:, :, c0 * P:c0 * P + w]
                                    else:
                                        pv = prob[:, T_AT[g][c0]:T_AT[g][c0] + n * w].rearrange("p (n w) -> p n w", w=w)
                                    ch.step(dve.tensor_reduce(mx[:, g, c0:c0 + step * (n - 1) + 1:step], pv,
                                                              AX.X, ALU.max))
                                ch.wait()
                                dve.tensor_scalar(st[:, g, :, 0], mx[:, g, :], -SCALE, None, ALU.mult)\
                                    .then_inc(scores_max, 1)

                            def rows(dst, m):
                                for q, (b0, nb) in enumerate(spans):
                                    bank = cv.filled(dve, m0, m + q)
                                    w = P if q < 2 else NS
                                    dve.tensor_copy(dst[0:w, b0:b0 + nb, :], bank[0:w, 0:nb * P]
                                                    .rearrange("p (a b) -> p a b", b=P)).then_inc(cv.misc_free, 1)
                                cv.copied(dve, m0, m + 2)
                                dve.sem_inc(krow_ready, 1)

                            scores(0)
                            dve.wait_ge(krow_out, h * 96 + 32)
                            rows(krow, M_K[0])
                            scores(1)
                            dve.wait_ge(krow_out, h * 96 + 64)
                            rows(krow, M_K[1])
                            scores(2)
                            dve.wait_ge(krow_out, h * 96 + 96)
                            rows(krow, M_K[2])
                            for b in range(NB):
                                bank = cv.filled(dve, m0, M_KT + b)
                                dve.tensor_copy(kt[b % 2][:, :, :], bank.rearrange("p (a b) -> p a b", b=P))\
                                    .then_inc(cv.misc_free, 1)
                            dve.wait_ge(vrow_out, h * V_OUT + V_OUT)
                            rows(vrow[0], M_V[0])
                            bank = cv.filled(dve, m0, M_NEW)
                            dve.tensor_tensor(sprob[:, KB * P:KW], bank[0:NS, 0:AG * NS], mask[:, KB * P:KW], ALU.add)\
                                .then_inc(cv.misc_free, 1)
                            dve.wait_ge(s_scores_done, h + 1)
                            dve.tensor_copy(sct[:, :, :], psum[:, 5, 0:KB * NS].rearrange("p (a b) -> p a b", b=NS))\
                                .then_inc(s_scores_out, 1)
                            dve.wait_ge(exp_done, h * AG + AG)
                            dve.wait_ge(stats_in, h * 16 + 16)
                            nm = [st[:, 0, :, 0], comm[:, :, 0, 0], comm[:, :, 1, 0]]
                            ls = [st[:, 0, :, 1], comm[:, :, 0, 1], comm[:, :, 1, 1]]
                            ch.link(dve.tensor_tensor(nmin[:, :], nm[0], nm[1], ALU.min))
                            ch.link(dve.tensor_tensor(nmin[:, :], nmin[:, :], nm[2], ALU.min))
                            for g in range(AG):
                                ch.step(dve.tensor_tensor(ex[:, g, :], nmin[:, :], nm[g], ALU.subtract))
                            ch.wait()
                            dve.sem_inc(spread, 1)
                            dve.wait_ge(group_exp, h + 1)
                            for g in range(AG):
                                ch.step(dve.tensor_tensor(lw[:, g, :], ex[:, g, :], ls[g], ALU.mult))
                            ch.wait()
                            ch.link(dve.tensor_tensor(den[:, :], lw[:, 0, :], lw[:, 1, :], ALU.add))
                            ch.link(dve.tensor_tensor(den[:, :], den[:, :], lw[:, 2, :], ALU.add))
                            ch.link(dve.reciprocal(den[:, :], den[:, :]))
                            ch.step(dve.tensor_tensor(w0[:, :], ex[:, 0, :], den[:, :], ALU.mult))
                            for g in (1, 2):
                                ch.step(dve.tensor_tensor(wt[:, :, g - 1], ex[:, g, :], den[:, :], ALU.mult))
                            ch.wait()
                            dve.sem_inc(weights_ready, 1)
                            bank = cv.filled(dve, m0, M_SC)
                            dve.tensor_tensor(sprob[:, 0:KB * P], bank[0:NS, :], mask[:, 0:KB * P], ALU.add)\
                                .then_inc(cv.misc_free, 1)
                            cv.copied(dve, m0, M_SC)
                            ch.link(dve.tensor_reduce(smx[:, :], sprob[:, :], AX.X, ALU.max))
                            dve.tensor_scalar(snm[:, :], smx[:, :], -SCALE, None, ALU.mult).then_inc(s_negmax, 1)
                            rows(vrow[1], M_V[1])
                            dve.wait_ge(s_exp_done, h + 1)
                            ch.link(dve.reciprocal(ssm[:, :], ssm[:, :]))
                            dve.tensor_scalar(sprob[:, :], sprob[:, :], ssm[:, :], None, ALU.mult)\
                                .then_inc(s_prob_ready, 1)
                            dve.wait_ge(weights_in, h * 48 + 48)
                            for g in range(AG):
                                for c in range(TILES):
                                    a, w = T_AT[g][c], T_COLS[g][c]
                                    sc = w0[:, c:c + 1] if g == 0 else w12[:, g - 1, c:c + 1]
                                    ch.step(dve.tensor_scalar(prob[:, a:a + w], prob[:, a:a + w], sc, None, ALU.mult))
                            ch.wait()
                            dve.sem_inc(scaled, 1)
                            bank = cv.filled(dve, m0, M_SPT)
                            dve.tensor_copy(spt[:, 0:KB, :], bank[:, 0:KB * NS].rearrange("p (a b) -> p a b", b=NS))
                            dve.tensor_copy(spt[0:NS, KB:KB + AG, :], bank[0:NS, KB * NS:(KB + AG) * NS]
                                            .rearrange("p (a b) -> p a b", b=NS)).then_inc(cv.misc_free, 1)
                            rows(vrow[2], M_V[2])
                            cv.emptied(dve, u + U_G)
                            ch.link(dve.tensor_tensor(gate[:, :], gate[:, :], graw[:, :], ALU.mult))
                            for n in range(N_PT):
                                bank = cv.filled(dve, m0, M_P[n])
                                nb = min(4, len(BLOCKS) - 4 * n)
                                dve.tensor_copy(pt[n % 2][:, 0:nb, :], bank[:, 0:nb * P]
                                                .rearrange("p (a b) -> p a b", b=P)).then_inc(cv.misc_free, 1)
                                if n == 0:
                                    bank = cv.filled(dve, m0, M_O)
                                    dve.tensor_tensor(yt[:, SEQ:NT], bank[:, 0:NS], gate[:, SEQ:NT], ALU.mult)\
                                        .then_inc(cv.misc_free, 1)
                            dve.wait_ge(o_done, h + 1)
                            cv.copied(dve, m0, M_O)
                            dve.tensor_tensor(yt[:, 0:SEQ], psum[:, 5:7, :].rearrange("p a b -> p (a b)"),
                                              gate[:, 0:SEQ], ALU.mult).then_inc(y_ready, 1)
                            ch.end(AH)

        def pool_phase(then):
            EXT = HIST + SEQ
            SEXT = HIST + TB
            scope = ExitStack()
            with scope:
                cv = Conveyor("c", scope, (3, 4, 5, 6), 2 * CG)
                hist = sb("c_hist", (NB * HIST, GROUP), F32, scope)
                ext = [sb(f"c_ext{i}", (P, EXT + NB * SEXT), F32, scope) for i in range(2)]
                acc = [sb(f"c_sum{i}", (P, EXT + NB * SEXT), F32, scope) for i in range(2)]
                pooled = sb("c_pooled", (P, NT), F32, scope)
                gate = sb("c_gate", (P, NT), F32, scope)
                graw = sb("c_gate_raw", (P, NT), F32, scope)
                yt = sb("c_y", (P, NT), F32, scope)
                count = sb("c_count", (P, CG, HIST), F32, scope)
                pw = sb("c_pool_w", (P, CG, P), F32, scope)
                last_p = sb("c_last_p", (HIST, GROUP), F32, scope)
                last_s = sb("c_last_s", (NB * HIST, GROUP), F32, scope)
                tail = sb("c_tail", (P, NB * HIST), F32, scope)
                const_in = sem("c_const_in", scope)
                cleared = sem("c_cleared", scope)
                copied_in = sem("c_copied_in", scope)
                tail_ready = sem("c_tail_ready", scope)
                pooled_ready = sem("c_pooled_ready", scope)
                y_ready = sem("c_y_ready", scope)
                y_out = sem("c_y_out", scope)
                rows_out = sem("c_rows_out", scope)
                chain = sem("c_chain", scope)
                MISC = 5
                cols = ((0, 512), (512, 512), (1024, NS))

                def samples(x):
                    return x[:, EXT:EXT + NB * SEXT].rearrange("p (b t) -> p b t", t=SEXT)

                with nc.Block() as block:
                    @block.sync
                    def _(sp):
                        sp.dma_start(hist[:, :], A["state_pool"][0].rearrange("b r c -> (b r) c")).then_inc(const_in, 16)
                        sp.dma_start(count[:, :, :], A["c_count"]).then_inc(const_in, 16)
                        sp.dma_start(pw[:, :, :], A["pool_w"][0].rearrange("g c d -> c g d")).then_inc(const_in, 16)
                        for g in range(1, CG):
                            cv.load(sp, 2 * g, 0, col(w_in, COL_CU + g * P))
                            cv.load(sp, 2 * g + 1, 1, col(w_in, COL_CG + g * P))
                        for j in range(SLOTS):
                            cv.load(sp, 2 * CG + j, j, then[j])
                        cv.copied(sp, (CG - 1) * MISC, 4)
                        sp.dma_start(OUT["pool_p"][0, 0], last_p[:, :]).then_inc(rows_out, 16)
                        sp.dma_start(OUT["pool_s"][0].rearrange("b r c -> (b r) c"), last_s[:, :])\
                            .then_inc(rows_out, 16)
                        sp.wait_ge(rows_out, 32)

                    @block.gpsimd
                    def _(pool):
                        for g in range(1, CG + 1):
                            for j in range(2):
                                cv.split(pool, 2 * g + j, j, g, KO)

                    @block.tensor
                    def _(pe):
                        def mix(g):
                            pe.wait_ge(pooled_ready, g + 1)
                            for q, (t0, n) in enumerate(cols):
                                bank = cv.fill(pe, g * MISC, 1 + q)
                                pe.matmul(bank[:, 0:n], pw[:, g, :], pooled[:, t0:t0 + n], start=True, stop=True)\
                                    .then_inc(cv.misc_done, 1)

                        def last_rows(g):
                            bank = cv.fill(pe, g * MISC, 4)
                            pe.wait_ge(tail_ready, g + 1)
                            pe.transpose(bank[0:HIST, 0:P], ext[g % 2][:, EXT - HIST:EXT], ident[:, :])
                            pe.transpose(bank[0:NB * HIST, P:2 * P], tail[:, :], ident[:, :]).then_inc(cv.misc_done, 1)

                        for g in range(CG):
                            for c in range(NCH):
                                cv.project(pe, 2 * g, 0, c, KO, x_hi, x_lo)
                                if c == 0:
                                    pe.wait_ge(const_in, 48)
                                    bank = cv.fill(pe, g * MISC, 0)
                                    pe.transpose(bank[:, 0:NB * HIST], hist[:, g * P:(g + 1) * P],
                                                 ident[0:NB * HIST, 0:NB * HIST]).then_inc(cv.misc_done, 1)
                            for c in range(NCH):
                                cv.project(pe, 2 * g + 1, 1, c, KO, x_hi, x_lo)
                            mix(g)
                            last_rows(g)

                    @block.scalar
                    def _(act):
                        for g in range(CG):
                            x = ext[g % 2]
                            act.wait_ge(cleared, 1)
                            if g >= 2:
                                cv.copied(act, (g - 2) * MISC, 4)
                            for c, (t0, n) in enumerate(CHUNKS):
                                cv.projected(act, 2 * g, c)
                                if c < NCH - 1:
                                    act.activation(x[:, HIST + t0:HIST + t0 + n], psum[:, c, 0:n], ACT.Copy)\
                                        .then_inc(cv.bank_free, 1)
                                else:
                                    act.activation(x[:, HIST + t0:EXT], psum[:, c, 0:SEQ - t0], ACT.Copy)
                                    act.activation(samples(x)[:, :, HIST:SEXT],
                                                   psum[:, c, SEQ - t0:n].rearrange("p (b t) -> p b t", t=TB),
                                                   ACT.Copy).then_inc(cv.bank_free, 1)
                            if g > 0:
                                act.wait_ge(y_ready, g)
                            for c in range(NCH):
                                cv.empty(act, 2 * g + 1, c, gate, ACT.Sigmoid, raw=graw)
                            act.wait_ge(y_ready, g + 1)
                            act.dma_start(y_d[Y_C + g], yt[:, :]).then_inc(y_out, 16)
                        act.wait_ge(y_out, 16 * CG)

                    @block.vector
                    def _(dve):
                        ch = Chain(dve, chain)
                        cv.dve_start(dve)
                        dve.wait_ge(const_in, 48)
                        ch.step(dve.memset(ext[0][:, 0:HIST], 0.0))
                        ch.link(dve.memset(ext[1][:, 0:HIST], 0.0))
                        dve.sem_inc(cleared, 1)
                        for g, win in enumerate(WINDOWS):
                            x = ext[g % 2]
                            bank = cv.filled(dve, g * MISC, 0)
                            dve.tensor_copy(samples(x)[:, :, 0:HIST], bank[:, 0:NB * HIST]
                                            .rearrange("p (b t) -> p b t", t=HIST)).then_inc(cv.misc_free, 1)
                            cv.copied(dve, g * MISC, 0)
                            cv.emptied(dve, 2 * g)
                            ch.step(dve.tensor_copy(tail[:, :].rearrange("p (b t) -> p b t", t=HIST),
                                                    samples(x)[:, :, TB:SEXT]))
                            src, w, n = x, 1, 0
                            end = EXT + NB * SEXT
                            while w < win:
                                dst = acc[n % 2]
                                ch.link(dve.tensor_tensor(dst[:, 2 * w - 1:end], src[:, 2 * w - 1:end],
                                                          src[:, w - 1:end - w], ALU.add))
                                src, w, n = dst, 2 * w, n + 1
                            if n == 1:
                                ch.wait()
                            dve.sem_inc(tail_ready, 1)
                            ch.step(dve.scalar_tensor_tensor(out=pooled[:, 0:SEQ], in0=src[:, HIST:EXT], scalar=1.0 / win,
                                                             in1=x[:, HIST:EXT], op0=ALU.mult, op1=ALU.subtract))
                            ch.link(dve.scalar_tensor_tensor(
                                out=pooled[:, SEQ:NT].rearrange("p (b t) -> p b t", t=TB),
                                in0=samples(src)[:, :, HIST:SEXT], scalar=1.0 / win,
                                in1=samples(x)[:, :, HIST:SEXT], op0=ALU.mult, op1=ALU.subtract))
                            ch.link(dve.tensor_tensor(pooled[:, 0:HIST], src[:, HIST:2 * HIST], count[:, g, :], ALU.mult))
                            dve.tensor_tensor(pooled[:, 0:HIST], pooled[:, 0:HIST], x[:, HIST:2 * HIST],
                                              ALU.subtract).then_inc(pooled_ready, 1)
                            cv.emptied(dve, 2 * g + 1)
                            ch.link(dve.tensor_tensor(gate[:, :], gate[:, :], graw[:, :], ALU.mult))
                            if g > 0:
                                dve.wait_ge(y_out, 16 * g)
                            for q, (t0, n) in enumerate(cols):
                                bank = cv.filled(dve, g * MISC, 1 + q)
                                dve.scalar_tensor_tensor(out=yt[:, t0:t0 + n], in0=bank[:, 0:n],
                                                         scalar=p_scale[:, g:g + 1], in1=gate[:, t0:t0 + n],
                                                         op0=ALU.mult, op1=ALU.mult).then_inc(cv.misc_free, 1)
                            cv.copied(dve, g * MISC, 3)
                            dve.sem_inc(y_ready, 1)
                            bank = cv.filled(dve, g * MISC, 4)
                            ch.step(dve.tensor_copy(last_p[:, g * P:(g + 1) * P], bank[0:HIST, 0:P]))
                            dve.tensor_copy(last_s[:, g * P:(g + 1) * P], bank[0:NB * HIST, P:2 * P])\
                                .then_inc(cv.misc_free, 1)

        def output_phase():
            scope = ExitStack()
            with scope:
                cv = Conveyor("o", scope, (3, 4, 5), KO)
                xt = sb("o_x", (P, TILES + 1, D), F32, scope)
                rows = sb("o_rows", (P, TILES + 1, D), F32, scope)
                ot = [sb(f"o_feature{i}", (P, NT), F32, scope) for i in range(2)]
                stage = [sb(f"o_merged{i}", (P, NT), F32, scope) for i in range(2)] + ot
                NST = len(stage)
                g_post = sb("o_g_post", (P, D), F32, scope)
                sq = sb("o_squares", (P, TILES + 1, P), F32, scope)
                ssq_k = sb("o_ssq_by_tile", (P, TILES + 1, KO), F32, scope)
                ssq = sb("o_ssq", (P, TILES + 1), F32, scope)
                rs = sb("o_rs", (P, TILES + 1), F32, scope)
                m_in = [sem(f"o_merged_in{i}", scope) for i in range(NST)]
                x_in = sem("o_x_in", scope)
                g_in = sem("o_g_in", scope)
                mh_ready = sem("o_merged_hi_ready", scope)
                ml_ready = sem("o_merged_lo_ready", scope)
                sq_ready = sem("o_squares_ready", scope)
                sq_used = sem("o_squares_used", scope)
                ssq_ready = sem("o_ssq_ready", scope)
                rms_ready = sem("o_rms_ready", scope)
                out_ready = sem("o_out_ready", scope)
                stored = sem("o_stored", scope)
                chain = sem("o_chain", scope)
                spans = ((0, 4), (4, 4), (8, 1))
                QS = len(spans)
                LOOPS = KO // 2 - 1

                with nc.Block() as block:
                    @block.sync
                    def _(sp):
                        for k in range(KO):
                            if k >= NST:
                                sp.wait_ge(ml_ready, k - NST + 1)
                            sp.dma_start(stage[k % NST][:, :], merged_d[k]).then_inc(m_in[k % NST], 16)
                        sp.dma_start(g_post[:, :], A["norm_post"].broadcast_to([P, D])).then_inc(g_in, 16)
                        for k in range(SLOTS, 2 * SLOTS):
                            cv.load(sp, k, k % SLOTS, col(w_out, k * P))
                        sp.dma_start(xt[:, 0:TILES, :], A["x_prompt"][0].rearrange("(b p) d -> p b d", p=P)).then_inc(x_in, 16)
                        sp.dma_start(xt[0:NS, TILES, :], A["x_sample"].rearrange("b t d -> (b t) d")).then_inc(x_in, 16)
                        for k in range(2 * SLOTS, KO):
                            cv.load(sp, k, k % SLOTS, col(w_out, k * P))
                        for t in range(TILES + 1):
                            sp.wait_ge(out_ready, t + 1)
                            if t < TILES:
                                sp.dma_start(OUT["y_prompt"][0, t * P:(t + 1) * P, :], rows[:, t, :]).then_inc(stored, 16)
                            else:
                                sp.dma_start(OUT["y_sample"].rearrange("b t d -> (b t) d"), rows[0:NS, t, :])\
                                    .then_inc(stored, 16)
                        sp.wait_ge(stored, 16 * (TILES + 1))

                    @block.gpsimd
                    def _(pool):
                        for k in range(SLOTS, KO):
                            cv.split(pool, k, k % SLOTS, k // SLOTS, KO)

                    @block.tensor
                    def _(pe):
                        def back(u, j):
                            cv.emptied(pe, u)
                            for q, (b0, nb) in enumerate(spans):
                                bank = cv.fill(pe, u * QS, q, q == 2)
                                w = P if q < 2 else NS
                                for b in range(nb):
                                    mm = pe.transpose(bank[0:w, b * P:(b + 1) * P],
                                                      ot[j][:, (b0 + b) * P:(b0 + b) * P + w], ident[:, :])
                                mm.then_inc(cv.misc_done, 1)

                        def tile(u, j, back_at):
                            for c in range(NCH):
                                cv.project(pe, u, j, c, KO, x_hi, x_lo)
                                if c == back_at:
                                    back(u - 1, 1 - j)

                        for c in range(NCH):
                            cv.project(pe, 0, 0, c, KO, x_hi, x_lo, each=ml_ready if c == 0 else None)
                        with pe.Fori(0, LOOPS) as i:
                            tile(i * 2 + 1, 1, 0)
                            tile(i * 2 + 2, 0, 0)
                        tile(KO - 1, 1, 0)
                        back(KO - 1, 1)

                    @block.scalar
                    def _(act):
                        for k in range(KO):
                            act.wait_ge(m_in[k % NST], 16 * (k // NST + 1))
                            act.activation(x_hi[:, k, :], stage[k % NST][:, :], ACT.Copy).then_inc(mh_ready, 1)

                        def squares(u):
                            act.wait_ge(sq_used, u + 1)
                            for q, (b0, nb) in enumerate(spans):
                                w = P if q < 2 else NS
                                act.wait_ge(cv.misc_done, u * QS + q + 1)
                                act.activation(sq[0:w, b0:b0 + nb, :],
                                               cv.bank(0, q)[0:w, 0:nb * P].rearrange("p (a b) -> p a b", b=P),
                                               ACT.Square).then_inc(sq_ready, 1)

                        act.wait_ge(ml_ready, KO)
                        for c in range(NCH):
                            cv.empty(act, 0, c, ot[0], ACT.Copy)

                        def tile(u, j):
                            cv.empty(act, u, 0, ot[j], ACT.Copy)
                            squares(u - 1)
                            for c in range(1, NCH):
                                cv.empty(act, u, c, ot[j], ACT.Copy)

                        with act.Fori(0, LOOPS) as i:
                            tile(i * 2 + 1, 1)
                            tile(i * 2 + 2, 0)
                        tile(KO - 1, 1)
                        squares(KO - 1)
                        act.wait_ge(ssq_ready, 1)
                        act.activation(rs[:, :], ssq[:, :], ACT.Sqrt, bias=eps[:, :], scale=1.0 / D)\
                            .then_inc(rms_ready, 1)

                    @block.vector
                    def _(dve):
                        ch = Chain(dve, chain)
                        cv.dve_start(dve)
                        dve.memset(sq[:, :, :], 1.0).then_inc(sq_used, 1)
                        for k in range(KO):
                            dve.wait_ge(mh_ready, k + 1)
                            dve.tensor_tensor(x_lo[:, k, :], stage[k % NST][:, :], x_hi[:, k, :].bitcast(F32),
                                              ALU.subtract).then_inc(ml_ready, 1)
                        dve.wait_ge(g_in, 16)
                        with dve.Fori(0, KO) as u:
                            for q, (b0, nb) in enumerate(spans):
                                dve.wait_ge(sq_ready, u * QS + q + 1)
                                bank = cv.filled(dve, u * QS, q)
                                w = P if q < 2 else NS
                                dve.tensor_tensor(rows[0:w, b0:b0 + nb, bass.ds(u * P, P)],
                                                  bank[0:w, 0:nb * P].rearrange("p (a b) -> p a b", b=P),
                                                  g_post[0:w, bass.ds(u * P, P)].unsqueeze(1).broadcast_to([w, nb, P]),
                                                  ALU.mult).then_inc(cv.misc_free, 1)
                            dve.tensor_reduce(ssq_k[:, :, bass.ds(u, 1)].rearrange("p t o -> p (t o)"), sq[:, :, :],
                                              AX.X, ALU.add).then_inc(sq_used, 1)
                        dve.wait_ge(sq_used, KO + 1)
                        dve.tensor_reduce(ssq[:, :], ssq_k[:, :, :], AX.X, ALU.add).then_inc(ssq_ready, 1)
                        dve.wait_ge(rms_ready, 1)
                        ch.link(dve.reciprocal(rs[:, :], rs[:, :]))
                        dve.wait_ge(x_in, 32)
                        cv.copied(dve, KO * QS, -1)
                        for t in range(TILES + 1):
                            n = P if t < TILES else NS
                            dve.scalar_tensor_tensor(out=rows[0:n, t, :], in0=rows[0:n, t, :],
                                                     scalar=rs[0:n, t:t + 1], in1=xt[0:n, t, :],
                                                     op0=ALU.mult, op1=ALU.add).then_inc(out_ready, 1)

        def first_of(base):
            return [col(w_in, at) for at in base]

        merge_b = ((0, BH, w_br["b"], COL_MG + D),)
        merge_ac = ((0, AH, w_br["a"], COL_MG), (AH, CG, w_br["c"], COL_MG + 2 * D))

        def first_pair(pairs):
            _, _, w, gate = pairs[0]
            return [col(w_in, gate), col(w, 0)]

        norm_phase(first_of((COL_BF, COL_BQ)))
        hgrn_phase(first_of((COL_AQ, COL_AK)))
        attention_phase(first_of((COL_CU, COL_CG)))
        pool_phase(first_pair(merge_b))
        fresh_semaphores()
        merge_phase("mb", 0, merge_b, True, first_pair(merge_ac))
        merge_phase("mac", Y_A, merge_ac, False, [col(w_out, 0), col(w_out, P)])
        output_phase()
        lot[0].close()


_INS = ["x_prompt", "x_sample", "cache_kv_w128", "cache_kv_w512", "cache_kv_w2048", "state_hgrn",
        "state_pool", "norm_pre", "norm_post", "w_in", "hgrn_lb_logits", "hgrn_norm", "pool_w",
        "pool_scale", "w_br_a", "w_br_b", "w_br_c", "w_out"]
_OUTS = [("y_prompt", (1, 1024, 1024)), ("y_sample", (8, 8, 1024)),
         ("kv128_p", (1, 1, 128, 2, 4, 128)), ("kv512_p", (1, 1, 512, 2, 4, 128)),
         ("kv2048_p", (1, 1, 1024, 2, 4, 128)), ("kv128_s", (1, 8, 8, 2, 4, 128)),
         ("kv512_s", (1, 8, 8, 2, 4, 128)), ("kv2048_s", (1, 8, 8, 2, 4, 128)),
         ("hgrn_p", (1, 1, 8, 128, 128)), ("hgrn_s", (1, 8, 8, 128, 128)),
         ("pool_p", (1, 1, 15, 512)), ("pool_s", (1, 8, 15, 512))]


def kernel(**inputs):
    import numpy as np
    import concourse.bacc as bacc
    from concourse.bass_utils import run_bass_kernel_spmd

    nc = bacc.Bacc("TRN2", target_bir_lowering=False, num_devices=1)
    arrays, ins, outs = {}, {}, {}
    for name in _INS:
        a = np.ascontiguousarray(inputs[name])
        arrays["in_" + name] = a
        ins[name] = nc.dram_tensor("in_" + name, a.shape, mybir.dt.from_np(a.dtype), kind="ExternalInput").ap()
    for name, a in constants(np).items():
        arrays["const_" + name] = a
        ins["c_" + name] = nc.dram_tensor("const_" + name, a.shape, mybir.dt.from_np(a.dtype),
                                          kind="ExternalInput").ap()
    for name, shape in _OUTS:
        outs[name] = nc.dram_tensor("out_" + name, shape, F32, kind="ExternalOutput").ap()
    build(nc, ins, outs)
    r = run_bass_kernel_spmd(nc, [arrays], core_ids=[0])
    return tuple(r.results[0]["out_" + name] for name, _ in _OUTS)
```

```python
import concourse.bass as bass
from concourse import mybir
from contextlib import ExitStack

F32 = mybir.dt.float32
F32R = mybir.dt.float32r
I32 = mybir.dt.int32
ALU = mybir.AluOpType
ACT = mybir.ActivationFunctionType
AX = mybir.AxisListType

D = 1024
P = 128
KO = D // P
SEQ = 1024
NB, TB = 8, 8
NS = NB * TB
NT = SEQ + NS
TILES = SEQ // P
EPS = 1e-6
NEG = -1e30
SCALE = P ** -0.5
AH, BH, CG, AG = 4, 8, 4, 3
GROUP = AH * P
HIST = 15
WINDOWS = (2, 4, 8, 16)
COL_AQ, COL_AK, COL_AV, COL_AG = 0, 3 * GROUP, 6 * GROUP, 9 * GROUP
COL_BQ = COL_AG + GROUP
COL_BF, COL_BI, COL_BG = COL_BQ + D, COL_BQ + 2 * D, COL_BQ + 3 * D
COL_CU = COL_BG + D
COL_CG = COL_CU + GROUP
COL_MG = COL_CG + GROUP

CHUNKS = ((0, 384), (384, 384), (768, NT - 768))
NCH = len(CHUNKS)
SLOTS = 2
Y_A, Y_C = BH, BH + AH
LEVELS = 8


def constants(np):
    i = np.arange(P)
    c = {}
    c["ident"] = np.eye(P, dtype=np.float32)
    band = np.zeros((P, 2 * P), np.float32)
    band[:, :P] = np.where(i[None, :] >= i[:, None], 0.0, NEG)
    band[:, P:] = np.where(i[None, :] <= i[:, None], 0.0, NEG)
    c["band"] = band
    gap = i[:, None] - i[None, :]
    c["pair"] = np.where((gap >= 0) & (gap % 2 == 0), 0.0, NEG).astype(np.float32)
    lev = np.zeros((P, LEVELS, P), np.int32)
    s, t = i[:, None], i[None, :]
    for n in range(1, LEVELS):
        h = n - 1
        lev[:, n, :] = ((s >> n) == (t >> n)) & (((s >> h) & 1) == 0) & (((t >> h) & 1) == 1)
    c["level"] = lev
    j = np.arange(NS)
    c["own_row"] = ((j[:, None] // TB) == np.arange(NB)[None, :]).astype(np.float32)
    c["own_col"] = np.broadcast_to((np.arange(NB)[:, None] == (j[None, :] // TB)).astype(np.float32),
                                   (P, NB, NS)).copy()
    tq = (j % TB)[:, None]
    m = np.full((NS, 4 * P + 3 * NS), NEG, np.float32)
    m[:, 0:P] = np.where(i[None, :] >= tq, 0.0, NEG)
    for blk in range(2):
        key = P * blk + i[None, :]
        m[:, (1 + blk) * P:(2 + blk) * P] = np.where((256 + tq - key) % 4 == 0, 0.0, NEG)
    key = 16 * (i[None, :] // 8) + i[None, :] % 8
    m[:, 3 * P:4 * P] = np.where((256 + tq - key) % 16 == 0, 0.0, NEG)
    for g, dil in enumerate((1, 4, 16)):
        gap = tq - (j % TB)[None, :]
        ok = ((j[:, None] // TB) == (j[None, :] // TB)) & (gap >= 0) & (gap % dil == 0)
        m[:, 4 * P + g * NS:4 * P + (g + 1) * NS] = np.where(ok, 0.0, NEG)
    c["sample_mask"] = m
    rc = np.zeros((P, CG, HIST), np.float32)
    for g, w in enumerate(WINDOWS):
        rc[:, g, :] = 1.0 / np.minimum(np.arange(HIST) + 1, w)
    c["count"] = rc
    return c


def build(nc, A, OUT):
    ctx = ExitStack()
    with ctx:
        def sb(name, shape, dt=F32, scope=ctx):
            return scope.enter_context(nc.sbuf_tensor(name, list(shape), dt))

        def sem(name, scope):
            h = lot[0].enter_context(nc.semaphore(name))
            taken.append(h.num)
            return h

        lot, taken = [ExitStack()], []

        def fresh_semaphores():
            nums = sorted(taken)
            runs = [[nums[0], nums[0] + 1]]
            for n in nums[1:]:
                if n == runs[-1][1]:
                    runs[-1][1] = n + 1
                else:
                    runs.append([n, n + 1])
            with nc.Block() as block:
                @block.gpsimd
                def _(pool):
                    for a, b in runs:
                        pool.sem_clear(range(a, b))
            lot[0].close()
            lot[0] = ExitStack()
            taken.clear()

        merged_d = nc.dram_tensor("merged_rows", (KO, P, NT), F32, kind="Internal").ap()
        y_d = nc.dram_tensor("branch_outputs", (2 * KO, P, NT), F32, kind="Internal").ap()
        stat_d = nc.dram_tensor("stat_rows", (AH, SEQ, 2, 2), F32, kind="Internal").ap()
        weight_d = nc.dram_tensor("group_weights", (AH, SEQ, 2), F32, kind="Internal").ap()

        psum = ctx.enter_context(nc.psum_tensor("psum", [P, 8, 512], F32))

        ident = sb("ident", (P, P))
        band = sb("band", (P, 2 * P))
        pair = sb("pair", (P, P))
        lb = sb("lb", (P, BH))
        one_lb = sb("one_lb", (P, BH))
        h_norm = sb("h_norm", (P, 1))
        p_scale = sb("p_scale", (P, CG))
        eps = sb("eps", (P, 1))
        w_raw = sb("w_raw", (P, SLOTS, KO, P))
        w_hi = sb("w_hi", (P, SLOTS, KO, P), F32R)
        w_lo = sb("w_lo", (P, SLOTS, KO, P), F32R)
        x_hi = sb("x_hi", (P, KO, NT), F32R)
        x_lo = sb("x_lo", (P, KO, NT), F32R)

        w_in = A["w_in"][0].rearrange("(ko p) n -> p ko n", p=P)
        w_out = A["w_out"][0].rearrange("(ko p) n -> p ko n", p=P)
        w_br = {k: A["w_br_" + k][0].rearrange("(ko p) n -> p ko n", p=P) for k in "abc"}

        def col(w, at):
            return w[:, :, bass.ds(at, P)]

        def nc_sem(name):
            return ctx.enter_context(nc.semaphore(name))

        class Conveyor:

            loaded = [nc_sem(f"w_loaded{s}") for s in range(SLOTS)]
            hi_ready, split_done = nc_sem("w_hi_ready"), nc_sem("w_split_done")
            proj_done, bank_free = nc_sem("proj_done"), nc_sem("bank_free")
            before = 0

            def __init__(self, tag, scope, misc_banks, units):
                assert units % SLOTS == 0
                self.u0 = Conveyor.before
                Conveyor.before += units
                self.misc_done = sem(f"{tag}_misc_done", scope)
                self.misc_free = sem(f"{tag}_misc_free", scope)
                self.held_pe = sem(f"{tag}_held_pe", scope)
                self.held_pool = sem(f"{tag}_held_pool", scope)
                self.held_sp = sem(f"{tag}_held_sp", scope)
                self.held_dve = sem(f"{tag}_held_dve", scope)
                self.banks = misc_banks
                self.ring = len(misc_banks)

            def load(self, sp, u, s, src):
                sp.wait_ge(self.split_done, u + (self.u0 + 1))
                sp.sem_inc(self.held_sp, 1)
                sp.dma_start(w_raw[:, s, 0:src.shape[1], :], src).then_inc(self.loaded[s], 16)

            def split(self, pool, u, s, turn, nko):
                pool.wait_ge(self.loaded[s], turn * 16 + (16 + 16 // SLOTS * self.u0))
                pool.wait_ge(self.proj_done, u * NCH + (NCH + NCH * self.u0))
                pool.sem_inc(self.held_pool, 1)
                pool.tensor_copy(w_hi[:, s, 0:nko, :], w_raw[:, s, 0:nko, :]).then_inc(self.hi_ready, 1)
                pool.wait_ge(self.hi_ready, u + (1 + self.u0))
                pool.tensor_tensor(w_lo[:, s, 0:nko, :], w_raw[:, s, 0:nko, :],
                                   w_hi[:, s, 0:nko, :].bitcast(F32), ALU.subtract)\
                    .then_inc(self.split_done, 1)

            def project(self, pe, u, s, c, nko, hi, lo, each=None, k0=0, half=None):
                t0, n = CHUNKS[c]
                steps = [(w_hi, x, k) for k in range(nko) for x in (hi, lo)] + [(w_lo, hi, k) for k in range(nko)]
                first, last = steps[0], steps[-1]
                if half is not None:
                    m = len(steps) // 2
                    steps = steps[m * half:m * (half + 1)]
                if half != 1:
                    if c == 0:
                        pe.wait_ge(self.hi_ready, u + (1 + self.u0))
                    pe.wait_ge(self.bank_free, u * NCH + (c + 1 + NCH * self.u0))
                for step in steps:
                    w, x, k = step
                    if w is w_hi and x is hi and each is not None:
                        pe.wait_ge(each, k0 + k + 1)
                    if w is w_lo and k == 0 and c == 0:
                        pe.wait_ge(self.split_done, u + (1 + SLOTS + self.u0))
                    mm = pe.matmul(psum[:, c, 0:n], w[:, s, k, :], x[:, k, t0:t0 + n],
                                   start=step is first, stop=step is last)
                if half != 0:
                    mm.then_inc(self.proj_done, 1)

            def projected(self, act, u, c):
                act.wait_ge(self.proj_done, u * NCH + (c + 1 + SLOTS * NCH + NCH * self.u0))

            def empty(self, act, u, c, dst, func, raw=None):
                t0, n = CHUNKS[c]
                self.projected(act, u, c)
                if raw is not None:
                    act.activation(raw[:, t0:t0 + n], psum[:, c, 0:n], ACT.Copy)
                act.activation(dst[:, t0:t0 + n], psum[:, c, 0:n], func).then_inc(self.bank_free, 1)

            def emptied(self, eng, u, c=NCH - 1):
                eng.wait_ge(self.bank_free, u * NCH + (c + 1 + NCH + NCH * self.u0))

            def dve_start(self, dve):
                dve.sem_inc(self.misc_free, self.ring)

            def bank(self, at, m):
                return psum[:, self.banks[(m + (at if isinstance(at, int) else 0)) % self.ring], :]

            def fill(self, pe, at, m, part=False):
                pe.wait_ge(self.misc_free, at + m + 1)
                if part:
                    pe.sem_inc(self.held_pe, 1)
                return self.bank(at, m)

            def filled(self, dve, at, m, part=False):
                dve.wait_ge(self.misc_done, at + m + 1)
                if part:
                    dve.sem_inc(self.held_dve, 1)
                return self.bank(at, m)

            def copied(self, eng, at, m):
                eng.wait_ge(self.misc_free, at + m + 1 + self.ring)

        class Chain:

            def __init__(self, eng, s):
                self.eng, self.sem, self.n, self.at = eng, s, 0, 0

            def loop(self, at, n):
                self.at, self.start, self.per = at, self.n, n

            def end(self, turns):
                assert self.n - self.start == self.per, ("steps in the body", self.n - self.start)
                self.n, self.at = self.start + turns * self.per, 0

            def step(self, ins):
                ins.then_inc(self.sem, 1)
                self.n += 1
                return ins

            def wait(self):
                self.eng.wait_ge(self.sem, self.at + self.n)

            def link(self, ins):
                self.step(ins)
                self.wait()

        EXT = HIST + SEQ
        SEXT = HIST + TB

        def samples(x):
            return x[:, EXT:EXT + NB * SEXT].rearrange("p (b t) -> p b t", t=SEXT)

        def empty_ext(cv, act, u, c, x):
            t0, n = CHUNKS[c]
            cv.projected(act, u, c)
            if c < NCH - 1:
                act.activation(x[:, HIST + t0:HIST + t0 + n], psum[:, c, 0:n], ACT.Copy).then_inc(cv.bank_free, 1)
            else:
                act.activation(x[:, HIST + t0:EXT], psum[:, c, 0:SEQ - t0], ACT.Copy)
                act.activation(samples(x)[:, :, HIST:SEXT],
                               psum[:, c, SEQ - t0:n].rearrange("p (b t) -> p b t", t=TB),
                               ACT.Copy).then_inc(cv.bank_free, 1)

        def norm_phase(then):
            scope = ExitStack()
            with scope:
                xt = sb("xt", (P, TILES + 1, D), F32, scope)
                g_pre = sb("g_pre", (P, D), F32, scope)
                junk = sb("junk", (P, D), F32, scope)
                ssq = sb("ssq", (P, TILES + 1), F32, scope)
                rs = sb("rs", (P, TILES + 1), F32, scope)
                lg = sb("lg", (P, BH), F32, scope)
                ex = sb("ex", (P, BH), F32, scope)
                x_in = [sem(f"x_in{i}", scope) for i in range(TILES + 1)]
                g_in = sem("g_in", scope)
                ident_in = sem("ident_in", scope)
                const_in = sem("const_in", scope)
                lb_in = sem("lb_in", scope)
                eps_ready = sem("eps_ready", scope)
                squared = sem("squared", scope)
                rms_ready = sem("rms_ready", scope)
                xn_ready = sem("xn_ready", scope)
                xt_done = sem("transposed", scope)
                xh_ready = sem("xh_ready", scope)
                banks_free = sem("banks_free", scope)
                lg_ready = sem("lg_ready", scope)
                exp_ready = sem("exp_ready", scope)
                chain = sem("norm_chain", scope)
                RING = 5
                N_CONST = 4
                LAG = 2
                HALF = KO // 2
                cv = Conveyor("n", scope, (3,), 0)

                def rows(t):
                    return P if t < TILES else NS

                with nc.Block() as block:
                    @block.sync
                    def _(sp):
                        for t in range(TILES):
                            sp.dma_start(xt[:, t, :], A["x_prompt"][0, t * P:(t + 1) * P, :]).then_inc(x_in[t], 16)
                            if t == 0:
                                sp.dma_start(g_pre[:, :], A["norm_pre"].broadcast_to([P, D])).then_inc(g_in, 16)
                                sp.dma_start(ident[:, :], A["c_ident"]).then_inc(ident_in, 16)
                            if t == 2:
                                cv.load(sp, 0, 0, then[0])
                        sp.dma_start(xt[0:NS, TILES, :], A["x_sample"].rearrange("b t d -> (b t) d"))\
                            .then_inc(x_in[TILES], 16)
                        cv.load(sp, 1, 1, then[1])
                        for dst, src in ((band[:, :], A["c_band"]), (pair[:, :], A["c_pair"]),
                                         (h_norm[:, :], A["hgrn_norm"].rearrange("a p -> p a")),
                                         (p_scale[:, :], A["pool_scale"][0].rearrange("(g p) -> p g", p=P))):
                            sp.dma_start(dst, src, allow_slow_non_contiguous=True).then_inc(const_in, 16)
                        sp.dma_start(lg[:, :], A["hgrn_lb_logits"][0].rearrange("(h p) -> p h", p=P),
                                     allow_slow_non_contiguous=True).then_inc(lb_in, 16)
                        sp.wait_ge(const_in, 16 * N_CONST)

                    @block.gpsimd
                    def _(pool):
                        pool.sem_inc(Conveyor.split_done, SLOTS)
                        for j in range(SLOTS):
                            cv.split(pool, j, j, 0, KO)

                    @block.scalar
                    def _(act):
                        act.sem_inc(Conveyor.bank_free, NCH)
                        act.wait_ge(eps_ready, 1)
                        for i in range(TILES + 1 + LAG):
                            if i <= TILES:
                                n = rows(i)
                                act.wait_ge(x_in[i], 16)
                                if i > 0:
                                    act.wait_ge(squared, i)
                                act.activation(junk[0:n, :], xt[0:n, i, :], ACT.Square,
                                               accum_out=ssq[0:n, i:i + 1]).then_inc(squared, 1)
                                act.wait_ge(squared, i + 1)
                                act.activation(rs[0:n, i:i + 1], ssq[0:n, i:i + 1], ACT.Sqrt, bias=eps[0:n, :],
                                               scale=1.0 / D).then_inc(rms_ready, 1)
                            t = i - LAG
                            for m in (2 * t, 2 * t + 1) if t >= 0 else ():
                                k0, n = m % 2 * HALF, rows(t)
                                act.wait_ge(xt_done, m + 1)
                                act.activation(x_hi[:, k0:k0 + HALF, t * P:t * P + n],
                                               psum[:, 3 + m % RING, 0:HALF * n].rearrange("p (k t) -> p k t", t=n),
                                               ACT.Copy).then_inc(xh_ready, 1)
                        act.wait_ge(lg_ready, 1)
                        act.activation(ex[:, :], lg[:, :], ACT.Exp).then_inc(exp_ready, 1)

                    @block.vector
                    def _(dve):
                        ch = Chain(dve, chain)
                        dve.memset(eps[:, :], EPS).then_inc(eps_ready, 1)
                        dve.wait_ge(g_in, 16)
                        for i in range(TILES + 1 + LAG):
                            if i <= TILES:
                                n = rows(i)
                                dve.wait_ge(rms_ready, i + 1)
                                ch.link(dve.reciprocal(rs[0:n, i:i + 1], rs[0:n, i:i + 1]))
                                dve.scalar_tensor_tensor(out=xt[0:n, i, :], in0=xt[0:n, i, :],
                                                         scalar=rs[0:n, i:i + 1], in1=g_pre[0:n, :],
                                                         op0=ALU.mult, op1=ALU.mult).then_inc(xn_ready, 1)
                            t = i - LAG
                            for m in (2 * t, 2 * t + 1) if t >= 0 else ():
                                k0, n = m % 2 * HALF, rows(t)
                                xs = slice(t * P, t * P + n)
                                dve.wait_ge(xh_ready, m + 1)
                                dve.tensor_tensor(x_lo[:, k0:k0 + HALF, xs],
                                                  psum[:, 3 + m % RING, 0:HALF * n].rearrange("p (k t) -> p k t", t=n),
                                                  x_hi[:, k0:k0 + HALF, xs].bitcast(F32), ALU.subtract)\
                                    .then_inc(banks_free, 1)
                        dve.wait_ge(lb_in, 16)
                        dve.tensor_tensor(lg[:, :], lg[:, :], lg[:, :], ALU.subtract).then_inc(lg_ready, 1)
                        dve.wait_ge(exp_ready, 1)
                        ch.link(dve.reciprocal(lg[:, :], ex[:, :]))
                        ch.link(dve.tensor_tensor(ex[:, :], ex[:, :], lg[:, :], ALU.mult))
                        ch.link(dve.tensor_tensor(lb[:, :], ex[:, :], ex[:, :], ALU.subtract))
                        ch.link(dve.tensor_scalar(one_lb[:, :], lb[:, :], -1.0, 1.0, ALU.mult, ALU.add))

                    @block.tensor
                    def _(pe):
                        pe.sem_inc(Conveyor.proj_done, SLOTS * NCH)
                        pe.wait_ge(ident_in, 16)
                        for t in range(TILES + 1):
                            n = rows(t)
                            pe.wait_ge(xn_ready, t + 1)
                            for m in (2 * t, 2 * t + 1):
                                if m >= RING:
                                    pe.wait_ge(banks_free, m - RING + 1)
                                for b in range(HALF):
                                    k = m % 2 * HALF + b
                                    mm = pe.transpose(psum[:, 3 + m % RING, b * n:b * n + n],
                                                      xt[0:n, t, k * P:(k + 1) * P], ident[0:n, 0:n])
                                mm.then_inc(xt_done, 1)
                            if t % 3 == 2 and t > 2:
                                pe.wait_ge(banks_free, 2 * (t - 2))
                                cv.project(pe, 0, 0, t // 3 - 1, KO, x_hi, x_lo)
                        pe.wait_ge(banks_free, 2 * (TILES + 1))
                        cv.project(pe, 0, 0, NCH - 1, KO, x_hi, x_lo)

        def prefetch(sp, dsts, srcs, done):
            for dst, src in zip(dsts, srcs):
                sp.dma_start(dst[:, :], src).then_inc(done, 16)

        def merge_phase(tag, y0, pairs, fresh, bufs, gt, here, ahead, then):
            N_PAIR = 2
            OUTER = 2 if fresh else 1
            LOOPS = KO // OUTER
            UNITS = 2 * N_PAIR
            scope = ExitStack()
            with scope:
                cv = Conveyor(tag, scope, (3,), LOOPS * UNITS)
                y_hi = sb(f"{tag}_y_hi", (P, KO, NT), F32R, scope)
                y_lo = sb(f"{tag}_y_lo", (P, KO, NT), F32R, scope)
                mt, pb, stage = bufs[-3], bufs[-2:], bufs
                NST = len(stage)
                y_in = [sem(f"{tag}_y_in{i}", scope) for i in range(NST)]
                yh_ready = sem(f"{tag}_yh_ready", scope)
                yl_ready = sem(f"{tag}_yl_ready", scope)
                rows_in = sem(f"{tag}_rows_in", scope)
                gated = sem(f"{tag}_gated", scope)
                rows_out = [sem(f"{tag}_rows_out{i}", scope) for i in range(2)]
                chain = sem(f"{tag}_chain", scope)
                ahead_in = sem(f"{tag}_ahead_in", scope)

                def pair(p):
                    return pairs[p % len(pairs)]

                def product(i, p):
                    return i * UNITS + (2 * p + 2)

                def gate_ahead(i, p):
                    return i * UNITS + (2 * p + 3)

                LAST = (LOOPS * UNITS - 2, LOOPS * UNITS - 1)

                def steps(eng, turn, last):
                    with eng.Fori(0, LOOPS - 1) as i:
                        turn(i)
                    last()

                with nc.Block() as block:
                    @block.sync
                    def _(sp):
                        def at(i, p):
                            return i * (OUTER * P) + (p * P if fresh else 0)

                        def load_rows(i):
                            if not fresh:
                                sp.wait_ge(gated, i * N_PAIR + 1)
                                sp.sem_inc(cv.held_sp, 1)
                                sp.dma_start(mt[:, :], merged_d[bass.ds(i, 1), :, :]
                                             .rearrange("o p t -> p (o t)")).then_inc(rows_in, 16)

                        def load_gate_ahead(i, p):
                            cv.load(sp, gate_ahead(i, p), 1, col(w_in, at(i, p) + (OUTER * P + pair(p)[3])))

                        def rest_of_turn(i):
                            cv.load(sp, product(i, 1), 0, col(pair(1)[2], at(i, 1)))
                            load_rows(i + 1)
                            load_gate_ahead(i, 1)
                            cv.load(sp, product(i + 1, 0), 0, col(pair(0)[2], at(i + 1, 0)))

                        def last():
                            cv.load(sp, LAST[1], 1, col(pair(1)[2], at(LOOPS - 1, 1)))
                            if not fresh:
                                sp.wait_ge(rows_out[1], 16 * (LOOPS - 1) + 16)
                                prefetch(sp, *ahead, ahead_in)
                            for j in range(SLOTS):
                                cv.load(sp, LOOPS * UNITS + j, j, then[j])

                        cv.load(sp, product(0, 0), 0, col(pair(0)[2], 0))
                        for k in range(here, KO):
                            if k >= NST:
                                sp.wait_ge(yl_ready, k - NST + 1)
                            sp.dma_start(stage[k % NST][:, :], y_d[y0 + k]).then_inc(y_in[k % NST], 16)
                        load_gate_ahead(0, 0)
                        sp.wait_ge(yl_ready, KO)
                        load_rows(0)
                        if fresh:
                            prefetch(sp, *ahead, ahead_in)
                        rest_of_turn(0)
                        with sp.Fori(1, LOOPS - 1) as i:
                            load_gate_ahead(i, 0)
                            rest_of_turn(i)
                        last()
                        sp.wait_ge(ahead_in, 16 * len(ahead[0]))

                    @block.gpsimd
                    def _(pool):
                        def turn(i):
                            for p in range(N_PAIR):
                                cv.split(pool, product(i, p), 0, i * N_PAIR + (p + 1), pair(p)[1])
                                cv.split(pool, gate_ahead(i, p), 1, i * N_PAIR + (p + 1), KO)

                        def last():
                            for p in range(N_PAIR):
                                cv.split(pool, LAST[p], p, LAST[p] // 2, pair(p)[1])
                            for u in (LOOPS * UNITS, LOOPS * UNITS + 1):
                                cv.split(pool, u, u % 2, u // 2, KO)

                        steps(pool, turn, last)

                    @block.tensor
                    def _(pe):
                        def gate(u, s):
                            for c in range(NCH):
                                cv.project(pe, u, s, c, KO, x_hi, x_lo)

                        def multiply(u, s, p):
                            k0, n, _, _ = pair(p)
                            for c in range(NCH):
                                cv.project(pe, u, s, c, n, y_hi[:, k0:k0 + n, :], y_lo[:, k0:k0 + n, :],
                                           each=yl_ready if c == 0 else None, k0=k0)

                        def turn(i):
                            for p in range(N_PAIR):
                                multiply(product(i, p), 0, p)
                                gate(gate_ahead(i, p), 1)

                        def last():
                            for p in range(N_PAIR):
                                multiply(LAST[p], p, p)
                            if fresh:
                                gate(LOOPS * UNITS, 0)

                        gate(1, 1)
                        steps(pe, turn, last)

                    @block.scalar
                    def _(act):
                        def gate(u, p, chunks=range(NCH)):
                            for c in chunks:
                                cv.empty(act, u, c, gt[p], ACT.Sigmoid)

                        def split_y(k):
                            if k >= here:
                                act.wait_ge(y_in[k % NST], 16 * (k // NST + (0 if k % NST < here else 1)))
                            act.activation(y_hi[:, k, :], stage[k % NST][:, :], ACT.Copy).then_inc(yh_ready, 1)

                        def multiply(i, u, p, store=True):
                            if fresh or p == 1:
                                act.wait_ge(rows_out[p], i * 16 + 16)
                            else:
                                act.wait_ge(gated, i * N_PAIR + 2)
                            for c in range(NCH):
                                cv.empty(act, u, c, pb[p], ACT.Copy)
                            act.wait_ge(gated, i * N_PAIR + p + 3)
                            if (fresh or p == 1) and store:
                                tile = i * 2 + p if fresh else i
                                act.dma_start(merged_d[bass.ds(tile, 1), :, :]
                                              .rearrange("o p t -> p (o t)"), pb[p][:, :])\
                                    .then_inc(rows_out[p], 16)

                        def turn(i):
                            for p in range(N_PAIR):
                                multiply(i, product(i, p), p)
                                gate(gate_ahead(i, p), p)

                        def last():
                            for p in range(N_PAIR):
                                multiply(LOOPS - 1, LAST[p], p, store=fresh)

                        for j in range(2):
                            act.sem_inc(rows_out[j], 16)
                        act.sem_inc(gated, 2)
                        gate(0, 0)
                        for k in range(KO):
                            split_y(k)
                            if k >= 4 and k < 4 + NCH:
                                gate(1, 1, (k - 4,))
                        act.wait_ge(yl_ready, KO)
                        steps(act, turn, last)
                        for j in range(2) if fresh else (1,):
                            act.wait_ge(rows_out[j], 16 * LOOPS + (16 if fresh else 0))

                    @block.vector
                    def _(dve):
                        ch = Chain(dve, chain)
                        per = 0 if fresh else N_PAIR

                        def combine(i, u, p):
                            cv.emptied(dve, u)
                            ins = dve.tensor_tensor(pb[p][:, :], pb[p][:, :], gt[p][:, :], ALU.mult)
                            if fresh:
                                ins.then_inc(gated, 1)
                                return
                            ch.link(ins)
                            if p == 0:
                                dve.wait_ge(rows_in, i * 16 + 16)
                            else:
                                dve.wait_ge(gated, i * N_PAIR + 3)
                            dve.tensor_tensor(pb[p][:, :], pb[p][:, :], mt[:, :] if p == 0 else pb[0][:, :],
                                              ALU.add).then_inc(gated, 1)

                        def turn(i):
                            ch.loop(i * per, per)
                            for p in range(N_PAIR):
                                combine(i, product(i, p), p)
                            ch.end(LOOPS - 1)

                        def last():
                            for p in range(N_PAIR):
                                combine(LOOPS - 1, LAST[p], p)

                        for k in range(KO):
                            dve.wait_ge(yh_ready, k + 1)
                            dve.tensor_tensor(y_lo[:, k, :], stage[k % NST][:, :], y_hi[:, k, :].bitcast(F32),
                                              ALU.subtract).then_inc(yl_ready, 1)
                        steps(dve, turn, last)

        def hgrn_phase(ext, p_gate, p_graw, then):
            tag = "b"
            UNITS = 4
            POOL_AT = (COL_CU, COL_CG, COL_CU + P, COL_CU + 2 * P)
            scope = ExitStack()
            with scope:
                cv = Conveyor(tag, scope, (3, 4, 5, 6, 7), BH * UNITS + len(POOL_AT))
                q_new = sb("b_q_new", (P, NT), F32, scope)
                f_new = sb("b_forget_new", (P, NT), F32, scope)
                v_new = sb("b_v_new", (P, NT), F32, scope)
                g_new = sb("b_gate_new", (P, NT), F32, scope)
                g_raw = sb("b_gate_raw", (P, NT), F32, scope)
                qp = sb("b_q_decayed", (P, NT), F32, scope)
                kr = sb("b_k_decayed", (P, NT), F32, scope)
                ff = sb("b_forget", (P, NT), F32, scope)
                gate = sb("b_gate", (P, NT), F32, scope)
                ft_n = [NT >> n if n <= 3 else SEQ >> n for n in range(LEVELS)]
                ft_at = [0] + [sum(ft_n[1:n]) for n in range(1, LEVELS + 1)]
                fts = sb("b_block_decay", (P, ft_at[LEVELS]), F32, scope)
                att = sb("b_att", (P, TILES + 1, P), F32, scope)
                vrow = sb("b_v_rows", (P, TILES + 1, P), F32, scope)
                krow = sb("b_k_rows", (P, TILES + 1, P), F32, scope)
                vown = sb("b_v_own", (NS, NB, P), F32, scope)
                qown = sb("b_q_own", (P, NB, NS), F32, scope)
                state = sb("b_state", (P, TILES + 1, P), F32, scope)
                s0 = sb("b_sample_state", (P, NB, P), F32, scope)
                osb = sb("b_o_rows", (P, TILES + 1, P), F32, scope)
                osq = krow
                ssq = sb("b_ssq", (P, TILES + 1), F32, scope)
                rms = sb("b_rms", (P, TILES + 1), F32, scope)
                level = sb("b_level", (P, LEVELS, P), I32, scope)
                own_row = sb("b_own_row", (NS, NB), F32, scope)
                own_col = sb("b_own_col", (P, NB, NS), F32, scope)
                const_in = sem("b_const_in", scope)
                s0_in = sem("b_s0_in", scope)
                level_ready = sem("b_level_ready", scope)
                own_ready = sem("b_own_ready", scope)
                states_ready = sem("b_states_ready", scope)
                new_states = sem("b_new_states", scope)
                stored = sem("b_stored", scope)
                gate_ready = sem("b_gate_ready", scope)
                ssq_ready = sem("b_ssq_ready", scope)
                rms_ready = sem("b_rms_ready", scope)
                o_ready = sem("b_o_ready", scope)
                y_ready = sem("b_y_ready", scope)
                y_out = sem("b_y_out", scope)
                chain = sem("b_chain", scope)
                spans = ((0, 4), (4, 4), (8, 1))
                COUNTS = (("v", 3), ("p0", 3), ("p1", 2), ("p2", 2), ("p3", 2), ("p4", 2), ("p5", 1), ("p6", 1),
                          ("p7", 1), ("k", 3), ("ds", 2), ("os", 1), ("dss", 2), ("o", 2), ("y", 3))
                M, MISC = {}, 0
                for name, n in COUNTS:
                    M[name] = MISC
                    MISC += n
                assert MISC % cv.ring == 0
                CHAIN = 17

                def level_uses(n):
                    if n == 0:
                        return ((0, 4, P), (4, 4, P), (8, 1, NS))
                    if n <= 3:
                        return ((0, 8, P), (8, 1, NS))
                    if n == 4:
                        return ((0, 4, P), (4, 4, P))
                    return ((0, 8, P),)

                def second(x, n):
                    if n == 0:
                        return x
                    return x.rearrange("p (n two m) -> p n two m", two=2, m=1 << (n - 1))[:, :, 1, :]

                with nc.Block() as block:
                    @block.sync
                    def _(sp):
                        for dst, src in ((level[:, :, :], A["c_level"]), (own_row[:, :], A["c_own_row"]),
                                         (own_col[:, :, :], A["c_own_col"])):
                            sp.dma_start(dst, src).then_inc(const_in, 16)
                        with sp.Fori(0, BH - 1) as i:
                            for j, base in enumerate((COL_BI, COL_BG, COL_BF + P, COL_BQ + P)):
                                cv.load(sp, i * UNITS + (SLOTS + j), j % 2, col(w_in, i * P + base))
                        last = [col(w_in, at) for at in (COL_BI + D - P, COL_BG + D - P, *POOL_AT)]
                        for j, src in enumerate([*last, *then]):
                            cv.load(sp, BH * UNITS - SLOTS + j, j % 2, src)

                    @block.gpsimd
                    def _(pool):
                        with pool.Fori(0, BH) as i:
                            for j in range(UNITS):
                                cv.split(pool, i * UNITS + (SLOTS + j), j % 2, i * (UNITS // 2) + (1 + j // 2), KO)
                        for u in range(BH * UNITS + SLOTS, BH * UNITS + SLOTS + len(POOL_AT)):
                            cv.split(pool, u, u % 2, u // 2, KO)

                    @block.scalar
                    def _(act):
                        act.sem_inc(stored, 32)
                        act.sem_inc(y_ready, 1)
                        act.sem_inc(y_out, 16)

                        def load_states(i):
                            act.wait_ge(stored, i * 32 + 32)
                            act.dma_start(s0[:, :, :], A["state_hgrn"][0, :, bass.ds(i, 1), :, :]
                                          .rearrange("b o k v -> k (o b) v")).then_inc(s0_in, 16)

                        def root(i):
                            act.wait_ge(ssq_ready, i + 1)
                            act.activation(rms[:, :], ssq[:, :], ACT.Sqrt, bias=eps[:, :], scale=1.0 / P)\
                                .then_inc(rms_ready, 1)

                        def store_states(i):
                            act.wait_ge(new_states, i + 1)
                            act.dma_start(OUT["hgrn_p"][0, 0, bass.ds(i, 1), :, :]
                                          .rearrange("o k v -> k (o v)"), state[:, TILES, :]).then_inc(stored, 16)
                            act.dma_start(OUT["hgrn_s"][0, :, bass.ds(i, 1), :, :]
                                          .rearrange("b o k v -> k (o b) v"), s0[:, :, :]).then_inc(stored, 16)

                        def store_y(i):
                            act.wait_ge(y_ready, i + 2)
                            act.dma_start(y_d[bass.ds(i, 1)].rearrange("o p t -> p (o t)"), gate[:, :])\
                                .then_inc(y_out, 16)

                        for j, (dst, func) in enumerate(((f_new, ACT.Sigmoid), (q_new, ACT.Copy), (v_new, ACT.Copy))):
                            for c in range(NCH):
                                cv.empty(act, j, c, dst, func)
                        for c in range(NCH):
                            cv.empty(act, 3, c, g_new, ACT.Sigmoid, raw=g_raw)
                        with act.Fori(0, BH - 1) as i:
                            u = i * UNITS + UNITS
                            load_states(i)
                            act.wait_ge(level_ready, i * 9 + 1)
                            for c in range(NCH):
                                cv.empty(act, u, c, f_new, ACT.Sigmoid)
                            act.wait_ge(level_ready, i * 9 + 2)
                            for c in range(NCH):
                                cv.empty(act, u + 1, c, q_new, ACT.Copy)
                            for c in range(NCH):
                                cv.empty(act, u + 2, c, v_new, ACT.Copy)
                            store_states(i)
                            root(i)
                            act.wait_ge(gate_ready, i + 1)
                            for c in range(NCH):
                                cv.empty(act, u + 3, c, g_new, ACT.Sigmoid, raw=g_raw)
                            store_y(i)
                        load_states(BH - 1)
                        for c in range(NCH):
                            empty_ext(cv, act, BH * UNITS, c, ext[0])
                        for c in range(NCH):
                            cv.empty(act, BH * UNITS + 1, c, p_gate, ACT.Sigmoid, raw=p_graw)
                        for c in range(NCH):
                            empty_ext(cv, act, BH * UNITS + 2, c, ext[1])
                        store_states(BH - 1)
                        root(BH - 1)
                        for c in range(NCH):
                            empty_ext(cv, act, BH * UNITS + 3, c, ext[2])
                        store_y(BH - 1)
                        act.wait_ge(stored, 32 * BH + 32)
                        act.wait_ge(y_out, 16 * BH + 16)

                    @block.tensor
                    def _(pe):
                        def product(i, n):
                            if n == 0:
                                cv.emptied(pe, i * UNITS + 1)
                            pe.wait_ge(level_ready, i * 9 + 1 + n)
                            q = q_new if n == 0 else qp
                            for m, (b0, nb, w) in enumerate(level_uses(n)):
                                bank = cv.fill(pe, i * MISC, M[f"p{n}"] + m, w < P or n == LEVELS - 1)
                                wq = w if n == 0 else w // 2
                                for b in range(nb):
                                    ts = slice((b0 + b) * P, (b0 + b) * P + w)
                                    if n == LEVELS - 1:
                                        mm = pe.matmul(bank[0:P // 2, b * wq:(b + 1) * wq],
                                                       kr[:, ts.start:ts.start + P // 2],
                                                       second(q[:, ts], n), start=True, stop=True)
                                        continue
                                    mm = pe.matmul(bank[0:w, b * wq:(b + 1) * wq], kr[:, ts],
                                                   second(q[:, ts], n), start=True, stop=True)
                                mm.then_inc(cv.misc_done, 1)

                        def rows_of(i, src, m):
                            for q, (b0, nb) in enumerate(spans):
                                bank = cv.fill(pe, i * MISC, m + q, q == 2)
                                w = P if q < 2 else NS
                                for b in range(nb):
                                    mm = pe.transpose(bank[0:w, b * P:b * P + P],
                                                      src[:, (b0 + b) * P:(b0 + b) * P + w], ident[:, :])
                                mm.then_inc(cv.misc_done, 1)

                        def own_states(i):
                            cv.copied(pe, i * MISC, M["k"] + 2)
                            for q in range(2):
                                bank = cv.fill(pe, i * MISC, M["ds"] + q)
                                for b in range(4):
                                    mm = pe.matmul(bank[:, b * P:(b + 1) * P], krow[:, 4 * q + b, :],
                                                   vrow[:, 4 * q + b, :], start=True, stop=True)
                                mm.then_inc(cv.misc_done, 1)
                            pe.wait_ge(own_ready, i + 1)
                            pe.wait_ge(s0_in, i * 16 + 16)
                            bank = cv.fill(pe, i * MISC, M["os"], True)
                            pe.matmul(bank[0:NS, 0:P], att[0:NS, TILES, 0:NS], vrow[0:NS, TILES, :],
                                      start=True, stop=False)
                            for b in range(NB):
                                mm = pe.matmul(bank[0:NS, 0:P], qown[:, b, :], s0[:, b, :],
                                               start=False, stop=(b == NB - 1))
                            mm.then_inc(cv.misc_done, 1)
                            for q in range(2):
                                bank = cv.fill(pe, i * MISC, M["dss"] + q, True)
                                pe.matmul(bank[:, :], krow[0:NS, TILES, :], vown[:, 4 * q:4 * q + 4, :],
                                          start=True, stop=True).then_inc(cv.misc_done, 1)

                        def outputs(i):
                            pe.wait_ge(states_ready, i + 1)
                            for q in range(2):
                                bank = cv.fill(pe, i * MISC, M["o"] + q)
                                for b in range(4):
                                    t = 4 * q + b
                                    mm = pe.matmul(bank[:, b * P:(b + 1) * P], att[:, t, :], vrow[:, t, :],
                                                   start=True, stop=(t == 0))
                                    if t > 0:
                                        mm = pe.matmul(bank[:, b * P:(b + 1) * P], qp[:, t * P:(t + 1) * P],
                                                       state[:, t, :], start=False, stop=True)
                                mm.then_inc(cv.misc_done, 1)

                        def back(i):
                            pe.wait_ge(o_ready, i + 1)
                            for q, (b0, nb) in enumerate(spans):
                                bank = cv.fill(pe, i * MISC, M["y"] + q, q == 2)
                                w = P if q < 2 else NS
                                for b in range(nb):
                                    mm = pe.transpose(bank[:, b * P:b * P + w], osb[0:w, b0 + b, :],
                                                      ident[0:w, 0:w])
                                mm.then_inc(cv.misc_done, 1)

                        def v_rows(i):
                            cv.emptied(pe, i * UNITS + 2)
                            rows_of(i, v_new, M["v"])

                        def k_rows(i):
                            pe.wait_ge(level_ready, i * 9 + 9)
                            rows_of(i, kr, M["k"])

                        for j in range(1, UNITS):
                            for c in range(NCH):
                                cv.project(pe, j, j % 2, c, KO, x_hi, x_lo)

                        def head(i, counts):
                            halves = [(j, c, half) for j in range(UNITS) for c in range(NCH) for half in range(2)]

                            def meanwhile(n):
                                for j, c, half in halves[:n]:
                                    cv.project(pe, i * UNITS + (UNITS + j), j % 2, c, KO, x_hi, x_lo, half=half)
                                del halves[:n]

                            before, levels, own, out, turn, after = counts
                            v_rows(i)
                            meanwhile(before)
                            for n in range(LEVELS):
                                product(i, n)
                                meanwhile(levels[n])
                            k_rows(i)
                            meanwhile(own)
                            own_states(i)
                            meanwhile(out)
                            outputs(i)
                            meanwhile(turn)
                            back(i)
                            meanwhile(after)
                            assert not halves

                        with pe.Fori(0, BH - 1) as i:
                            head(i, (1, (1, 1, 1, 1, 2, 1, 1, 1), 2, 4, 4, 4))
                        head(BH - 1, (1, (1, 1, 1, 1, 2, 1, 1, 1), 3, 5, 6, 0))
                        for c in range(NCH):
                            cv.project(pe, BH * UNITS + len(POOL_AT), 0, c, KO, x_hi, x_lo)

                    @block.vector
                    def _(dve):
                        ch = Chain(dve, chain)
                        cv.dve_start(dve)
                        ch.step(dve.memset(osb[:, :, :], 0.0))
                        ch.link(dve.memset(att[:, :, :], 0.0))
                        dve.wait_ge(const_in, 48)
                        with dve.Fori(0, BH) as i:
                            ch.loop(i * CHAIN, CHAIN)
                            u, m0 = i * UNITS, i * MISC

                            def take(n):
                                if n > 0:
                                    cv.copied(dve, m0, M[f"p{n}"] - 1)
                                for m, (b0, nb, w) in enumerate(level_uses(n)):
                                    bank = cv.filled(dve, m0, M[f"p{n}"] + m, n > 0)
                                    if n == 0:
                                        dve.tensor_tensor(att[0:w, b0:b0 + nb, 0:w],
                                                          bank[0:w, 0:nb * w].rearrange("p (a b) -> p a b", b=w),
                                                          ident[0:w, 0:w].unsqueeze(1).broadcast_to([w, nb, w]),
                                                          ALU.mult).then_inc(cv.misc_free, 1)
                                        continue
                                    hf = 1 << (n - 1)
                                    if n == LEVELS - 1:
                                        dve.tensor_copy(att[0:hf, :TILES, hf:P], bank[0:hf, 0:nb * hf]
                                                        .rearrange("p (a m) -> p a m", m=hf)).then_inc(cv.misc_free, 1)
                                        continue
                                    nx = w // (2 * hf)

                                    def halves(x):
                                        return x.rearrange("p a (x two m) -> p a x two m", two=2, m=hf)[:, :, :, 1, :]

                                    dst = halves(att[0:w, b0:b0 + nb, 0:w])
                                    msk = halves(level[0:w, n:n + 1, 0:w]).broadcast_to([w, nb, nx, hf])
                                    src = bank[0:w, 0:nb * w // 2].rearrange("p (a x m) -> p a x m", a=nb, m=hf)
                                    dve.copy_predicated(dst, msk, src).then_inc(cv.misc_free, 1)

                            def update(n):
                                dve.wait_ge(cv.misc_done, m0 + M[f"p{n}"] + len(level_uses(n)))
                                dve.wait_ge(level_ready, i * 9 + n + 1)
                                if n == 0:
                                    dve.tensor_tensor(qp[:, :], q_new[:, :], ff[:, :], ALU.mult)\
                                        .then_inc(level_ready, 1)
                                    return
                                nt = NT if n <= 3 else SEQ
                                nb, half_ = nt >> n, 1 << (n - 1)
                                prev = ff if n == 1 else fts[:, ft_at[n - 1]:ft_at[n - 1] + ft_n[n - 1]]
                                fv = prev[:, 0:2 * nb].rearrange("p (n two) -> p n two", two=2)
                                qv = qp[:, 0:nt].rearrange("p (n two m) -> p n two m", two=2, m=half_)
                                kv = kr[:, 0:nt].rearrange("p (n two m) -> p n two m", two=2, m=half_)
                                ch.step(dve.tensor_tensor(fts[:, ft_at[n]:ft_at[n] + nb], fv[:, :, 0], fv[:, :, 1],
                                                          ALU.mult))
                                dve.tensor_tensor(qv[:, :, 1, :], qv[:, :, 1, :],
                                                  fv[:, :, 0:1].broadcast_to([P, nb, half_]), ALU.mult)
                                dve.tensor_tensor(kv[:, :, 0, :], kv[:, :, 0, :],
                                                  fv[:, :, 1:2].broadcast_to([P, nb, half_]), ALU.mult)\
                                    .then_inc(level_ready, 1)

                            def rows_to(dst, m):
                                for q, (b0, nb) in enumerate(spans):
                                    bank = cv.filled(dve, m0, m + q)
                                    w = P if q < 2 else NS
                                    dve.tensor_copy(dst[0:w, b0:b0 + nb, :], bank[0:w, 0:nb * P]
                                                    .rearrange("p (a b) -> p a b", b=P)).then_inc(cv.misc_free, 1)

                            cv.emptied(dve, u)
                            ch.link(dve.tensor_scalar(ff[:, :], f_new[:, :], one_lb[:, bass.ds(i, 1)],
                                                      lb[:, bass.ds(i, 1)], ALU.mult, ALU.add))
                            dve.tensor_scalar(kr[:, :], ff[:, :], -1.0, 1.0, ALU.mult, ALU.add)\
                                .then_inc(level_ready, 1)
                            rows_to(vrow, M["v"])
                            for n in range(4):
                                update(n)
                                take(n)
                            ch.step(dve.tensor_tensor(
                                vown[:, :, :], vrow[0:NS, TILES:TILES + 1, :].broadcast_to([NS, NB, P]),
                                own_row[:, :].unsqueeze(2).broadcast_to([NS, NB, P]), ALU.mult))
                            dve.wait_ge(level_ready, i * 9 + 5)
                            dve.tensor_tensor(qown[:, :, :], qp[:, SEQ:NT].unsqueeze(1)
                                              .broadcast_to([P, NB, NS]), own_col[:, :, :], ALU.mult)\
                                .then_inc(own_ready, 1)
                            for n in range(4, LEVELS):
                                update(n)
                                take(n)
                            cv.emptied(dve, u + 3)
                            dve.wait_ge(y_out, i * 16 + 16)
                            dve.tensor_tensor(gate[:, :], g_new[:, :], g_raw[:, :], ALU.mult)\
                                .then_inc(gate_ready, 1)
                            rows_to(krow, M["k"])
                            f7 = fts[:, ft_at[7]:ft_at[7] + TILES]
                            f3 = fts[:, ft_at[3] + SEQ // TB:ft_at[3] + NT // TB]
                            dve.wait_ge(stored, i * 32 + 32)
                            for t in range(TILES):
                                if t % 4 == 0:
                                    bank = cv.filled(dve, m0, M["ds"] + t // 4)
                                src = bank[:, (t % 4) * P:(t % 4 + 1) * P]
                                if t == 0:
                                    ch.step(dve.tensor_copy(state[:, 1, :], src))
                                    continue
                                ch.wait()
                                ins = dve.scalar_tensor_tensor(
                                    out=state[:, t + 1, :], in0=state[:, t, :], scalar=f7[:, t:t + 1],
                                    in1=src, op0=ALU.mult, op1=ALU.add)
                                if t == 3:
                                    ins.then_inc(cv.misc_free, 1)
                                    cv.copied(dve, m0, M["ds"])
                                elif t == TILES - 1:
                                    ins.then_inc(cv.misc_free, 1)
                                else:
                                    ch.step(ins)
                            cv.copied(dve, m0, M["ds"] + 1)
                            dve.sem_inc(states_ready, 1)
                            bank = cv.filled(dve, m0, M["os"])
                            dve.tensor_copy(osb[0:NS, TILES, :], bank[0:NS, 0:P]).then_inc(cv.misc_free, 1)
                            for q in range(2):
                                bank = cv.filled(dve, m0, M["dss"] + q)
                                for b in range(4 * q, 4 * q + 4):
                                    ins = dve.scalar_tensor_tensor(
                                        out=s0[:, b, :], in0=s0[:, b, :], scalar=f3[:, b:b + 1],
                                        in1=bank[:, (b % 4) * P:(b % 4 + 1) * P], op0=ALU.mult, op1=ALU.add)
                                ins.then_inc(cv.misc_free, 1)
                            cv.copied(dve, m0, M["dss"] + 1)
                            dve.sem_inc(new_states, 1)
                            for q in range(2):
                                bank = cv.filled(dve, m0, M["o"] + q)
                                dve.tensor_copy(osb[:, 4 * q:4 * q + 4, :],
                                                bank[:, :].rearrange("p (a b) -> p a b", b=P))\
                                    .then_inc(cv.misc_free, 1)
                            cv.copied(dve, m0, M["o"] + 1)
                            ch.link(dve.tensor_tensor(osq[:, :, :], osb[:, :, :], osb[:, :, :], ALU.mult))
                            dve.tensor_reduce(ssq[:, :], osq[:, :, :], AX.X, ALU.add).then_inc(ssq_ready, 1)
                            dve.wait_ge(rms_ready, i + 1)
                            ch.link(dve.reciprocal(rms[:, :], rms[:, :]))
                            dve.tensor_tensor(osb[:, :, :], osb[:, :, :],
                                              rms[:, :].unsqueeze(2).broadcast_to([P, TILES + 1, P]), ALU.mult)\
                                .then_inc(o_ready, 1)
                            dve.wait_ge(gate_ready, i + 1)
                            for q, (b0, nb) in enumerate(spans):
                                bank = cv.filled(dve, m0, M["y"] + q)
                                n = nb * P if q < 2 else NS
                                ts = slice(b0 * P, b0 * P + n)
                                dve.scalar_tensor_tensor(out=gate[:, ts], in0=bank[:, 0:n], scalar=h_norm[:, :],
                                                         in1=gate[:, ts], op0=ALU.mult, op1=ALU.mult)\
                                    .then_inc(cv.misc_free, 1)
                            cv.copied(dve, m0, M["y"] + 2)
                            dve.sem_inc(y_ready, 1)
                            ch.end(BH)

        def attention_phase(then):
            UNITS, MISC = 10, 51
            KB = 4
            KW = KB * P + AG * NS
            K_G = (0, 1, 1, 2)
            scope = ExitStack()
            with scope:
                cv = Conveyor("a", scope, (3, 4, 7), AH * UNITS)
                qk = [sb(f"a_feature{i}", (P, NT), F32, scope) for i in range(4)]
                vrow = [sb(f"a_v_rows{g}", (P, TILES + 1, P), F32, scope) for g in range(AG)]
                krow = sb("a_k_rows", (P, TILES + 1, P), F32, scope)
                gate = sb("a_gate", (P, NT), F32, scope)
                graw = sb("a_gate_raw", (P, NT), F32, scope)
                T_COLS = [[P] + [2 * P] * 7, [P, 2 * P] * 4, [P] * 8]
                T_AT, at = [], 0
                for g in range(AG):
                    row = []
                    for w in T_COLS[g]:
                        row.append(at)
                        at += w
                    T_AT.append(row)
                prob = sb("a_prob", (P, at), F32, scope)
                pt = [sb(f"a_prob_t{i}", (P, 4, P), F32, scope) for i in range(2)]
                mx = sb("a_max", (P, AG, TILES), F32, scope)
                st = sb("a_stats", (P, AG, TILES, 2), F32, scope)
                comm = sb("a_stats_by_token", (P, TILES, 2, 2), F32, scope)
                nmin = sb("a_least", (P, TILES), F32, scope)
                ex = sb("a_group_exp", (P, AG, TILES), F32, scope)
                lw = sb("a_group_sum", (P, AG, TILES), F32, scope)
                den = sb("a_denominator", (P, TILES), F32, scope)
                wt = sb("a_weight", (P, TILES, 2), F32, scope)
                w0 = sb("a_weight0", (P, TILES), F32, scope)
                w12 = sb("a_weight12", (P, 2, TILES), F32, scope)
                yt = graw
                kv = [sb(f"s_cached{i}", (P, KB, P), F32, scope) for i in range(NB + 4)]
                VC = [8, 9, 10, 11, 0, 1, 2, 3]
                mask = sb("s_mask", (NS, KW), F32, scope)
                qh = sb("s_q", (P, AG, NS), F32, scope)
                kh = sb("s_k", (P, AG, NS), F32, scope)
                kt = [sb(f"s_k_feature{i}", (P, KB, P), F32, scope) for i in range(2)]
                sct = sb("s_scores_t", (P, KB, NS), F32, scope)
                sprob = sb("s_prob", (NS, KW), F32, scope)
                spt = sb("s_prob_t", (NS, AG, NS), F32, scope)
                own = sb("s_prob_t_own", (P, KB * NB * NS + NS), F32, scope)
                orow = sb("s_o_rows", (NS, P), F32, scope)
                s_rows_ready = sem("s_rows_ready", scope)
                s_turned = sem("s_turned", scope)
                smx = sb("s_max", (NS, 1), F32, scope)
                snm = sb("s_negmax", (NS, 1), F32, scope)
                ssm = sb("s_sum", (NS, 1), F32, scope)
                mask_in = sem("s_mask_in", scope)
                k_in = [sem(f"s_k_in{b}", scope) for b in range(NB)]
                v_in = [sem(f"s_v_in{b}", scope) for b in range(NB)]
                keys_used = sem("s_keys_used", scope)
                s_scores_done = sem("s_scores_done", scope)
                s_scores_out = sem("s_scores_copied", scope)
                s_negmax = sem("s_negmax_ready", scope)
                s_exp_done = sem("s_exp_done", scope)
                s_prob_ready = sem("s_prob_ready", scope)
                s_o_done = sem("s_o_done", scope)
                caches = [A["cache_kv_w128"][0], A["cache_kv_w512"][0], A["cache_kv_w2048"][0]]

                scores_max = sem("a_negmax_ready", scope)
                exp_done = sem("a_exp_done", scope)
                stats_out = sem("a_stats_out", scope)
                stats_in = sem("a_stats_in", scope)
                spread = sem("a_spread_ready", scope)
                group_exp = sem("a_group_exp_ready", scope)
                weights_ready = sem("a_weights_ready", scope)
                weights_out = sem("a_weights_out", scope)
                weights_in = sem("a_weights_in", scope)
                scaled = sem("a_prob_scaled", scope)
                krow_ready = sem("a_krow_ready", scope)
                krow_out = sem("a_krow_out", scope)
                vrow_out = sem("a_vrow_out", scope)
                o_done = sem("a_o_done", scope)
                y_ready = sem("a_y_ready", scope)
                y_out = sem("a_y_out", scope)
                chain = sem("a_chain", scope)
                CHAIN = 52
                spans = ((0, 4), (4, 4), (8, 1))
                COLS = [COL_AQ, COL_AK, COL_AQ + GROUP, COL_AK + GROUP, COL_AQ + 2 * GROUP,
                        COL_AK + 2 * GROUP, COL_AV, COL_AV + GROUP, COL_AV + 2 * GROUP, COL_AG]
                DST = [qk[0], qk[1], qk[2], qk[3], qk[0], qk[1], qk[2], qk[3], qk[0], gate]
                U_Q, U_K, U_V, U_G = (0, 2, 4), (1, 3, 5), (6, 7, 8), 9
                M_S, M_K, M_V = (0, 7, 14), (4, 11, 18), (29, 34, 38)
                M_KT, M_NEW, M_SC, M_SPT, M_O = 21, 32, 33, 37, 42
                M_P = [41] + [43 + n for n in range(8)]
                V_OUT = 16 * 6

                def tokens(src, g, c):
                    if g == 0:
                        return src[:, c * P:(c + 1) * P]
                    if g == 1:
                        r, n = c // 2, c % 2
                        return src[:, 4 * P * n + r:4 * P * n + r + 4 * (P - 1) + 1:4]
                    return src[:, c:c + 8 * (P - 1) + 1:8]

                def keys(src, g, c):
                    if g == 0 and c > 0:
                        return src[:, (c - 1) * P:(c + 1) * P]
                    if g == 1 and c % 2 == 1:
                        return src[:, c // 2:c // 2 + 4 * (2 * P - 1) + 1:4]
                    return tokens(src, g, c)

                BLOCKS = []
                for g in range(AG):
                    for c in range(TILES):
                        w = T_COLS[g][c] // P
                        for b in range(w):
                            BLOCKS.append((g, c, T_AT[g][c] + b * P, c - (w - 1) + b))
                N_PT = (len(BLOCKS) + 3) // 4
                assert N_PT == len(M_P)

                def load_rows(sp, dst, b, which, hd, done):
                    c = [x[b, :, which, hd, :] for x in caches]
                    sp.dma_start(dst[:, 0:1, :], c[0].rearrange("(n p) o e -> p n (o e)", p=P)).then_inc(done, 16)
                    sp.dma_start(dst[:, 1:3, :], c[1].rearrange("(n p) o e -> p n (o e)", p=P)).then_inc(done, 16)
                    sp.dma_start(dst[:, 3, :], c[2].rearrange("(a r) o e -> a r (o e)", r=16)[:, 0:8, :])\
                        .then_inc(done, 16)

                with nc.Block() as block:
                    @block.sync
                    def _(sp):
                        sp.dma_start(mask[:, :], A["c_sample_mask"]).then_inc(mask_in, 16)
                        def head(h, after):
                            hd = bass.ds(h, 1)
                            for j in range(SLOTS, UNITS):
                                cv.load(sp, h * UNITS + j, j % 2, col(w_in, h * P + COLS[j]))
                                if j == 4:
                                    sp.wait_ge(s_o_done, h + 1)
                                    sp.sem_inc(cv.held_sp, 1)
                                if j in (4, 5):
                                    for b in range(4 * (j - 4), 4 * (j - 4) + 4):
                                        load_rows(sp, kv[b], b, 0, hd, k_in[b])
                                if j == 6:
                                    for b in range(4):
                                        load_rows(sp, kv[VC[b]], b, 1, hd, v_in[b])
                            cv.load(sp, h * UNITS + UNITS, 0, after[0])
                            sp.wait_ge(keys_used, h + 1)
                            sp.sem_inc(cv.held_sp, 1)
                            for b in range(4, NB):
                                load_rows(sp, kv[VC[b]], b, 1, hd, v_in[b])
                            sp.wait_ge(exp_done, h * AG + AG)
                            sp.sem_inc(cv.held_sp, 1)
                            d = stat_d[bass.ds(h, 1)]
                            sp.dma_start(d[:, :, 0, :].rearrange("o (n i r) s -> i (o r) n s", n=2, r=4),
                                         st[:, 1, :, :].rearrange("p (r n) s -> p r n s", n=2),
                                         allow_slow_non_contiguous=True).then_inc(stats_out, 16)
                            sp.dma_start(d[:, :, 1, :].rearrange("o (i j) s -> i (o j) s", j=8),
                                         st[:, 2, :, :], allow_slow_non_contiguous=True).then_inc(stats_out, 16)
                            sp.wait_ge(stats_out, h * 32 + 32)
                            sp.sem_inc(cv.held_sp, 1)
                            sp.dma_start(comm[:, :, :, :], d.rearrange("o (b p) g s -> p (o b) g s", p=P),
                                         allow_slow_non_contiguous=True).then_inc(stats_in, 16)
                            cv.load(sp, h * UNITS + (UNITS + 1), 1, after[1])
                            sp.wait_ge(weights_ready, h + 1)
                            sp.sem_inc(cv.held_sp, 1)
                            d = weight_d[bass.ds(h, 1)]
                            sp.dma_start(d.rearrange("o (b p) g -> p (o b) g", p=P), wt[:, :, :],
                                         allow_slow_non_contiguous=True).then_inc(weights_out, 16)
                            sp.wait_ge(weights_out, h * 16 + 16)
                            sp.sem_inc(cv.held_sp, 1)
                            for n in range(2):
                                sp.dma_start(w12[:, 0, n:TILES:2],
                                             d[:, :, 0].rearrange("o (n i r) -> n i (o r)", n=2, r=4)[n],
                                             allow_slow_non_contiguous=True).then_inc(weights_in, 16)
                            sp.dma_start(w12[:, 1, :], d[:, :, 1].rearrange("o (i j) -> i (o j)", j=8),
                                         allow_slow_non_contiguous=True).then_inc(weights_in, 16)

                        with sp.Fori(0, AH - 1) as h:
                            head(h, [col(w_in, h * P + (P + COLS[j])) for j in range(SLOTS)])
                        head(AH - 1, then)

                    @block.gpsimd
                    def _(pool):
                        with pool.Fori(0, AH) as h:
                            for j in range(UNITS):
                                cv.split(pool, h * UNITS + (SLOTS + j), j % 2, h * (UNITS // 2) + (1 + j // 2), KO)

                    @block.tensor
                    def _(pe):
                        pe.sem_inc(s_o_done, 1)
                        with pe.Fori(0, AH) as h:
                            u, m0 = h * UNITS, h * MISC

                            def chunk(j, c):
                                cv.project(pe, u + j, j % 2, c, KO, x_hi, x_lo)

                            def unit(j):
                                for c in range(NCH):
                                    chunk(j, c)

                            def scores(g):
                                cv.emptied(pe, u + U_K[g])
                                for n in range(4):
                                    bank = cv.fill(pe, m0, M_S[g] + n)
                                    for c in (2 * n, 2 * n + 1):
                                        w = T_COLS[g][c]
                                        a = (c % 2) * 2 * P
                                        mm = pe.matmul(bank[:, a:a + w], tokens(DST[U_Q[g]], g, c),
                                                       keys(DST[U_K[g]], g, c), start=True, stop=True)
                                    mm.then_inc(cv.misc_done, 1)

                            def rows(src, m, g):
                                for q, (b0, nb) in enumerate(spans):
                                    bank = cv.fill(pe, m0, m + q, q == 2)
                                    for b in range(b0, b0 + nb):
                                        if b == TILES:
                                            mm = pe.transpose(bank[0:NS, 0:P], src[:, SEQ:NT], ident[:, :])
                                        else:
                                            mm = pe.transpose(bank[:, (b % 4) * P:(b % 4 + 1) * P],
                                                              tokens(src, g, b), ident[:, :])
                                    mm.then_inc(cv.misc_done, 1)

                            def v_rows(g):
                                cv.emptied(pe, u + U_V[g])
                                rows(DST[U_V[g]], M_V[g], g)

                            unit(1)
                            unit(2)
                            scores(0)
                            rows(DST[U_K[0]], M_K[0], 0)
                            unit(3)
                            unit(4)
                            scores(1)
                            rows(DST[U_K[1]], M_K[1], 0)
                            unit(5)
                            unit(6)
                            scores(2)
                            rows(DST[U_K[2]], M_K[2], 0)
                            def keys_t(b):
                                pe.wait_ge(k_in[b], h * 48 + 48)
                                bank = cv.fill(pe, m0, M_KT + b)
                                for n in range(KB):
                                    mm = pe.transpose(bank[:, n * P:(n + 1) * P], kv[b][:, n, :], ident[:, :])
                                mm.then_inc(cv.misc_done, 1)

                            def key_scores(b):
                                cv.copied(pe, m0, M_KT + b)
                                pe.sem_inc(cv.held_pe, 1)
                                for n in range(KB):
                                    mm = pe.matmul(psum[:, 5, n * NS + b * TB:n * NS + (b + 1) * TB],
                                                   kt[b % 2][:, n, :], qh[:, K_G[n], b * TB:(b + 1) * TB],
                                                   start=True, stop=True)
                                return mm

                            pe.wait_ge(scores_max, h * AG + AG)
                            pe.wait_ge(y_ready, h + 1)
                            keys_t(0)
                            keys_t(1)
                            chunk(7, 0)
                            key_scores(0)
                            key_scores(1)
                            keys_t(2)
                            keys_t(3)
                            chunk(7, 1)
                            key_scores(2)
                            key_scores(3).then_inc(keys_used, 1)
                            keys_t(4)
                            keys_t(5)
                            chunk(7, 2)
                            key_scores(4)
                            key_scores(5)
                            keys_t(6)
                            keys_t(7)
                            v_rows(0)
                            chunk(8, 0)
                            key_scores(6)
                            key_scores(7).then_inc(s_scores_done, 1)
                            bank = cv.fill(pe, m0, M_NEW, True)
                            for g in range(AG):
                                mm = pe.matmul(bank[0:NS, g * NS:(g + 1) * NS], qh[:, g, :], kh[:, g, :],
                                               start=True, stop=True)
                            mm.then_inc(cv.misc_done, 1)
                            chunk(8, 1)
                            pe.wait_ge(s_scores_out, h + 1)
                            bank = cv.fill(pe, m0, M_SC, True)
                            for n in range(KB):
                                mm = pe.transpose(bank[0:NS, n * P:(n + 1) * P], sct[:, n, :], ident[:, :])
                            mm.then_inc(cv.misc_done, 1)
                            chunk(8, 2)
                            v_rows(1)
                            unit(9)
                            pe.wait_ge(s_prob_ready, h + 1)
                            bank = cv.fill(pe, m0, M_SPT, True)
                            for n in range(KB):
                                mm = pe.transpose(bank[:, n * NS:(n + 1) * NS], sprob[:, n * P:(n + 1) * P],
                                                  ident[0:NS, 0:NS])
                            for n in range(KB, KB + AG):
                                a = KB * P + (n - KB) * NS
                                mm = pe.transpose(bank[0:NS, n * NS:(n + 1) * NS], sprob[:, a:a + NS],
                                                  ident[0:NS, 0:NS])
                            mm.then_inc(cv.misc_done, 1)
                            v_rows(2)

                            def sample_values():
                                cv.copied(pe, m0, M_V[2] + 2)
                                bank = cv.fill(pe, m0, M_O, True)
                                for g in range(AG):
                                    pe.matmul(bank[0:NS, 0:P], spt[:, g, :], vrow[g][0:NS, TILES, :],
                                              start=(g == 0), stop=False)
                                for b in range(NB):
                                    pe.wait_ge(v_in[b], h * 48 + 48)
                                    for n in range(KB):
                                        a = (n * NB + b) * NS
                                        mm = pe.matmul(bank[0:NS, 0:P], own[:, a:a + NS], kv[VC[b]][:, n, :],
                                                       start=False, stop=(b == NB - 1 and n == KB - 1))
                                mm.then_inc(cv.misc_done, 1)
                                pe.sem_inc(s_o_done, 1)

                            def sample_turn():
                                pe.wait_ge(s_rows_ready, h + 1)
                                pe.sem_inc(cv.held_pe, 1)
                                pe.transpose(cv.bank(0, M_O)[:, P:P + NS], orow[:, :], ident[0:NS, 0:NS])\
                                    .then_inc(s_turned, 1)

                            def turn(n):
                                bank = cv.fill(pe, m0, M_P[n])
                                for b, (g, c, at, kb) in enumerate(BLOCKS[4 * n:4 * n + 4]):
                                    mm = pe.transpose(bank[:, b * P:(b + 1) * P], prob[:, at:at + P], ident[:, :])
                                mm.then_inc(cv.misc_done, 1)

                            def values(n):
                                cv.copied(pe, m0, M_P[n])
                                mm = None
                                for b, (g, c, at, kb) in enumerate(BLOCKS[4 * n:4 * n + 4]):
                                    rhs = pt[n % 2][:, b, :]
                                    v = vrow[g][:, kb, :]
                                    if g == 0:
                                        mm = pe.matmul(psum[:, 5 + c // 4, (c % 4) * P:(c % 4 + 1) * P], v, rhs,
                                                       start=(c % 4 == 0 and kb == max(c - 1, 0)), stop=False,
                                                       skip_group_check=True)
                                    elif g == 1:
                                        mm = pe.matmul(psum[:, 5 + c % 2, c // 2:c // 2 + 4 * (P - 1) + 1:4], v, rhs,
                                                       start=False, stop=False, skip_group_check=True)
                                    else:
                                        for k in range(2):
                                            mm = pe.matmul(psum[:, 5 + k, c:c + 8 * 63 + 1:8], v,
                                                           rhs[:, 64 * k:64 * k + 64], start=False,
                                                           stop=(c == TILES - 1), skip_group_check=True)
                                return mm

                            pe.wait_ge(scaled, h + 1)
                            turn(0)
                            sample_values()
                            chunk(UNITS, 0)
                            sample_turn()
                            for n in range(1, N_PT):
                                turn(n)
                                values(n - 1)
                            values(N_PT - 1).then_inc(o_done, 1)
                            chunk(UNITS, 1)
                            chunk(UNITS, 2)

                    @block.scalar
                    def _(act):
                        act.sem_inc(y_ready, 1)
                        act.sem_inc(y_out, 16)
                        act.sem_inc(krow_out, 32)
                        act.sem_inc(vrow_out, V_OUT)
                        with act.Fori(0, AH) as h:
                            u = h * UNITS

                            def unit(j):
                                for c in range(NCH):
                                    cv.empty(act, u + j, c, DST[j], ACT.Copy)

                            def exps(g):
                                act.wait_ge(scores_max, h * AG + g + 1)
                                for c in range(TILES):
                                    a, w = T_AT[g][c], T_COLS[g][c]
                                    ins = act.activation(prob[:, a:a + w], prob[:, a:a + w], ACT.Exp,
                                                         bias=st[:, g, c, 0:1], scale=SCALE,
                                                         accum_out=st[:, g, c, 1:2])
                                ins.then_inc(exp_done, 1)

                            def rows_out(g, which, src, done):
                                o = OUT[("kv128_p", "kv512_p", "kv2048_p")[g]]
                                hd = bass.ds(h, 1)
                                if g == 0:
                                    act.dma_start(o[0, 0, :, which, hd, :], src[:, TILES - 1:TILES, :]).then_inc(done, 16)
                                elif which == 0:
                                    b0 = 4 if g == 1 else 0
                                    act.dma_start(o[0, 0, :, which, hd, :].rearrange("(b p) o e -> p b (o e)", p=P),
                                                  src[:, b0:TILES, :]).then_inc(done, 16)
                                elif g == 1:
                                    act.dma_start(o[0, 0, :, which, hd, :].rearrange("(i r) o e -> i r (o e)", r=4),
                                                  src[:, 1:TILES:2, :]).then_inc(done, 16)
                                else:
                                    act.dma_start(o[0, 0, :, which, hd, :].rearrange("(i j) o e -> i j (o e)", j=8),
                                                  src[:, 0:TILES, :]).then_inc(done, 16)
                                o = OUT[("kv128_s", "kv512_s", "kv2048_s")[g]]
                                act.dma_start(o[0, :, :, which, hd, :].rearrange("b t o e -> (b t) (o e)"),
                                              src[0:NS, TILES, :]).then_inc(done, 16)

                            unit(0)
                            unit(1)
                            unit(2)
                            unit(3)
                            exps(0)
                            act.wait_ge(krow_ready, h * 6 + 1)
                            rows_out(0, 0, krow, krow_out)
                            unit(4)
                            unit(5)
                            exps(1)
                            act.wait_ge(krow_ready, h * 6 + 2)
                            rows_out(1, 0, krow, krow_out)
                            unit(6)
                            unit(7)
                            exps(2)
                            act.wait_ge(krow_ready, h * 6 + 3)
                            rows_out(2, 0, krow, krow_out)
                            act.wait_ge(spread, h + 1)
                            act.activation(ex[:, :, :], ex[:, :, :], ACT.Exp).then_inc(group_exp, 1)
                            unit(8)
                            act.wait_ge(krow_ready, h * 6 + 4)
                            rows_out(0, 1, vrow[0], vrow_out)
                            act.wait_ge(s_negmax, h + 1)
                            act.activation(sprob[:, :], sprob[:, :], ACT.Exp, bias=snm[:, :], scale=SCALE,
                                           accum_out=ssm[:, :]).then_inc(s_exp_done, 1)
                            act.wait_ge(y_out, h * 16 + 16)
                            for c in range(NCH):
                                cv.empty(act, u + U_G, c, gate, ACT.Sigmoid, raw=graw)
                            act.wait_ge(krow_ready, h * 6 + 5)
                            rows_out(1, 1, vrow[1], vrow_out)
                            act.wait_ge(krow_ready, h * 6 + 6)
                            rows_out(2, 1, vrow[2], vrow_out)
                            act.wait_ge(y_ready, h + 2)
                            act.dma_start(y_d[bass.ds(h + Y_A, 1), :, :].rearrange("o p t -> p (o t)"), yt[:, :])\
                                .then_inc(y_out, 16)
                        act.wait_ge(y_out, 16 * AH + 16)
                        act.wait_ge(krow_out, 96 * AH + 32)
                        act.wait_ge(vrow_out, V_OUT * AH + V_OUT)

                    @block.vector
                    def _(dve):
                        ch = Chain(dve, chain)
                        cv.dve_start(dve)
                        ch.link(dve.memset(own[:, :], 0.0))
                        dve.wait_ge(mask_in, 16)
                        with dve.Fori(0, AH) as h:
                            ch.loop(h * CHAIN, CHAIN)
                            u, m0 = h * UNITS, h * MISC

                            def scores(g):
                                cv.emptied(dve, u + U_K[g])
                                for dst, src in ((qh, DST[U_Q[g]]), (kh, DST[U_K[g]])):
                                    ch.step(dve.tensor_copy(dst[:, g, :], src[:, SEQ:NT]))
                                for n in range(4):
                                    bank = cv.filled(dve, m0, M_S[g] + n)
                                    for c in (2 * n, 2 * n + 1):
                                        a, w = T_AT[g][c], T_COLS[g][c]
                                        mask = pair[:, :] if g == 2 else band[:, 2 * P - w:2 * P]
                                        ps_ = bank[:, (c % 2) * 2 * P:(c % 2) * 2 * P + w]
                                        ins = dve.tensor_tensor(prob[:, a:a + w], ps_, mask, ALU.add)
                                        if c % 2:
                                            ins.then_inc(cv.misc_free, 1)
                                cv.copied(dve, m0, M_S[g] + 3)
                                if g == 0:
                                    parts = ((0, 1, 1, P), (1, 7, 1, 2 * P))
                                elif g == 1:
                                    parts = ((0, 4, 2, P), (1, 4, 2, 2 * P))
                                else:
                                    parts = ((0, 8, 1, P),)
                                for c0, n, step, w in parts:
                                    if g == 1:
                                        pv = prob[:, T_AT[1][0]:T_AT[1][0] + 12 * P]\
                                            .rearrange("p (n w) -> p n w", w=3 * P)[:, :, c0 * P:c0 * P + w]
                                    else:
                                        pv = prob[:, T_AT[g][c0]:T_AT[g][c0] + n * w].rearrange("p (n w) -> p n w", w=w)
                                    ch.step(dve.tensor_reduce(mx[:, g, c0:c0 + step * (n - 1) + 1:step], pv,
                                                              AX.X, ALU.max))
                                ch.wait()
                                dve.tensor_scalar(st[:, g, :, 0], mx[:, g, :], -SCALE, None, ALU.mult)\
                                    .then_inc(scores_max, 1)

                            def rows(dst, m):
                                for q, (b0, nb) in enumerate(spans):
                                    bank = cv.filled(dve, m0, m + q)
                                    w = P if q < 2 else NS
                                    dve.tensor_copy(dst[0:w, b0:b0 + nb, :], bank[0:w, 0:nb * P]
                                                    .rearrange("p (a b) -> p a b", b=P)).then_inc(cv.misc_free, 1)
                                cv.copied(dve, m0, m + 2)
                                dve.sem_inc(krow_ready, 1)

                            scores(0)
                            dve.wait_ge(krow_out, h * 96 + 32)
                            rows(krow, M_K[0])
                            scores(1)
                            dve.wait_ge(krow_out, h * 96 + 64)
                            rows(krow, M_K[1])
                            scores(2)
                            dve.wait_ge(krow_out, h * 96 + 96)
                            rows(krow, M_K[2])
                            for b in range(NB):
                                bank = cv.filled(dve, m0, M_KT + b)
                                dve.tensor_copy(kt[b % 2][:, :, :], bank.rearrange("p (a b) -> p a b", b=P))\
                                    .then_inc(cv.misc_free, 1)
                            dve.wait_ge(vrow_out, h * V_OUT + V_OUT)
                            rows(vrow[0], M_V[0])
                            bank = cv.filled(dve, m0, M_NEW)
                            dve.tensor_tensor(sprob[:, KB * P:KW], bank[0:NS, 0:AG * NS], mask[:, KB * P:KW], ALU.add)\
                                .then_inc(cv.misc_free, 1)
                            dve.wait_ge(s_scores_done, h + 1)
                            dve.tensor_copy(sct[:, :, :], psum[:, 5, 0:KB * NS].rearrange("p (a b) -> p a b", b=NS))\
                                .then_inc(s_scores_out, 1)
                            dve.wait_ge(exp_done, h * AG + AG)
                            dve.wait_ge(stats_in, h * 16 + 16)
                            nm = [st[:, 0, :, 0], comm[:, :, 0, 0], comm[:, :, 1, 0]]
                            ls = [st[:, 0, :, 1], comm[:, :, 0, 1], comm[:, :, 1, 1]]
                            ch.link(dve.tensor_tensor(nmin[:, :], nm[0], nm[1], ALU.min))
                            ch.link(dve.tensor_tensor(nmin[:, :], nmin[:, :], nm[2], ALU.min))
                            for g in range(AG):
                                ch.step(dve.tensor_tensor(ex[:, g, :], nmin[:, :], nm[g], ALU.subtract))
                            ch.wait()
                            dve.sem_inc(spread, 1)
                            dve.wait_ge(group_exp, h + 1)
                            for g in range(AG):
                                ch.step(dve.tensor_tensor(lw[:, g, :], ex[:, g, :], ls[g], ALU.mult))
                            ch.wait()
                            ch.link(dve.tensor_tensor(den[:, :], lw[:, 0, :], lw[:, 1, :], ALU.add))
                            ch.link(dve.tensor_tensor(den[:, :], den[:, :], lw[:, 2, :], ALU.add))
                            ch.link(dve.reciprocal(den[:, :], den[:, :]))
                            ch.step(dve.tensor_tensor(w0[:, :], ex[:, 0, :], den[:, :], ALU.mult))
                            for g in (1, 2):
                                ch.step(dve.tensor_tensor(wt[:, :, g - 1], ex[:, g, :], den[:, :], ALU.mult))
                            ch.wait()
                            dve.sem_inc(weights_ready, 1)
                            bank = cv.filled(dve, m0, M_SC)
                            dve.tensor_tensor(sprob[:, 0:KB * P], bank[0:NS, :], mask[:, 0:KB * P], ALU.add)\
                                .then_inc(cv.misc_free, 1)
                            cv.copied(dve, m0, M_SC)
                            ch.link(dve.tensor_reduce(smx[:, :], sprob[:, :], AX.X, ALU.max))
                            dve.tensor_scalar(snm[:, :], smx[:, :], -SCALE, None, ALU.mult).then_inc(s_negmax, 1)
                            rows(vrow[1], M_V[1])
                            dve.wait_ge(s_exp_done, h + 1)
                            ch.link(dve.reciprocal(ssm[:, :], ssm[:, :]))
                            dve.tensor_scalar(sprob[:, :], sprob[:, :], ssm[:, :], None, ALU.mult)\
                                .then_inc(s_prob_ready, 1)
                            dve.wait_ge(weights_in, h * 48 + 48)
                            for g in range(AG):
                                for c in range(TILES):
                                    a, w = T_AT[g][c], T_COLS[g][c]
                                    sc = w0[:, c:c + 1] if g == 0 else w12[:, g - 1, c:c + 1]
                                    ch.step(dve.tensor_scalar(prob[:, a:a + w], prob[:, a:a + w], sc, None, ALU.mult))
                            ch.wait()
                            dve.sem_inc(scaled, 1)
                            bank = cv.filled(dve, m0, M_SPT)
                            for n in range(KB):
                                a = n * NB * NS
                                dve.tensor_copy(own[:, a:a + NB * (NS + TB)].rearrange("p (b x) -> p b x", x=NS + TB)
                                                [:, :, 0:TB], bank[:, n * NS:(n + 1) * NS]
                                                .rearrange("p (b t) -> p b t", t=TB))
                            dve.tensor_copy(spt[:, :, :], bank[0:NS, KB * NS:(KB + AG) * NS]
                                            .rearrange("p (a b) -> p a b", b=NS)).then_inc(cv.misc_free, 1)
                            rows(vrow[2], M_V[2])
                            cv.emptied(dve, u + U_G)
                            ch.link(dve.tensor_tensor(gate[:, :], gate[:, :], graw[:, :], ALU.mult))
                            for n in range(N_PT):
                                bank = cv.filled(dve, m0, M_P[n])
                                nb = min(4, len(BLOCKS) - 4 * n)
                                dve.tensor_copy(pt[n % 2][:, 0:nb, :], bank[:, 0:nb * P]
                                                .rearrange("p (a b) -> p a b", b=P)).then_inc(cv.misc_free, 1)
                                if n == 0:
                                    bank = cv.filled(dve, m0, M_O)
                                    dve.tensor_copy(orow[:, :], bank[0:NS, 0:P]).then_inc(s_rows_ready, 1)
                                    dve.wait_ge(s_turned, h + 1)
                                    dve.tensor_tensor(yt[:, SEQ:NT], bank[:, P:P + NS], gate[:, SEQ:NT], ALU.mult)\
                                        .then_inc(cv.misc_free, 1)
                            dve.wait_ge(o_done, h + 1)
                            cv.copied(dve, m0, M_O)
                            dve.tensor_tensor(yt[:, 0:SEQ], psum[:, 5:7, :].rearrange("p a b -> p (a b)"),
                                              gate[:, 0:SEQ], ALU.mult).then_inc(y_ready, 1)
                            ch.end(AH)

        def pool_phase(ext, gate, graw, ahead, then):
            scope = ExitStack()
            with scope:
                cv = Conveyor("c", scope, (3, 4, 5, 6), 4)
                hist = sb("c_hist", (NB * HIST, GROUP), F32, scope)
                acc = [sb(f"c_sum{i}", (P, EXT + NB * SEXT), F32, scope) for i in range(2)]
                pooled = sb("c_pooled", (P, NT), F32, scope)
                gates = [(gate, graw), (sb("c_gate1", (P, NT), F32, scope), sb("c_gate_raw1", (P, NT), F32, scope))]
                yt = sb("c_y", (P, NT), F32, scope)
                count = sb("c_count", (P, CG, HIST), F32, scope)
                pw = sb("c_pool_w", (P, CG, P), F32, scope)
                last_p = sb("c_last_p", (HIST, GROUP), F32, scope)
                last_s = sb("c_last_s", (NB * HIST, GROUP), F32, scope)
                tail = sb("c_tail", (P, NB * HIST), F32, scope)
                const_in = sem("c_const_in", scope)
                tail_ready = sem("c_tail_ready", scope)
                pooled_ready = sem("c_pooled_ready", scope)
                y_ready = sem("c_y_ready", scope)
                y_out = sem("c_y_out", scope)
                rows_out = sem("c_rows_out", scope)
                ahead_in = sem("c_ahead_in", scope)
                chain = sem("c_chain", scope)
                MISC = 5
                cols = ((0, 512), (512, 512), (1024, NS))
                U_CU3 = 2
                U_GATE = (None, 0, 1, 3)

                with nc.Block() as block:
                    @block.sync
                    def _(sp):
                        sp.dma_start(hist[:, :], A["state_pool"][0].rearrange("b r c -> (b r) c")).then_inc(const_in, 16)
                        sp.dma_start(count[:, :, :], A["c_count"]).then_inc(const_in, 16)
                        sp.dma_start(pw[:, :, :], A["pool_w"][0].rearrange("g c d -> c g d")).then_inc(const_in, 16)
                        for j, src in enumerate((col(w_in, COL_CU + 3 * P), col(w_in, COL_CG + 3 * P), *then)):
                            cv.load(sp, SLOTS + j, j % 2, src)
                        prefetch(sp, *ahead, ahead_in)
                        cv.copied(sp, (CG - 1) * MISC, 4)
                        sp.dma_start(OUT["pool_p"][0, 0], last_p[:, :]).then_inc(rows_out, 16)
                        sp.dma_start(OUT["pool_s"][0].rearrange("b r c -> (b r) c"), last_s[:, :])\
                            .then_inc(rows_out, 16)
                        sp.wait_ge(rows_out, 32)
                        sp.wait_ge(ahead_in, 16 * len(ahead[0]))

                    @block.gpsimd
                    def _(pool):
                        for u in range(SLOTS, SLOTS + 4):
                            cv.split(pool, u, u % 2, u // 2, KO)

                    @block.tensor
                    def _(pe):
                        def mix(g):
                            pe.wait_ge(pooled_ready, g + 1)
                            for q, (t0, n) in enumerate(cols):
                                bank = cv.fill(pe, g * MISC, 1 + q)
                                pe.matmul(bank[:, 0:n], pw[:, g, :], pooled[:, t0:t0 + n], start=True, stop=True)\
                                    .then_inc(cv.misc_done, 1)

                        def last_rows(g):
                            bank = cv.fill(pe, g * MISC, 4)
                            pe.wait_ge(tail_ready, g + 1)
                            pe.transpose(bank[0:HIST, 0:P], ext[g % 3][:, EXT - HIST:EXT], ident[:, :])
                            pe.transpose(bank[0:NB * HIST, P:2 * P], tail[:, :], ident[:, :]).then_inc(cv.misc_done, 1)

                        pe.wait_ge(const_in, 48)
                        for g in range(CG):
                            bank = cv.fill(pe, g * MISC, 0)
                            pe.transpose(bank[:, 0:NB * HIST], hist[:, g * P:(g + 1) * P],
                                         ident[0:NB * HIST, 0:NB * HIST]).then_inc(cv.misc_done, 1)
                            for c in range(NCH if g < CG - 1 else NCH - 1):
                                cv.project(pe, g + 1, (g + 1) % 2, c, KO, x_hi, x_lo)
                            mix(g)
                            last_rows(g)
                        cv.project(pe, CG, 0, NCH - 1, KO, x_hi, x_lo)

                    @block.scalar
                    def _(act):
                        def gate_of(g):
                            if g > 1:
                                act.wait_ge(y_ready, g - 1)
                            for c in range(NCH):
                                cv.empty(act, U_GATE[g], c, gates[g % 2][0], ACT.Sigmoid, raw=gates[g % 2][1])

                        def store_y(g):
                            act.wait_ge(y_ready, g + 1)
                            act.dma_start(y_d[Y_C + g], yt[:, :]).then_inc(y_out, 16)

                        gate_of(1)
                        store_y(0)
                        gate_of(2)
                        cv.copied(act, 0, 4)
                        for c in range(NCH):
                            empty_ext(cv, act, U_CU3, c, ext[0])
                        store_y(1)
                        gate_of(3)
                        store_y(2)
                        store_y(3)
                        act.wait_ge(y_out, 16 * CG)

                    @block.vector
                    def _(dve):
                        ch = Chain(dve, chain)
                        cv.dve_start(dve)
                        dve.wait_ge(const_in, 48)
                        for x in ext:
                            ch.step(dve.memset(x[:, 0:HIST], 0.0))
                        ch.wait()
                        for g, win in enumerate(WINDOWS):
                            x = ext[g % 3]
                            bank = cv.filled(dve, g * MISC, 0)
                            dve.tensor_copy(samples(x)[:, :, 0:HIST], bank[:, 0:NB * HIST]
                                            .rearrange("p (b t) -> p b t", t=HIST)).then_inc(cv.misc_free, 1)
                            cv.copied(dve, g * MISC, 0)
                            if g == 3:
                                cv.emptied(dve, U_CU3)
                            ch.step(dve.tensor_copy(tail[:, :].rearrange("p (b t) -> p b t", t=HIST),
                                                    samples(x)[:, :, TB:SEXT]))
                            src, w, n = x, 1, 0
                            end = EXT + NB * SEXT
                            while w < win:
                                dst = acc[n % 2]
                                ch.link(dve.tensor_tensor(dst[:, 2 * w - 1:end], src[:, 2 * w - 1:end],
                                                          src[:, w - 1:end - w], ALU.add))
                                src, w, n = dst, 2 * w, n + 1
                            if n == 1:
                                ch.wait()
                            dve.sem_inc(tail_ready, 1)
                            ch.step(dve.scalar_tensor_tensor(out=pooled[:, 0:SEQ], in0=src[:, HIST:EXT], scalar=1.0 / win,
                                                             in1=x[:, HIST:EXT], op0=ALU.mult, op1=ALU.subtract))
                            ch.link(dve.scalar_tensor_tensor(
                                out=pooled[:, SEQ:NT].rearrange("p (b t) -> p b t", t=TB),
                                in0=samples(src)[:, :, HIST:SEXT], scalar=1.0 / win,
                                in1=samples(x)[:, :, HIST:SEXT], op0=ALU.mult, op1=ALU.subtract))
                            ch.link(dve.tensor_tensor(pooled[:, 0:HIST], src[:, HIST:2 * HIST], count[:, g, :], ALU.mult))
                            dve.tensor_tensor(pooled[:, 0:HIST], pooled[:, 0:HIST], x[:, HIST:2 * HIST],
                                              ALU.subtract).then_inc(pooled_ready, 1)
                            if g > 0:
                                cv.emptied(dve, U_GATE[g])
                            sg, raw = gates[g % 2]
                            ch.link(dve.tensor_tensor(sg[:, :], sg[:, :], raw[:, :], ALU.mult))
                            if g > 0:
                                dve.wait_ge(y_out, 16 * g)
                            for q, (t0, n) in enumerate(cols):
                                bank = cv.filled(dve, g * MISC, 1 + q)
                                dve.scalar_tensor_tensor(out=yt[:, t0:t0 + n], in0=bank[:, 0:n],
                                                         scalar=p_scale[:, g:g + 1], in1=sg[:, t0:t0 + n],
                                                         op0=ALU.mult, op1=ALU.mult).then_inc(cv.misc_free, 1)
                            cv.copied(dve, g * MISC, 3)
                            dve.sem_inc(y_ready, 1)
                            bank = cv.filled(dve, g * MISC, 4)
                            ch.step(dve.tensor_copy(last_p[:, g * P:(g + 1) * P], bank[0:HIST, 0:P]))
                            dve.tensor_copy(last_s[:, g * P:(g + 1) * P], bank[0:NB * HIST, P:2 * P])\
                                .then_inc(cv.misc_free, 1)

        def output_phase(spare, ot, sq, g_post):
            scope = ExitStack()
            with scope:
                cv = Conveyor("o", scope, (3, 4, 5), KO)
                xt = sb("o_x", (P, TILES + 1, D), F32, scope)
                rows = sb("o_rows", (P, TILES + 1, D), F32, scope)
                LOADED = range(len(spare), KO - 1)
                flat = rows[:, :, :].rearrange("p t d -> p (t d)")
                stage = [*spare, *(flat[:, j * NT:(j + 1) * NT] for j in range(len(LOADED))), ot[1]]
                ssq_k = sb("o_ssq_by_tile", (P, TILES + 1, KO), F32, scope)
                ssq = sb("o_ssq", (P, TILES + 1), F32, scope)
                rs = sb("o_rs", (P, TILES + 1), F32, scope)
                m_in = [sem(f"o_merged_in{i}", scope) for i in range(KO)]
                x_in = sem("o_x_in", scope)
                g_in = sem("o_g_in", scope)
                mh_ready = sem("o_merged_hi_ready", scope)
                ml_ready = sem("o_merged_lo_ready", scope)
                sq_ready = sem("o_squares_ready", scope)
                sq_used = sem("o_squares_used", scope)
                ssq_ready = sem("o_ssq_ready", scope)
                rms_ready = sem("o_rms_ready", scope)
                out_ready = sem("o_out_ready", scope)
                stored = sem("o_stored", scope)
                chain = sem("o_chain", scope)
                spans = ((0, 4), (4, 4), (8, 1))
                QS = len(spans)
                LOOPS = KO // 2 - 1

                with nc.Block() as block:
                    @block.sync
                    def _(sp):
                        for k in LOADED:
                            sp.dma_start(stage[k], merged_d[k]).then_inc(m_in[k], 16)
                        sp.dma_start(g_post[:, :], A["norm_post"].broadcast_to([P, D])).then_inc(g_in, 16)
                        for k in range(SLOTS, 2 * SLOTS):
                            cv.load(sp, k, k % SLOTS, col(w_out, k * P))
                        sp.dma_start(xt[:, 0:TILES, :], A["x_prompt"][0].rearrange("(b p) d -> p b d", p=P))\
                            .then_inc(x_in, 16)
                        sp.dma_start(xt[0:NS, TILES, :], A["x_sample"].rearrange("b t d -> (b t) d")).then_inc(x_in, 16)
                        for k in range(2 * SLOTS, KO):
                            cv.load(sp, k, k % SLOTS, col(w_out, k * P))
                        for t in range(TILES + 1):
                            sp.wait_ge(out_ready, t + 1)
                            if t < TILES:
                                sp.dma_start(OUT["y_prompt"][0, t * P:(t + 1) * P, :], rows[:, t, :]).then_inc(stored, 16)
                            else:
                                sp.dma_start(OUT["y_sample"].rearrange("b t d -> (b t) d"), rows[0:NS, t, :])\
                                    .then_inc(stored, 16)
                        sp.wait_ge(stored, 16 * (TILES + 1))

                    @block.gpsimd
                    def _(pool):
                        for k in range(SLOTS, KO):
                            cv.split(pool, k, k % SLOTS, k // SLOTS, KO)

                    @block.tensor
                    def _(pe):
                        def back(u, j):
                            cv.emptied(pe, u)
                            for q, (b0, nb) in enumerate(spans):
                                bank = cv.fill(pe, u * QS, q, q == 2)
                                w = P if q < 2 else NS
                                for b in range(nb):
                                    mm = pe.transpose(bank[0:w, b * P:(b + 1) * P],
                                                      ot[j][:, (b0 + b) * P:(b0 + b) * P + w], ident[:, :])
                                mm.then_inc(cv.misc_done, 1)

                        def tile(u, j, back_at):
                            for c in range(NCH):
                                cv.project(pe, u, j, c, KO, x_hi, x_lo)
                                if c == back_at:
                                    back(u - 1, 1 - j)

                        for c in range(NCH):
                            cv.project(pe, 0, 0, c, KO, x_hi, x_lo, each=ml_ready if c == 0 else None)
                        with pe.Fori(0, LOOPS) as i:
                            tile(i * 2 + 1, 1, 0)
                            tile(i * 2 + 2, 0, 0)
                        tile(KO - 1, 1, 0)
                        back(KO - 1, 1)

                    @block.scalar
                    def _(act):
                        for k in range(KO):
                            if k in LOADED:
                                act.wait_ge(m_in[k], 16)
                            act.activation(x_hi[:, k, :], stage[k][:, :], ACT.Copy).then_inc(mh_ready, 1)

                        def squares(u):
                            act.wait_ge(sq_used, u + 1)
                            for q, (b0, nb) in enumerate(spans):
                                w = P if q < 2 else NS
                                act.wait_ge(cv.misc_done, u * QS + q + 1)
                                act.activation(sq[0:w, b0:b0 + nb, :],
                                               cv.bank(0, q)[0:w, 0:nb * P].rearrange("p (a b) -> p a b", b=P),
                                               ACT.Square).then_inc(sq_ready, 1)

                        act.wait_ge(ml_ready, KO)
                        for c in range(NCH):
                            cv.empty(act, 0, c, ot[0], ACT.Copy)

                        def tile(u, j):
                            cv.empty(act, u, 0, ot[j], ACT.Copy)
                            squares(u - 1)
                            for c in range(1, NCH):
                                cv.empty(act, u, c, ot[j], ACT.Copy)

                        with act.Fori(0, LOOPS) as i:
                            tile(i * 2 + 1, 1)
                            tile(i * 2 + 2, 0)
                        tile(KO - 1, 1)
                        squares(KO - 1)
                        act.wait_ge(ssq_ready, 1)
                        act.activation(rs[:, :], ssq[:, :], ACT.Sqrt, bias=eps[:, :], scale=1.0 / D)\
                            .then_inc(rms_ready, 1)

                    @block.vector
                    def _(dve):
                        ch = Chain(dve, chain)
                        cv.dve_start(dve)
                        for k in range(KO):
                            dve.wait_ge(mh_ready, k + 1)
                            dve.tensor_tensor(x_lo[:, k, :], stage[k][:, :], x_hi[:, k, :].bitcast(F32),
                                              ALU.subtract).then_inc(ml_ready, 1)
                        dve.memset(sq[:, :, :], 1.0).then_inc(sq_used, 1)
                        dve.wait_ge(g_in, 16)
                        with dve.Fori(0, KO) as u:
                            for q, (b0, nb) in enumerate(spans):
                                dve.wait_ge(sq_ready, u * QS + q + 1)
                                bank = cv.filled(dve, u * QS, q)
                                w = P if q < 2 else NS
                                dve.tensor_tensor(rows[0:w, b0:b0 + nb, bass.ds(u * P, P)],
                                                  bank[0:w, 0:nb * P].rearrange("p (a b) -> p a b", b=P),
                                                  g_post[0:w, bass.ds(u * P, P)].unsqueeze(1).broadcast_to([w, nb, P]),
                                                  ALU.mult).then_inc(cv.misc_free, 1)
                            dve.tensor_reduce(ssq_k[:, :, bass.ds(u, 1)].rearrange("p t o -> p (t o)"), sq[:, :, :],
                                              AX.X, ALU.add).then_inc(sq_used, 1)
                        dve.wait_ge(sq_used, KO + 1)
                        dve.tensor_reduce(ssq[:, :], ssq_k[:, :, :], AX.X, ALU.add).then_inc(ssq_ready, 1)
                        dve.wait_ge(rms_ready, 1)
                        ch.link(dve.reciprocal(rs[:, :], rs[:, :]))
                        dve.wait_ge(x_in, 32)
                        cv.copied(dve, KO * QS, -1)
                        for t in range(TILES + 1):
                            n = P if t < TILES else NS
                            dve.scalar_tensor_tensor(out=rows[0:n, t, :], in0=rows[0:n, t, :],
                                                     scalar=rs[0:n, t:t + 1], in1=xt[0:n, t, :],
                                                     op0=ALU.mult, op1=ALU.add).then_inc(out_ready, 1)

        def first_of(base):
            return [col(w_in, at) for at in base]

        merge_b = ((0, BH, w_br["b"], COL_MG + D),)
        merge_ac = ((0, AH, w_br["a"], COL_MG), (AH, CG, w_br["c"], COL_MG + 2 * D))

        norm_phase(first_of((COL_AQ, COL_AK)))
        attention_phase(first_of((COL_BF, COL_BQ)))
        with ExitStack() as kept:
            ext = [sb(f"c_ext{i}", (P, EXT + NB * SEXT), F32, kept) for i in range(3)]
            gate = sb("c_gate", (P, NT), F32, kept)
            graw = sb("c_gate_raw", (P, NT), F32, kept)
            hgrn_phase(ext, gate, graw, first_of((COL_CG + P, COL_CG + 2 * P)))

            spare = [sb(f"spare{i}", (P, NT), F32, kept) for i in range(3)]
            product = [x[:, 0:NT] for x in ext[:2]]
            so_far = ext[2][:, 0:NT]
            bufs = [*spare, so_far, *product]
            pool_phase(ext, gate, graw, (spare, [y_d[k] for k in range(3)]), first_of((COL_MG + D, COL_MG + D + P)))
            fresh_semaphores()
            merge_phase("mb", 0, merge_b, True, bufs, (gate, graw), 3,
                        ([*spare, so_far], [y_d[Y_A + k] for k in range(4)]), first_of((COL_MG, COL_MG + 2 * D)))
            merge_phase("mac", Y_A, merge_ac, False, bufs, (gate, graw), 4,
                        (spare, [merged_d[k] for k in range(3)]), [col(w_out, 0), col(w_out, P)])
            output_phase(spare, product, ext[2][:, 0:(TILES + 1) * P].rearrange("p (t e) -> p t e", e=P),
                         gate[:, 0:D])
        lot[0].close()


_INS = ["x_prompt", "x_sample", "cache_kv_w128", "cache_kv_w512", "cache_kv_w2048", "state_hgrn",
        "state_pool", "norm_pre", "norm_post", "w_in", "hgrn_lb_logits", "hgrn_norm", "pool_w",
        "pool_scale", "w_br_a", "w_br_b", "w_br_c", "w_out"]
_OUTS = [("y_prompt", (1, 1024, 1024)), ("y_sample", (8, 8, 1024)),
         ("kv128_p", (1, 1, 128, 2, 4, 128)), ("kv512_p", (1, 1, 512, 2, 4, 128)),
         ("kv2048_p", (1, 1, 1024, 2, 4, 128)), ("kv128_s", (1, 8, 8, 2, 4, 128)),
         ("kv512_s", (1, 8, 8, 2, 4, 128)), ("kv2048_s", (1, 8, 8, 2, 4, 128)),
         ("hgrn_p", (1, 1, 8, 128, 128)), ("hgrn_s", (1, 8, 8, 128, 128)),
         ("pool_p", (1, 1, 15, 512)), ("pool_s", (1, 8, 15, 512))]


def kernel(**inputs):
    import numpy as np
    import concourse.bacc as bacc
    from concourse.bass_utils import run_bass_kernel_spmd

    nc = bacc.Bacc("TRN2", target_bir_lowering=False, num_devices=1)
    arrays, ins, outs = {}, {}, {}
    for name in _INS:
        a = np.ascontiguousarray(inputs[name])
        arrays["in_" + name] = a
        ins[name] = nc.dram_tensor("in_" + name, a.shape, mybir.dt.from_np(a.dtype), kind="ExternalInput").ap()
    for name, a in constants(np).items():
        arrays["const_" + name] = a
        ins["c_" + name] = nc.dram_tensor("const_" + name, a.shape, mybir.dt.from_np(a.dtype),
                                          kind="ExternalInput").ap()
    for name, shape in _OUTS:
        outs[name] = nc.dram_tensor("out_" + name, shape, F32, kind="ExternalOutput").ap()
    build(nc, ins, outs)
    r = run_bass_kernel_spmd(nc, [arrays], core_ids=[0])
    return tuple(r.results[0]["out_" + name] for name, _ in _OUTS)
```
